# Optimizing a Trainium2 kernel written in Bass

```python
import jax, jax.numpy as jnp
from jax import lax
import numpy as np

D_MODEL = 2048
BATCH = 1
SEQ = 256
DEPTH = 1
DEC_BATCH = 8
DEC_SEQ = 8
PAST_LEN = 2048
PAGE_SIZE = 128

MIX_WIDTH = D_MODEL // 2
RWKV_HEAD_DIM = 64
RWKV_HEADS = MIX_WIDTH // RWKV_HEAD_DIM
DECAY_RANK = 64
AAA_RANK = 64
GATE_RANK = 128
SGU_CHUNK = 128
SGU_GROUPS = 8
SGU_GROUP_DIM = MIX_WIDTH // SGU_GROUPS
XATTN_HEADS = 4
XATTN_HEAD_DIM = MIX_WIDTH // XATTN_HEADS
MEM_LEN = 256
N_BRANCH = 3
D_FF = 11 * D_MODEL // 4
CONV_WIDTH = 3
RMS_EPS = 1e-6
LN_EPS = 1e-5
GN_EPS = 64e-5
N_SHIFT = 3 * MIX_WIDTH + DECAY_RANK + AAA_RANK + GATE_RANK
N_IN = N_SHIFT + 2 * MIX_WIDTH + MIX_WIDTH + N_BRANCH * D_MODEL

kernel_name = 'rwkv7_sgu_memxattn_gated_hybrid_step'

def rmsnorm(x, g):
    xf = x.astype(jnp.float32)
    y = xf * lax.rsqrt(jnp.mean(xf * xf, axis=-1, keepdims=True) + RMS_EPS)
    return (y * g.astype(jnp.float32)).astype(x.dtype)

def rwkv7_mix(rw, wkv0, w0, w_decay, a0, w_aaa, w_gate, k_k, k_a, r_k, lnx_w, lnx_b):
    f32 = jnp.float32
    B, T, _ = rw.shape
    W = MIX_WIDTH
    r, k, v, xw, xa, xg = jnp.split(rw.astype(f32), [W, 2 * W, 3 * W, 3 * W + DECAY_RANK, 3 * W + DECAY_RANK + AAA_RANK], axis=-1)
    w_log = -jax.nn.softplus(-(w0.astype(f32) + jnp.tanh(xw) @ w_decay.astype(f32))) - 0.5
    decay = jnp.exp(-jnp.exp(w_log))
    a = jax.nn.sigmoid(a0.astype(f32) + xa @ w_aaa.astype(f32))
    g = jax.nn.sigmoid(xg) @ w_gate.astype(f32)
    kk = k * k_k.astype(f32)
    k = k * (1.0 + (a - 1.0) * k_a.astype(f32))
    heads = lambda t: t.reshape(B, T, RWKV_HEADS, RWKV_HEAD_DIM)
    kk = heads(kk)
    kk = kk / jnp.maximum(jnp.sqrt(jnp.sum(kk * kk, axis=-1, keepdims=True)), 1e-12)
    r_h, k_h, v_h, w_h, a_h = heads(r), heads(k), heads(v), heads(decay), heads(a)
    a_vec = -kk
    b_vec = kk * a_h

    def step(S, inp):
        r_t, w_t, k_t, v_t, av_t, bv_t = inp
        sa = jnp.einsum('bhvk,bhk->bhv', S, av_t)
        S = S * w_t[:, :, None, :] + sa[..., None] * bv_t[:, :, None, :] + v_t[..., None] * k_t[:, :, None, :]
        return S, jnp.einsum('bhvk,bhk->bhv', S, r_t)

    seq = tuple(jnp.moveaxis(t, 1, 0) for t in (r_h, w_h, k_h, v_h, a_vec, b_vec))
    S, ys = lax.scan(step, wkv0.astype(f32), seq)
    y = jnp.moveaxis(ys, 0, 1)
    mu = jnp.mean(y, axis=-1, keepdims=True)
    var = jnp.mean(jnp.square(y - mu), axis=-1, keepdims=True)
    yn = ((y - mu) * lax.rsqrt(var + GN_EPS)).reshape(B, T, W) * lnx_w.astype(f32) + lnx_b.astype(f32)
    bonus = jnp.sum(r_h * k_h * r_k.astype(f32), axis=-1, keepdims=True) * v_h
    out = (yn + bonus.reshape(B, T, W)) * g
    return out.astype(rw.dtype), S.astype(wkv0.dtype)

def sgu_mix(gu, gv, sgu_g, sgu_b, w_s, b_s):
    B, T, W = gv.shape
    u = jax.nn.gelu(gu)
    vf = jax.nn.gelu(gv).astype(jnp.float32)
    mu = jnp.mean(vf, axis=-1, keepdims=True)
    var = jnp.mean(jnp.square(vf - mu), axis=-1, keepdims=True)
    v = (((vf - mu) * lax.rsqrt(var + LN_EPS)) * sgu_g.astype(jnp.float32) + sgu_b.astype(jnp.float32)).astype(gv.dtype)
    n_chunks = -(-T // SGU_CHUNK)
    pad = n_chunks * SGU_CHUNK - T
    vp = jnp.pad(v, ((0, 0), (0, pad), (0, 0))).reshape(B, n_chunks, SGU_CHUNK, SGU_GROUPS, SGU_GROUP_DIM)
    tril = jnp.tril(jnp.ones((SGU_CHUNK, SGU_CHUNK), dtype=bool))
    ws = jnp.where(tril, w_s, jnp.zeros_like(w_s))
    s = jnp.einsum('gts,bnsgc->bntgc', ws, vp) + jnp.transpose(b_s)[None, None, :, :, None]
    s = s.reshape(B, n_chunks * SGU_CHUNK, W)[:, :T]
    return u * s, v

def memory_kv(mem, g_mem, w_mem_k, w_mem_v):
    B, M, _ = mem.shape
    mn = rmsnorm(mem, g_mem)
    k = (mn @ w_mem_k).reshape(B, M, XATTN_HEADS, XATTN_HEAD_DIM)
    v = (mn @ w_mem_v).reshape(B, M, XATTN_HEADS, XATTN_HEAD_DIM)
    return k, v

def mem_xattn(q, mem_k, mem_v):
    B, T, _ = q.shape
    qh = q.reshape(B, T, XATTN_HEADS, XATTN_HEAD_DIM)
    s = jnp.einsum('bthd,bmhd->bhtm', qh, mem_k).astype(jnp.float32) * (XATTN_HEAD_DIM ** -0.5)
    pr = jax.nn.softmax(s, axis=-1).astype(q.dtype)
    return jnp.einsum('bhtm,bmhd->bthd', pr, mem_v).reshape(B, T, MIX_WIDTH)

def conv_ffn(h, conv_prev, w_up, conv_w, conv_b, w_down):
    T = h.shape[1]
    up = h @ w_up
    ext = jnp.concatenate([conv_prev.astype(up.dtype), up], axis=1)
    conv = conv_b + sum(conv_w[j] * ext[:, j:j + T] for j in range(CONV_WIDTH))
    gate, val = jnp.split(conv, 2, axis=-1)
    out = (jax.nn.gelu(gate) * val) @ w_down
    return out, ext[:, -(CONV_WIDTH - 1):]

def layer(x, shift_prev, wkv0, mem_k, mem_v, conv_prev, p):
    B, T, _ = x.shape
    xn = rmsnorm(x, p['g_pre_mix'])
    proj = xn @ p['w_in']
    W = MIX_WIDTH
    rw, gu, gv, q, gt = jnp.split(proj, [N_SHIFT, N_SHIFT + W, N_SHIFT + 2 * W, N_SHIFT + 3 * W], axis=-1)
    prev = jnp.concatenate([shift_prev[:, None, :].astype(rw.dtype), rw[:, :-1]], axis=1)
    rw_s = rw + p['mu_shift'] * (prev - rw)
    a_out, wkv_new = rwkv7_mix(rw_s, wkv0, p['w0'], p['w_decay'], p['a0'], p['w_aaa'], p['w_gate'],
                               p['k_k'], p['k_a'], p['r_k'], p['lnx_w'], p['lnx_b'])
    b_out, v_rows = sgu_mix(gu, gv, p['sgu_g'], p['sgu_b'], p['w_s'], p['b_s'])
    c_out = mem_xattn(q, mem_k, mem_v)
    branches = jnp.stack([a_out, b_out, c_out], axis=2)
    br = jnp.einsum('btnw,nwd->btnd', branches, p['w_branch'])
    gates = jax.nn.sigmoid(gt.reshape(B, T, N_BRANCH, D_MODEL))
    mix = jnp.sum(gates * br, axis=2) @ p['w_out']
    h = x + rmsnorm(mix, p['g_post_mix'])
    f, conv_new = conv_ffn(rmsnorm(h, p['g_pre_ffn']), conv_prev, p['w_up'], p['conv_w'], p['conv_b'], p['w_down'])
    y = h + rmsnorm(f, p['g_post_ffn'])
    return y, rw[:, -1], wkv_new, v_rows, conv_new

def setup_inputs(seed: int = 0) -> dict:
    key = jax.random.key(seed)
    ks = iter(jax.random.split(key, 48))
    f32 = jnp.float32
    L, D, W, F2 = DEPTH, D_MODEL, MIX_WIDTH, 2 * D_FF
    nrm = lambda shape, s: jax.random.normal(next(ks), shape, f32) * s
    gain = lambda shape: 1.0 + nrm(shape, 0.05)
    return {
        'x_prompt': nrm((BATCH, SEQ, D), 1.0),
        'x_sample': nrm((DEC_BATCH, DEC_SEQ, D), 1.0),
        'mem_prompt': nrm((BATCH, MEM_LEN, D), 1.0),
        'state_wkv': nrm((L, DEC_BATCH, RWKV_HEADS, RWKV_HEAD_DIM, RWKV_HEAD_DIM), 0.3),
        'state_shift': nrm((L, DEC_BATCH, N_SHIFT), 1.0),
        'cache_mem_k': nrm((L, DEC_BATCH, MEM_LEN, XATTN_HEADS, XATTN_HEAD_DIM), 1.0),
        'cache_mem_v': nrm((L, DEC_BATCH, MEM_LEN, XATTN_HEADS, XATTN_HEAD_DIM), 1.0),
        'state_ffn_conv': nrm((L, DEC_BATCH, CONV_WIDTH - 1, F2), 1.0),
        'g_pre_mix': gain((L, D)),
        'w_in': nrm((L, D, N_IN), D ** -0.5),
        'mu_shift': jax.random.uniform(next(ks), (L, N_SHIFT), f32),
        'w0': jax.random.uniform(next(ks), (L, W), f32, -5.0, -0.5),
        'w_decay': nrm((L, DECAY_RANK, W), DECAY_RANK ** -0.5),
        'a0': nrm((L, W), 0.5),
        'w_aaa': nrm((L, AAA_RANK, W), AAA_RANK ** -0.5),
        'w_gate': nrm((L, GATE_RANK, W), GATE_RANK ** -0.5),
        'k_k': 0.85 + nrm((L, W), 0.05),
        'k_a': gain((L, W)),
        'r_k': nrm((L, RWKV_HEADS, RWKV_HEAD_DIM), 0.1),
        'lnx_w': gain((L, W)),
        'lnx_b': nrm((L, W), 0.02),
        'sgu_g': gain((L, W)),
        'sgu_b': nrm((L, W), 0.02),
        'w_s': nrm((L, SGU_GROUPS, SGU_CHUNK, SGU_CHUNK), SGU_CHUNK ** -0.5),
        'b_s': 1.0 + nrm((L, SGU_GROUPS, SGU_CHUNK), 0.1),
        'g_mem': gain((L, D)),
        'w_mem_k': nrm((L, D, W), D ** -0.5),
        'w_mem_v': nrm((L, D, W), D ** -0.5),
        'w_branch': nrm((L, N_BRANCH, W, D), W ** -0.5),
        'w_out': nrm((L, D, D), D ** -0.5),
        'g_post_mix': gain((L, D)),
        'g_pre_ffn': gain((L, D)),
        'w_up': nrm((L, D, F2), D ** -0.5),
        'conv_w': nrm((L, CONV_WIDTH, F2), CONV_WIDTH ** -0.5),
        'conv_b': nrm((L, F2), 0.02),
        'w_down': nrm((L, D_FF, D), D_FF ** -0.5),
        'g_post_ffn': gain((L, D)),
    }

def reference(x_prompt, x_sample, mem_prompt, state_wkv, state_shift, cache_mem_k, cache_mem_v, state_ffn_conv,
              g_pre_mix, w_in, mu_shift, w0, w_decay, a0, w_aaa, w_gate, k_k, k_a, r_k, lnx_w, lnx_b,
              sgu_g, sgu_b, w_s, b_s, g_mem, w_mem_k, w_mem_v, w_branch, w_out, g_post_mix, g_pre_ffn,
              w_up, conv_w, conv_b, w_down, g_post_ffn):
    y_p, y_s = x_prompt, x_sample
    B = x_prompt.shape[0]
    wkv_p_l, sh_p_l, mk_p_l, mv_p_l, cv_p_l = [], [], [], [], []
    wkv_s_l, sh_s_l, vr_s_l, cv_s_l = [], [], [], []
    for l in range(DEPTH):
        p = dict(g_pre_mix=g_pre_mix[l], w_in=w_in[l], mu_shift=mu_shift[l], w0=w0[l], w_decay=w_decay[l],
                 a0=a0[l], w_aaa=w_aaa[l], w_gate=w_gate[l], k_k=k_k[l], k_a=k_a[l], r_k=r_k[l],
                 lnx_w=lnx_w[l], lnx_b=lnx_b[l], sgu_g=sgu_g[l], sgu_b=sgu_b[l], w_s=w_s[l], b_s=b_s[l],
                 w_branch=w_branch[l], w_out=w_out[l], g_post_mix=g_post_mix[l], g_pre_ffn=g_pre_ffn[l],
                 w_up=w_up[l], conv_w=conv_w[l], conv_b=conv_b[l], w_down=w_down[l], g_post_ffn=g_post_ffn[l])
        mk_p, mv_p = memory_kv(mem_prompt, g_mem[l], w_mem_k[l], w_mem_v[l])
        shift0 = jnp.zeros((B, N_SHIFT), x_prompt.dtype)
        wkv0 = jnp.zeros((B, RWKV_HEADS, RWKV_HEAD_DIM, RWKV_HEAD_DIM), x_prompt.dtype)
        conv0 = jnp.zeros((B, CONV_WIDTH - 1, 2 * D_FF), x_prompt.dtype)
        y_p, sh_p, wkv_p, _, cv_p = layer(y_p, shift0, wkv0, mk_p, mv_p, conv0, p)
        y_s, sh_s, wkv_s, vr_s, cv_s = layer(y_s, state_shift[l], state_wkv[l], cache_mem_k[l], cache_mem_v[l],
                                             state_ffn_conv[l], p)
        wkv_p_l.append(wkv_p); sh_p_l.append(sh_p); mk_p_l.append(mk_p); mv_p_l.append(mv_p); cv_p_l.append(cv_p)
        wkv_s_l.append(wkv_s); sh_s_l.append(sh_s); vr_s_l.append(vr_s); cv_s_l.append(cv_s)
    new_wkv_prompt = jnp.stack(wkv_p_l)
    new_shift_prompt = jnp.stack(sh_p_l)
    new_mem_k_prompt = jnp.stack(mk_p_l)
    new_mem_v_prompt = jnp.stack(mv_p_l)
    new_ffn_conv_prompt = jnp.stack(cv_p_l)
    new_wkv_sample = jnp.stack(wkv_s_l)
    new_shift_sample = jnp.stack(sh_s_l)
    new_sgu_v_sample = jnp.stack(vr_s_l)
    new_ffn_conv_sample = jnp.stack(cv_s_l)
    return (y_p, y_s, new_wkv_prompt, new_shift_prompt, new_mem_k_prompt, new_mem_v_prompt, new_ffn_conv_prompt,
            new_wkv_sample, new_shift_sample, new_sgu_v_sample, new_ffn_conv_sample)


_drawn_inputs = setup_inputs


def setup_inputs(seed=0):
    import zlib

    import numpy as np

    out = dict(_drawn_inputs(seed))
    spreads = {}
    factors = {'lnx_b': 6.371, 'sgu_b': 2.835, 'conv_b': 3.433}
    for name, (base, spread) in spreads.items():
        noise = np.random.default_rng([zlib.crc32(name.encode()), seed]).standard_normal(out[name].shape)
        drawn = base * np.exp(spread * noise) if base else spread * noise
        out[name] = __import__('jax').numpy.asarray(drawn.astype(out[name].dtype))
    for name, factor in factors.items():
        out[name] = (out[name] * factor).astype(out[name].dtype)
    return out
```

```python
from contextlib import ExitStack, contextmanager

import concourse.bass as bass
from concourse import mybir

F32 = mybir.dt.float32
F32R = mybir.dt.float32r
ALU = mybir.AluOpType
ACT = mybir.ActivationFunctionType
AX_X = mybir.AxisListType.X
ds = bass.ds

P = 128
D = 2048
KD = D // P
TP, NB, TB = 256, 8, 8
TS = NB * TB
T = TP + TS
W = D // 2
KW = W // P
HD = 64
NH = W // HD
NSH = 3 * W + 64 + 64 + 128
KSH = NSH // P
CH = 64
NCK = TP // CH
NC = NCK + 1
XT_ = T + 24
MEM = 256
XH = 4
DFF = 11 * D // 4
F2 = 2 * DFF
KF = DFF // P
NCH = KF // 4
EXT = TP + 1 + NB * (TB + 1)
CEXT = TP + 2 + NB * (TB + 2)
RMS_EPS, LN_EPS, GN_EPS = 1e-6, 1e-5, 64e-5
C_DECAY = 0.6065306597126334
NS = 2

U_MEM, U_RW, U_GUQ = 0, 16, 42
U_BR = [66, 90, 114]
U_OUT, U_FFN, U_END = 138, 154, 286
T_MEM, T_RW, T_GUQ = 0, 8, 34
T_BR = [58, 90, 122]
T_OUT, T_FFN = 154, 170
PARTS_FFN = 2 * U_FFN

PARAMS = [("g_pre_mix", D), ("mu_shift", NSH), ("w0", W), ("a0", W), ("k_k", W), ("k_a", W), ("r_k", W),
          ("lnx_w", W), ("lnx_b", W), ("sgu_g", W), ("sgu_b", W), ("g_mem", D), ("g_post_mix", D),
          ("g_pre_ffn", D), ("g_post_ffn", D), ("conv_w", 3 * F2), ("conv_b", F2)]
COL = {}
_at = 0
for _name, _n in PARAMS:
    COL[_name] = _at
    _at += _n // P
NPRM = _at


class Prog:

    def __init__(self, eng, sem, own):
        self.eng, self.sem, self.own, self.n, self.k, self.i = eng, sem, own, {}, {}, 0

    def value(self, name):
        k = self.k.get(name, 0)
        n = self.n.get(name, 0)
        return n if not k else k * self.i + n

    def do(self, ins, name=None):
        name = name or self.own
        ins.then_inc(self.sem(name), 1)
        self.n[name] = self.n.get(name, 0) + 1
        self.eng.wait_ge(self.sem(name), self.value(name))

    @contextmanager
    def loop(self, start, end, per):
        with self.eng.Fori(start, end) as i:
            first = {m: self.n.get(m, 0) for m in per}
            self.k, self.i = dict(per), i
            for m in per:
                self.n[m] = first[m] - per[m] * start
            before = dict(self.n)
            yield i
            got = {m: self.n[m] - before.get(m, 0) for m in self.n if self.n[m] != before.get(m, 0)}
            assert got == {m: v for m, v in per.items() if v}, (got, per)
        self.k = {}
        for m in per:
            self.n[m] = first[m] + per[m] * (end - start)


def hybrid_step(nc, A, O):
    ctx = ExitStack()
    with ctx:
        sems = {}

        def S(name):
            if name not in sems:
                sems[name] = ctx.enter_context(nc.semaphore(name))
            return sems[name]

        def sb(name, shape, dt=F32):
            return ctx.enter_context(nc.sbuf_tensor(name, shape, dt))

        raw = [sb(f"raw{i}", [P, 2048]) for i in range(2)]
        hi = [sb(f"hi{i}", [P, 2048], F32R) for i in range(NS)]
        lo = [sb(f"lo{i}", [P, 2048], F32R) for i in range(NS)]
        ah = sb("ah", [P, KD, T], F32R)
        al_ = sb("al", [P, KD, T], F32R)
        bh = sb("bh", [P, KW, T], F32R)
        bl = sb("bl", [P, KW, T], F32R)
        mix = sb("mix", [P, KD, T])
        rwr = sb("rw", [P, KSH * EXT])
        rw = rwr[:, :].rearrange("p (k t) -> p k t", k=KSH)
        qr = sb("q", [P, KW * XT_])
        q = qr[:, :].rearrange("p (k t) -> p k t", k=KW)
        wk = sb("work", [P, 5120])
        zz = sb("small", [P, 1600])
        prm = sb("prm", [P, NPRM])
        ident = sb("ident", [P, P])
        ones = sb("ones", [P, P])
        blk = sb("head_ones", [P, P])
        m_bd = sb("m_bd", [P, CH])
        m_ad = sb("m_ad", [P, CH])
        m_bo = sb("m_bo", [P, CH])
        m_in = sb("m_in", [P, NC, CH])
        m_st = sb("m_st", [P, NC, CH])
        m_e8 = sb("m_e8", [P, NB])
        m_sc = sb("m_scan", [P, T])
        rep8 = sb("rep8", [NB, TS])
        bank = [ctx.enter_context(nc.psum_tensor(f"bank{i}", [P, 512], F32)) for i in range(8)]
        mixf = mix[:, :, :].rearrange("p k t -> p (k t)")
        gs = zz[:, 0:4 * T].rearrange("p (c t) -> p c t", c=4)

        def mslot(n):
            return mixf[:, T * n:T * (n + 1)]

        def wslot(n):
            return wk[:, T * n:T * (n + 1)]

        def c5(ap):
            return ap.rearrange("p (c t) -> p c t", c=NC)

        def pcol(name, j, n=1):
            c = COL[name] + j
            return prm[:, c:c + n] if isinstance(c, int) else prm[:, ds(c, n)]

        block = ctx.enter_context(nc.Block())

        def parts_of(u):
            if u < U_FFN:
                return 2 * (u + 1)
            v = u - U_FFN
            if v < 8:
                return PARTS_FFN + 2 * (v + 1)
            c, j = divmod(v - 8, 12)
            base = PARTS_FFN + 16 + 32 * c
            if c == NCH - 1:
                return base + 4 * (j + 1)
            return base + (2 * (j + 1) if j < 4 else 8 + 4 * (j - 3) if j < 8 else 24 + 2 * (j - 7))

        def lin(c, k, i):
            return c if not k else k * i + c

        def load_unit(sp, src, c, k=0, i=0):
            if c >= 2 or k:
                count = lin(c - 1, k, i)
                if k:
                    count = sp.to_reg(count)
                    sp.wait_ge(S("hi_done"), 1)
                sp.wait_ge(S("hi_done"), count)
                sp.wait_ge(S("lo_done"), count)
            sp.dma_start(raw[c % 2][:, :].rearrange("p (k n) -> p k n", n=src.shape[2]), src)\
              .then_inc(S(f"raw_loaded{c % 2}"), 16)

        def pe_left(eng, c, k, i, parts_k):
            if c >= NS or k:
                eng.wait_ge(S("parts"), lin(parts_of(c - NS), parts_k, i))

        def hi_unit(act, c, k=0, i=0, pk=None):
            if c >= U_END:
                return
            act.wait_ge(S(f"raw_loaded{c % 2}"), lin(16 * (c // 2 + 1), 8 * k, i))
            pe_left(act, c, k, i, 2 * k if pk is None else pk)
            act.activation(hi[c % NS][:, :], raw[c % 2][:, :], ACT.Copy).then_inc(S("hi_done"), 1)

        def lo_unit(dve, c, k=0, i=0, pk=None):
            if c >= U_END:
                return
            dve.wait_ge(S("hi_done"), lin(c + 1, k, i))
            pe_left(dve, c, k, i, 2 * k if pk is None else pk)
            dve.tensor_tensor(lo[c % NS][:, :], raw[c % 2][:, :], hi[c % NS][:, :], ALU.subtract)\
               .then_inc(S("lo_done"), 1)

        def bank_free(pe, t, k=0, i=0):
            if t >= 4:
                pe.wait_ge(S(f"tile_out{t % 4}"), lin(t // 4, k // 4, i))

        def three(pe, out, a_hi, a_lo, b_hi, b_lo, first, last):
            pe.matmul(out, a_hi, b_hi, start=first, stop=False)
            pe.matmul(out, a_hi, b_lo, start=False, stop=False)
            return pe.matmul(out, a_lo, b_hi, start=False, stop=last)

        def pe_group(pe, u, t, xh, xl, units, uk=0, tk=0, i=0):
            for h in range(units):
                pe.wait_ge(S("lo_done"), lin(u + h + 1, uk, i))
                s = (u + h) % NS
                for c in range(2):
                    if h == 0:
                        bank_free(pe, t + c, tk, i)
                    for k in range(8):
                        o = 256 * k + 128 * c
                        last = three(pe, bank[(t + c) % 4][:, 0:T], hi[s][:, o:o + P], lo[s][:, o:o + P],
                                     xh[:, 8 * h + k, :], xl[:, 8 * h + k, :], h + k == 0, h == units - 1 and k == 7)
                    last.then_inc(S("parts"), 1)

        def tile_ready(eng, u, pk=0, i=0, part=2):
            eng.wait_ge(S("parts"), lin(parts_of(u) if part == 2 else parts_of(u) - 2 + part, pk, i))

        def kv(w, k0, n0, nk=8, nn=256):
            return w.rearrange("(kt p) n -> p kt n", p=P)[:, k0:k0 + nk, ds(n0, nn) if not isinstance(n0, int) else slice(n0, n0 + nn)]


        x_tok = [wk[:, 896:896 + D], wk[:, 896 + D:896 + 2 * D], qr[0:TS, 0:D]]
        mem_tok = [rwr[:, 0:D], rwr[:, D:2 * D]]
        mkv_stage = [rwr[:, 2 * D + 512 * j:2 * D + 512 * j + 512] for j in range(4)]
        shift_t = zz[:, 0:208]
        ss, rs = zz[:, 220:225], zz[:, 225:230]
        m_u = sb("m_u", [P, P])
        m_id = sb("m_id", [P, CH])
        half_b = sb("half_bias", [P, 2 * KW])

        def pool_constants(pool, pp):
            def full(ap, v):
                pp.do(pool.memset(ap, v))

            def keep(ap, op, base, pattern, cm, fill=0.0, name=None):
                pp.do(pool.affine_select(out=ap, in_=ap, compare_op=op, fill=fill, base=base, pattern=pattern,
                                         channel_multiplier=cm), name)

            full(ident[:, :], 0.0)
            keep(ident[:, :], ALU.not_equal, 0, [[-1, P]], 1, 1.0)
            full(ones[:, :], 1.0)
            full(blk[:, :], 0.0)
            for h in range(2):
                full(blk[64 * h:64 * h + 64, 64 * h:64 * h + 64], 1.0)
            full(m_e8[:, :], 1.0)
            full(m_bd[:, :], 1.0)
            full(m_ad[:, :], 1.0)
            full(m_bo[:, :], 1.0)
            full(m_st[:, :, :], 1.0)
            full(m_in[:, :, :], 1.0)
            full(m_sc[:, :], 1.0)
            full(m_u[:, :], 1.0)
            for h in range(2):
                r = slice(64 * h, 64 * h + 64)
                keep(m_e8[r, :], ALU.is_ge, 0, [[-8, 8]], 1)
                keep(m_e8[r, :], ALU.is_ge, 7, [[8, 8]], -1)
                for m, op, c in ((m_bd, ALU.is_gt, -1), (m_ad, ALU.is_gt, 1)):
                    keep(m[r, :], op, 0, [[-c, 64]], c)
                    mv = m[r, :].rearrange("p (b t) -> p b t", b=8)
                    keep(mv, ALU.is_ge, 0, [[-8, 8], [0, 8]], 1)
                    keep(mv, ALU.is_ge, 7, [[8, 8], [0, 8]], -1)
                keep(m_bo[r, :].rearrange("p (b t) -> p b t", b=8), ALU.is_gt, 0, [[8, 8], [0, 8]], -1)
                keep(m_st[r, 0:NCK, :], ALU.is_gt, 0, [[0, NCK], [1, 64]], -1)
                keep(m_in[r, :, :], ALU.is_ge, 0, [[0, NC], [1, 64]], -1)
                mv = m_in[r, NCK, :].rearrange("p (b t) -> p b t", b=8)
                keep(mv, ALU.is_ge, 0, [[-8, 8], [0, 8]], 1)
                keep(m_st[r, NCK, :], ALU.is_gt, 0, [[1, 64]], -1)
                mv = m_st[r, NCK, :].rearrange("p (b t) -> p b t", b=8)
                keep(mv, ALU.is_ge, 7, [[8, 8], [0, 8]], -1)
                keep(mv, ALU.is_ge, 0, [[-8, 8], [0, 8]], 1)
            keep(m_u[:, :], ALU.is_ge, 0, [[1, P]], -1)
            full(m_sc[:, 0:TP].rearrange("p (c t) -> p c t", c=NCK)[:, :, 0:1], 0.0)
            full(m_sc[:, TP:T].rearrange("p (c t) -> p c t", c=NB)[:, :, 0:1], 0.0)
            full(rep8[:, :], 0.0)
            keep(rep8[:, :].rearrange("p (b t) -> p b t", b=8), ALU.not_equal, 0, [[0, 8], [-1, 8]], 1, 1.0, "consts")

        def pool_loads(pool):
            for k in range(2):
                pool.dma_start(mem_tok[k], A["mem_prompt"][128 * k:128 * k + 128, :]).then_inc(S("mem_in"), 16)
            row = 0
            for name, n in PARAMS:
                src = A[name].rearrange("(r p) -> r p", p=P)
                k, at = n // P, 0
                while at < k:
                    m = min(k - at, P - row % P)
                    c = 128 * (row // P)
                    pool.dma_start(wk[row % P:row % P + m, c:c + 128], src[at:at + m, :]).then_inc(S("par_in"), 16)
                    par_dmas[0] += 1
                    at += m
                    row += m
            shift = A["state_shift"].rearrange("b (j p) -> (b j) p", p=P)
            pool.dma_start(wk[:, 640:768], shift[0:P, :]).then_inc(S("par_in"), 16)
            pool.dma_start(wk[0:80, 768:896], shift[P:208, :]).then_inc(S("par_in"), 16)
            par_dmas[0] += 2
            for k in range(2):
                pool.dma_start(x_tok[k], A["x_prompt"][128 * k:128 * k + 128, :]).then_inc(S("x_in"), 16)
            pool.dma_start(x_tok[2], A["x_sample"]).then_inc(S("x_in"), 16)

        par_dmas = [0]
        n_par, row = 2, 0
        for name, n in PARAMS:
            at, k = 0, n // P
            while at < k:
                m = min(k - at, P - row % P)
                n_par, at, row = n_par + 1, at + m, row + m

        def entry_act(act, aa):
            for j, (tok, sem, m) in enumerate([(mem_tok[0], "mem_in", P), (mem_tok[1], "mem_in", P), (x_tok[0], "x_in", P),
                                               (x_tok[1], "x_in", P), (x_tok[2], "x_in", TS)]):
                act.wait_ge(S(sem), 32 if sem == "mem_in" else 48)
                if j == 0:
                    act.wait_ge(S("rs_zero"), 1)
                aa.do(act.activation(mixf[0:m, 0:D], tok, ACT.Square, accum_out=ss[0:m, j:j + 1]),
                      "sum_mem" if j == 1 else "sum_x" if j == 4 else None)
            act.wait_ge(S("ms_ready"), 1)
            aa.do(act.activation(rs, ss, ACT.Sqrt), "rms_ready")
            act.wait_ge(S("entry_ps"), 2)
            aa.do(act.activation(prm[:, 0:512], bank[4][:, :], ACT.Copy))
            aa.do(act.activation(prm[:, 512:NPRM], bank[5][:, 0:NPRM - 512], ACT.Copy))
            aa.do(act.activation(shift_t, bank[5][:, 128:336], ACT.Copy), "prm_ready")
            for k in range(8):
                act.wait_ge(S("mem_g"), k + 1)
                aa.do(act.activation(ah[:, 2 * k:2 * k + 2, 0:MEM], memg(k), ACT.Copy), "mem_hi")

        def memg(k):
            return mixf[:, 512 * (k % 2):512 * (k % 2) + 512].rearrange("p (a t) -> p a t", a=2)

        def entry_dve(dve, vv):
            vv.do(dve.memset(ss, 1.0), "rs_zero")
            dve.wait_ge(S("sum_mem"), 1)
            dve.wait_ge(S("sum_x"), 1)
            vv.do(dve.tensor_scalar(ss, ss, 1.0 / D, RMS_EPS, ALU.mult, ALU.add), "ms_ready")
            dve.wait_ge(S("rms_ready"), 1)
            vv.do(dve.reciprocal(rs, rs))
            for j, tok in enumerate(mem_tok + x_tok):
                m = TS if j == 4 else P
                vv.do(dve.tensor_scalar(tok, tok, rs[0:m, j:j + 1], None, ALU.mult), "tok_normed")
            dve.wait_ge(S("prm_ready"), 1)
            vv.do(dve.tensor_scalar(half_b[:, :], prm[:, COL["w0"]:COL["w0"] + 2 * KW], 0.5, None, ALU.mult))
            dve.wait_ge(S("consts"), 1)
            vv.do(dve.tensor_tensor(m_id[:, :], ident[:, 0:64], ident[:, 64:128], ALU.add))
            for k in range(8):
                dve.wait_ge(S("entry_ps"), 3 + k)
                g = bc(pcol("g_mem", 2 * k, 2), MEM)
                vv.do(dve.tensor_tensor(memg(k), bank[4 + k % 4][:, :].rearrange("p (a t) -> p a t", a=2), g, ALU.mult), "mem_g")
                dve.wait_ge(S("mem_hi"), k + 1)
                vv.do(dve.tensor_tensor(al_[:, 2 * k:2 * k + 2, 0:MEM], memg(k), ah[:, 2 * k:2 * k + 2, 0:MEM], ALU.subtract),
                      "mem_lo")
            for k in range(KD):
                dve.wait_ge(S("entry_ps"), 11 + k)
                vv.do(dve.tensor_scalar(mix[:, k, :], bank[4 + k % 4][:, 0:T], pcol("g_pre_mix", k), None, ALU.mult), "x_g")

        def bc(ap, n):
            return ap.rearrange("p (a o) -> p a o", o=1).broadcast_to([ap.shape[0], ap.shape[1], n])

        def entry_pe(pe):
            pe.wait_ge(S("consts"), 1)
            pe.wait_ge(S("par_in"), 16 * n_par)
            for j in range(4):
                last = pe.transpose(bank[4][:, 128 * j:128 * j + 128], wk[:, 128 * j:128 * j + 128], ident[:, :])
            last.then_inc(S("entry_ps"), 1)
            m = NPRM - 512
            pe.transpose(bank[5][:, 0:m], wk[0:m, 512:640], ident[0:m, 0:m])
            pe.transpose(bank[5][:, 128:256], wk[:, 640:768], ident[:, :])
            pe.transpose(bank[5][:, 256:336], wk[0:80, 768:896], ident[0:80, 0:80]).then_inc(S("entry_ps"), 1)
            pe.wait_ge(S("tok_normed"), 2)
            for k in range(8):
                if k < 4:
                    pe.wait_ge(S("prm_ready"), 1)
                else:
                    pe.wait_ge(S("mem_g"), k - 3)
                for a in range(2):
                    for t in range(2):
                        last = pe.transpose(bank[4 + k % 4][:, 256 * a + 128 * t:256 * a + 128 * t + 128],
                                            mem_tok[t][:, 128 * (2 * k + a):128 * (2 * k + a) + 128], ident[:, :])
                last.then_inc(S("entry_ps"), 1)
            pe.wait_ge(S("tok_normed"), 5)
            for k in range(KD):
                if k < 4:
                    pe.wait_ge(S("mem_g"), k + 5)
                else:
                    pe.wait_ge(S("x_g"), k - 3)
                if k == 0:
                    pe.wait_ge(S("mem_lo"), 8)
                x_transposes(pe, x_tok, k, bank[4 + k % 4]).then_inc(S("entry_ps"), 1)

        def x_transposes(pe, toks, k, out):
            for t in range(3):
                m = TS if t == 2 else P
                last = pe.transpose(out[:, 128 * t:128 * t + m], toks[t][:, 128 * k:128 * k + 128], ident[0:m, 0:m])
            return last

        def mem_pe(pe):
            pe.wait_ge(S("mem_lo"), 8)
            for u in range(16):
                g, s = u // 4, u % NS
                pe.wait_ge(S("lo_done"), u + 1)
                for tt in range(2):
                    t = 2 * g + tt
                    if u % 4 == 0:
                        bank_free(pe, t)
                    for k in range(4):
                        kk, r = 4 * (u % 4) + k, slice(128 * tt, 128 * tt + 128)
                        a_h, a_l = ah[:, kk, r], al_[:, kk, r]
                        w_h, w_l = hi[s][:, 512 * k:512 * k + 512], lo[s][:, 512 * k:512 * k + 512]
                        last = three(pe, bank[t % 4][:, :], a_h, a_l, w_h, w_l, kk == 0, kk == KD - 1)
                    last.then_inc(S("parts"), 1)

        def mem_act(act):
            for u in range(16):
                hi_unit(act, u + 2)
                if u % 4 == 3:
                    for t in range(2 * (u // 4), 2 * (u // 4) + 2):
                        tile_ready(act, u, part=t % 2 + 1)
                        if t == 0:
                            act.wait_ge(S("mem_lo"), 8)
                        if t >= 4:
                            act.wait_ge(S(f"mem_stored{t % 4}"), 16)
                        act.activation(mkv_stage[t % 4], bank[t % 4][:, :], ACT.Copy).then_inc(S(f"tile_out{t % 4}"), 1)

        def mem_dve(dve):
            for u in range(16):
                lo_unit(dve, u + 2)

        def mem_pool(pool):
            for t in range(8):
                pool.wait_ge(S(f"tile_out{t % 4}"), t // 4 + 1)
                g, tt = t // 2, t % 2
                dst = O["mem_k"] if g < 2 else O["mem_v"]
                pool.dma_start(dst[128 * tt:128 * tt + 128, 512 * (g % 2):512 * (g % 2) + 512], mkv_stage[t % 4])\
                    .then_inc(S(f"mem_stored{t % 4}"), 16)

        def split_x_act(act, aa):
            act.wait_ge(S("x_g"), KD)
            tile_ready(act, 15)
            for c in range(4):
                aa.do(act.activation(ah[:, 4 * c:4 * c + 4, :], mix[:, 4 * c:4 * c + 4, :], ACT.Copy), "xn_hi")
            for t in range(4):
                act.wait_ge(S(f"mem_stored{t}"), 32)

        def split_x_dve(dve, vv):
            tile_ready(dve, 15)
            for c in range(4):
                dve.wait_ge(S("xn_hi"), c + 1)
                vv.do(dve.tensor_tensor(al_[:, 4 * c:4 * c + 4, :], mix[:, 4 * c:4 * c + 4, :], ah[:, 4 * c:4 * c + 4, :],
                                        ALU.subtract), "xn_lo")
            for t in range(4):
                dve.wait_ge(S(f"mem_stored{t}"), 32)
            vv.do(dve.memset(rw[:, :, 0:1], 0.0))
            vv.do(dve.tensor_copy(smp(rw, KSH)[:, :, :, 0], shift_t.rearrange("p (b k) -> p k b", b=NB)), "shift_set")

        def smp(t, k):
            return t[:, :, TP + 1:EXT].rearrange("p k (b t) -> p k b t", b=NB)

        def rw_pe(pe):
            pe.wait_ge(S("xn_lo"), 4)
            pe_group(pe, U_RW, T_RW, ah, al_, 2)
            with pe.Fori(0, 6) as i:
                for g in range(2):
                    pe_group(pe, U_RW + 2 + 2 * g, T_RW + 2 + 2 * g, ah, al_, 2, 4, 4, i)

        def rw_out(act, k, t, tk=0, i=0):
            kk = ds(k, 1) if tk else slice(k, k + 1)
            b = t % 4
            act.activation(rw[:, kk, 1:1 + TP].rearrange("p k t -> p (k t)"), bank[b][:, 0:TP], ACT.Copy)
            act.activation(rw[:, kk, TP + 1:EXT].rearrange("p k (b t) -> p (k b) t", b=NB)[:, :, 1:1 + TB],
                           bank[b][:, TP:T].rearrange("p (b t) -> p b t", b=NB), ACT.Copy).then_inc(S(f"tile_out{b}"), 1)

        def rw_act(act):
            def group(u, t, k, uk=0, i=0):
                for h in range(2):
                    hi_unit(act, u + 2 + h, uk, i)
                for c in range(2):
                    tile_ready(act, u + 1, 2 * uk, i, c + 1)
                    rw_out(act, k + c, t + c, uk, i)
            act.wait_ge(S("shift_set"), 1)
            group(U_RW, T_RW, 0)
            with act.Fori(0, 6) as i:
                for g in range(2):
                    group(U_RW + 2 + 2 * g, T_RW + 2 + 2 * g, 4 * i + 2 + 2 * g, 4, i)

        def rw_dve(dve):
            for h in range(2):
                lo_unit(dve, U_RW + 2 + h)
            with dve.Fori(0, 6) as i:
                for h in range(4):
                    lo_unit(dve, U_RW + 4 + h, 4, i)

        wa_in, sg = qr[:, 0:T], qr[:, T:2 * T]
        s0t = qr[:, 640:1152].rearrange("p (b v) -> p b v", b=NB)
        alm = qr[:, 1152:1664].rearrange("p (b t) -> p b t", b=NB)
        st_pp = [qr[:, 1664:1728], qr[:, 1728:1792]]
        xs_, sa_ = qr[:, 1792:1856], qr[:, 1856:1920]
        r_, k_, v_, alp, be, ka, rh, pt, bon, gg = [mslot(n) for n in range(10)]
        t_ad, t_bd, t_bo, t_bk, t_cb, t_ck = [mslot(n) for n in range(10, 16)]
        be_t, ka_t, v_t, t_a2, t_b2, t_r, t_rt = [wslot(n) for n in range(7)]
        sam = wk[:, 2240:2752].rearrange("p (b v) -> p b v", b=NB)
        vtm = wk[:, 2752:3264].rearrange("p (b v) -> p b v", b=NB)
        wlr = wk[:, 3264:3520]
        s_out = wk[0:64, 3520:4544]
        sp_out = wk[0:64, 4544:4672]
        s0raw = zz[0:64, 0:1024]
        last_t = zz[:, 1024:1258]
        sh_stage = wk[:, 4700:4956]

        RING = (4, 5, 7)
        PR = {}
        for _n in ["z", "za", "g", "ssq", "s0t", "bonus", "A", "B", "Bk", "Cb", "Ck", "beT", "kaT", "vT", "A2", "B2",
                   "R1", "RT1", "A4", "B4", "R2", "RT2", "Q", "QT", "Q2", "QT2", "QT4", "W1", "W2", "W3"] + \
                [f"{m}{c}" for c in range(NCK) for m in ("X", "SA", "S")] + \
                ["X4", "SA4", "S4", "tr0", "tr1", "trp", "mean", "var"]:
            PR[_n] = len(PR)
        NPR = len(PR)
        N_OUT = NPR - 3

        def pbank(name):
            return bank[RING[PR[name] % 3]]

        def wkv_pool(pool):
            pool.wait_ge(S("shift_stage"), 2)
            pool.dma_start(O["shift_p"], sh_stage[0:KSH, 0:128]).then_inc(S("stored"), 16)
            pool.dma_start(O["shift_s"][0:102, :], sh_stage[KSH:128, 0:128]).then_inc(S("stored"), 16)
            pool.dma_start(O["shift_s"][102:208, :], sh_stage[0:106, 128:256]).then_inc(S("stored"), 16)
            for j in range(KW):
                if j:
                    pool.wait_ge(S("wkv_ps"), NPR * (j - 1) + PR["s0t"] + 1)
                n = slice(128 * j, 128 * j + 128)
                pool.dma_start(wlr[0:64, 0:128], A["w_decay"][:, n]).then_inc(S("pair_in"), 16)
                pool.dma_start(wlr[64:128, 0:128], A["w_aaa"][:, n]).then_inc(S("pair_in"), 16)
                pool.dma_start(wlr[:, 128:256], A["w_gate"][:, n]).then_inc(S("pair_in"), 16)
                for h in range(2):
                    dst = s0raw.rearrange("v (b h k) -> v b h k", b=NB, h=2)[:, :, h, :]
                    pool.dma_start(dst, A["state_wkv"][:, 2 * j + h].rearrange("b v k -> v b k")).then_inc(S("pair_in"), 16)
                pool.wait_ge(S("ring_out"), N_OUT * j + PR["trp"] - 2)
                for h in range(2):
                    src = s_out.rearrange("v (b h k) -> v b h k", b=NB, h=2)[:, :, h, :]
                    pool.dma_start(O["wkv_s"][:, 2 * j + h].rearrange("b v k -> v b k"), src).then_inc(S("state_stored"), 16)
                pool.dma_start(O["wkv_p"][2 * j:2 * j + 2].rearrange("h v k -> v h k"),
                               sp_out.rearrange("v (h k) -> v h k", h=2)).then_inc(S("state_stored"), 16)

        def mix_shift(dve, vv, dst, tile, mu):
            d = mixf[:, 3200:3200 + EXT - 1]
            tt = slice(tile, tile + 1) if isinstance(tile, int) else ds(tile, 1)
            row = rw[:, tt, :].rearrange("p k t -> p (k t)")
            vv.do(dve.tensor_tensor(d, row[:, 0:EXT - 1], row[:, 1:EXT], ALU.subtract))
            vv.do(dve.scalar_tensor_tensor(out=dst[:, 0:TP], in0=d[:, 0:TP], scalar=mu, in1=row[:, 1:1 + TP],
                                           op0=ALU.mult, op1=ALU.add))
            ds8 = mixf[:, 3200 + TP + 1:3200 + EXT].rearrange("p (b t) -> p b t", b=NB)[:, :, 0:TB]
            vv.do(dve.scalar_tensor_tensor(out=dst[:, TP:T].rearrange("p (b t) -> p b t", b=NB), in0=ds8, scalar=mu,
                                           in1=row[:, TP + 1:EXT].rearrange("p (b t) -> p b t", b=NB)[:, :, 1:],
                                           op0=ALU.mult, op1=ALU.add))

        def wkv_dve(dve, vv):
            for t in range(4):
                dve.wait_ge(S(f"tile_out{t}"), 8 if t >= 2 else 9)
            vv.do(dve.tensor_copy(last_t[:, 0:KSH], rw[:, :, TP]))
            vv.do(dve.tensor_copy(last_t[:, KSH:].rearrange("p (b k) -> p k b", b=NB), smp(rw, KSH)[:, :, :, TB]), "last_rows")
            mix_shift(dve, vv, wa_in, 24, pcol("mu_shift", 24))
            mix_shift(dve, vv, sg, 25, pcol("mu_shift", 25))
            vv.do(dve.memset(alm, 0.0), "low_in")
            dve.wait_ge(S("sig_g"), 2)
            vv.do(dve.tensor_scalar(sg, sg, 0.5, 0.5, ALU.mult, ALU.add), "low_ready")
            with vv.loop(0, KW, PER_V) as i:
                def ps(name):
                    dve.wait_ge(S("wkv_ps"), NPR * i + PR[name] + 1)

                def tt(o, a, b, op, sem=None):
                    vv.do(dve.tensor_tensor(o, a, b, op), sem)

                def stt(o, a, s, b, op0, op1, sem=None):
                    vv.do(dve.scalar_tensor_tensor(out=o, in0=a, scalar=s, in1=b, op0=op0, op1=op1), sem)

                mix_shift(dve, vv, r_, i, pcol("mu_shift", i))
                mix_shift(dve, vv, k_, i + 8, pcol("mu_shift", i + 8))
                mix_shift(dve, vv, v_, i + 16, pcol("mu_shift", i + 16))
                kkv, sq, ld, av, cum, pinv = t_ad, t_bd, t_bo, t_bk, t_cb, t_ck
                vv.do(dve.tensor_scalar(kkv, k_, pcol("k_k", i), None, ALU.mult))
                tt(sq, kkv, kkv, ALU.mult, "kk_sq")
                dve.wait_ge(S("low_out"), 3 * i + 2)
                vv.do(dve.tensor_scalar(ld, ld, -0.5 * C_DECAY, -0.5 * C_DECAY, ALU.mult, ALU.add))
                vv.do(dve.tensor_tensor_scan(cum, m_sc[:, :], ld, 0.0, ALU.mult, ALU.add))
                tt(ld, cum, ld, ALU.subtract, "logs")
                vv.do(dve.tensor_scalar(av, av, 0.5, 0.5, ALU.mult, ALU.add))
                ps("ssq")
                vv.do(dve.tensor_scalar(sq, pbank("ssq")[:, 0:T], 1e-24, None, ALU.max), "ring_out")
                ps("s0t")
                vv.do(dve.tensor_copy(qr[:, 640:1152], pbank("s0t")[:, :]), "ring_out")
                dve.wait_ge(S("exps"), 4 * (i + 1))
                vv.do(dve.reciprocal(sq, sq))
                tt(kkv, kkv, sq, ALU.mult)
                vv.do(dve.tensor_scalar(cum, av, -1.0, pcol("k_a", i), ALU.add, ALU.mult))
                stt(cum, cum, 1.0, k_, ALU.add, ALU.mult)
                stt(alp, kkv, -1.0, ld, ALU.mult, ALU.mult)
                stt(ld, r_, pcol("r_k", i), cum, ALU.mult, ALU.mult, "rk_ready")
                tt(kkv, kkv, av, ALU.mult)
                tt(be, kkv, pinv, ALU.mult)
                tt(ka, cum, pinv, ALU.mult)
                tt(rh, r_, pt, ALU.mult)
                for b in range(NB):
                    vv.do(dve.tensor_copy(alm[:, b, 8 * b:8 * b + 8], alp[:, TP + 8 * b:TP + 8 * b + 8]),
                          "ops_ready" if b == NB - 1 else None)
                ps("bonus")
                tt(bon, pbank("bonus")[:, 0:T], v_, ALU.mult, "ring_out")

                def masked(o, name, m, sem="ring_out"):
                    ps(name)
                    m = m[:, :, :] if len(m.shape) == 3 else bmid(m[:, :], NC)
                    tt(c5(o), c5(pbank(name)[:, 0:T]), m, ALU.mult, sem)

                def plain(o, name, n=T):
                    ps(name)
                    vv.do(dve.tensor_copy(o[:, 0:n], pbank(name)[:, 0:n]), "ring_out")

                def plus(o, name, n=T):
                    ps(name)
                    tt(o[:, 0:n], o[:, 0:n], pbank(name)[:, 0:n], ALU.add, "ring_out")

                masked(t_ad, "A", m_ad)
                masked(t_bd, "B", m_bd, None)
                tt(c5(t_bo)[:, 0:NCK], c5(pbank("B")[:, 0:T])[:, 0:NCK], bmid(m_bo[:, :], NCK), ALU.mult, "ring_out")
                masked(t_bk, "Bk", m_st)
                masked(t_cb, "Cb", m_in)
                masked(t_ck, "Ck", m_in)
                plain(be_t, "beT")
                plain(ka_t, "kaT")
                plain(v_t, "vT")
                tt(c5(t_r), c5(t_bd), bmid(m_id[:, :], NC), ALU.add)
                tt(c5(t_rt), c5(t_ad), bmid(m_id[:, :], NC), ALU.add, "r_ready")
                plain(t_a2, "A2")
                plain(t_b2, "B2")
                plus(t_r, "R1")
                plus(t_rt, "RT1")
                plain(t_ad, "A4")
                plain(t_bd, "B4")
                plus(t_r, "R2")
                plus(t_rt, "RT2")
                plain(t_a2, "Q", TP)
                plain(t_b2, "QT", TP)
                plain(t_ad, "Q2", TP)
                plain(t_bd, "QT2", TP)
                plain(t_rt, "QT4", TP)
                plus(t_r, "W1", TP)
                plus(t_r, "W2", TP)
                plus(t_r, "W3", TP)
                for c in range(NCK):
                    plain(xs_, f"X{c}", 64)
                    plain(sa_, f"SA{c}", 64)
                    ps(f"S{c}")
                    pend = pt[:, 64 * c + 63:64 * c + 64]
                    src = pbank(f"S{c}")[:, 0:64]
                    if c:
                        tt(st_pp[c % 2], src, st_pp[(c + 1) % 2], ALU.add)
                        src = st_pp[c % 2]
                    vv.do(dve.tensor_scalar(st_pp[c % 2], src, pend, None, ALU.mult), "ring_out")
                plain(xs_, "X4", 64)
                ps("SA4")
                vv.do(dve.tensor_copy(sa_, pbank("SA4")[:, 0:64]), "ring_out")
                tt(sam, bmid(sa_, NB), bc(m_e8[:, :], HD), ALU.mult)
                tt(vtm, bmid(v_t[:, TP:T], NB), bc(m_e8[:, :], HD), ALU.mult, "sam_ready")
                ps("S4")
                tt(sam, pbank("S4")[:, :].rearrange("p (b v) -> p b v", b=NB), s0t, ALU.add)
                tt(sam, sam, bc(pt[:, TP:T].rearrange("p (b t) -> p b t", b=NB)[:, :, TB - 1], HD), ALU.mult, "ring_out")
                dve.wait_ge(S("state_stored"), 48 * i)
                for n in range(2):
                    ps(f"tr{n}")
                    vv.do(dve.tensor_copy(s_out[:, 512 * n:512 * n + 512], pbank(f"tr{n}")[0:64, :]), "ring_out")
                ps("trp")
                vv.do(dve.tensor_copy(sp_out, pbank("trp")[0:64, 0:128]), "ring_out")
                dve.wait_ge(S("y_ps"), i + 1)
                y, ym, sq = alp, be, ka
                vv.do(dve.tensor_copy(y, bank[6][:, 0:T]), "y_out")
                ps("mean")
                stt(ym, pbank("mean")[:, 0:T], -1.0 / HD, y, ALU.mult, ALU.add, "ring_out")
                tt(sq, ym, ym, ALU.mult, "ym_sq")
                ps("var")
                vv.do(dve.tensor_scalar(sq, pbank("var")[:, 0:T], 1.0 / HD, GN_EPS, ALU.mult, ALU.add), "ring_out")
                dve.wait_ge(S("gn_sqrt"), i + 1)
                vv.do(dve.reciprocal(sq, sq))
                tt(ym, ym, sq, ALU.mult)
                vv.do(dve.tensor_scalar(ym, ym, pcol("lnx_w", i), pcol("lnx_b", i), ALU.mult, ALU.add))
                tt(ym, ym, bon, ALU.add)
                tt(rw[:, ds(i, 1), 0:T].rearrange("p k t -> p (k t)"), ym, gg, ALU.mult, "pair_done")

        def bmid(ap, n):
            return ap.rearrange("p (o t) -> p o t", o=1).broadcast_to([ap.shape[0], n, ap.shape[1]])

        PER_V = {"dve": 40, "kk_sq": 1, "logs": 1, "ring_out": N_OUT, "rk_ready": 1, "ops_ready": 1, "r_ready": 1,
                 "sam_ready": 1, "y_out": 1, "ym_sq": 1, "pair_done": 1}

        def wkv_act(act, aa):
            for n in range(2):
                act.wait_ge(S("last_ps"), n + 1)
                m = 128 if n == 0 else 106
                aa.do(act.activation(sh_stage[0:m, 128 * n:128 * n + 128], bank[4 + n][0:m, 0:128], ACT.Copy), "shift_stage")
            act.wait_ge(S("low_in"), 1)
            aa.do(act.activation(wa_in[0:64, :], wa_in[0:64, :], ACT.Tanh), "sig_g")
            aa.do(act.activation(sg, sg, ACT.Tanh, scale=0.5), "sig_g")
            with aa.loop(0, KW, {"low_out": 3, "exps": 4, "gn_sqrt": 1}) as i:
                act.wait_ge(S("wkv_ps"), NPR * i + 1)
                act.wait_ge(S("kk_sq"), i + 1)
                aa.do(act.activation(t_bo, pbank("z")[:, 0:T], ACT.Tanh, scale=0.5, bias=half_b[:, ds(i, 1)]), "low_out")
                act.wait_ge(S("wkv_ps"), NPR * i + 2)
                aa.do(act.activation(t_bk, pbank("za")[:, 0:T], ACT.Tanh, scale=0.5, bias=half_b[:, ds(i + 8, 1)]), "low_out")
                act.wait_ge(S("wkv_ps"), NPR * i + 3)
                aa.do(act.activation(gg, pbank("g")[:, 0:T], ACT.Copy), "low_out")
                act.wait_ge(S("logs"), i + 1)
                aa.do(act.activation(pt, t_cb, ACT.Exp), "exps")
                aa.do(act.activation(t_ck, t_cb, ACT.Exp, scale=-1.0), "exps")
                aa.do(act.activation(t_bo, t_bo, ACT.Exp), "exps")
                act.wait_ge(S("ring_out"), N_OUT * i + 1)
                aa.do(act.activation(t_bd, t_bd, ACT.Sqrt), "exps")
                act.wait_ge(S("ring_out"), N_OUT * (i + 1))
                aa.do(act.activation(ka, ka, ACT.Sqrt), "gn_sqrt")

        def wkv_pe(pe):
            pe.wait_ge(S("last_rows"), 1)
            pe.transpose(bank[4][:, 0:128], last_t[:, 0:128], ident[:, :]).then_inc(S("last_ps"), 1)
            pe.transpose(bank[5][0:106, 0:128], last_t[:, 128:234], ident[:, :]).then_inc(S("last_ps"), 1)
            pe.wait_ge(S("shift_stage"), 2)
            pe.wait_ge(S("low_ready"), 1)
            with pe.Fori(0, KW) as i:
                done = [0]

                def wait(name, value):
                    value = pe.to_reg(value)
                    pe.wait_ge(S("low_ready"), 1)
                    pe.wait_ge(S(name), value)

                def begin(name, *needs):
                    p = PR[name]
                    assert p == done[0], name
                    if p < 3:
                        wait("ring_out", N_OUT * i)
                    elif p < 6:
                        wait("low_out", 3 * i + p - 2)
                    need = [PR[n] - 2 for n in needs] + ([p - 5] if p >= 6 else [])
                    if need:
                        wait("ring_out", N_OUT * i + max(need))
                    return pbank(name)

                def end(ins):
                    ins.then_inc(S("wkv_ps"), 1)
                    done[0] += 1

                def heads(out, pairs, start=True, stop=True, **kw):
                    for h in range(2):
                        r = slice(64 * h, 64 * h + 64)
                        for n, (a, b) in enumerate(pairs):
                            last = pe.matmul(out[r, :], a[r, :], b[r, :], start=start and n == 0,
                                             stop=stop and n == len(pairs) - 1, **kw)
                    return last

                def each(name, a, b, needs=(), n=NC):
                    o = begin(name, *needs)
                    for c in range(n):
                        s = slice(64 * c, 64 * c + 64)
                        last = heads(o[:, s], [(a[:, s], b[:, s])])
                    end(last)

                begin("z")
                pe.wait_ge(S("pair_in"), 80 * (i + 1))
                end(pe.matmul(pbank("z")[:, 0:T], wlr[0:64, 0:128], wa_in[0:64, :], start=True, stop=True))
                begin("za")
                end(pe.matmul(pbank("za")[:, 0:T], wlr[64:128, 0:128], wa_in[64:128, :], start=True, stop=True))
                begin("g")
                end(pe.matmul(pbank("g")[:, 0:T], wlr[:, 128:256], sg, start=True, stop=True))
                begin("ssq")
                pe.wait_ge(S("kk_sq"), i + 1)
                end(pe.matmul(pbank("ssq")[:, 0:T], blk[:, :], t_bd, start=True, stop=True))
                o = begin("s0t")
                for b in range(NB):
                    last = pe.transpose(o[:, 64 * b:64 * b + 64], s0raw[:, 128 * b:128 * b + 128], ident[0:64, 0:64])
                end(last)
                begin("bonus")
                pe.wait_ge(S("rk_ready"), i + 1)
                end(pe.matmul(pbank("bonus")[:, 0:T], blk[:, :], t_bo, start=True, stop=True))
                wait("ops_ready", i + 1)
                each("A", alp, be)
                each("B", be, alp)
                each("Bk", ka, alp)
                each("Cb", be, rh)
                each("Ck", ka, rh)
                for name, src in (("beT", be), ("kaT", ka), ("vT", v_)):
                    o = begin(name)
                    for c in range(NC):
                        s = slice(64 * c, 64 * c + 64)
                        last = heads(o[:, s], [(src[:, s], m_id[:, :])])
                    end(last)
                each("A2", t_bd, t_ad, ("B",))
                each("B2", t_ad, t_bd)
                wait("r_ready", i + 1)
                each("R1", t_a2, t_r, ("A2",))
                each("RT1", t_b2, t_rt, ("B2",))
                each("A4", t_b2, t_a2)
                each("B4", t_a2, t_b2)
                each("R2", t_ad, t_r, ("A4", "R1"))
                each("RT2", t_bd, t_rt, ("B4", "RT1"))
                each("Q", t_rt, t_bo, ("RT2",), NCK)
                each("QT", t_bo, t_rt, (), NCK)
                each("Q2", t_b2, t_a2, ("QT",), NCK)
                each("QT2", t_a2, t_b2, (), NCK)
                each("QT4", t_ad, t_bd, ("QT2",), NCK)
                each("W1", t_rt, t_r, ("QT4", "R2"), NCK)
                each("W2", t_bd, t_r, ("W1",), NCK)
                each("W3", t_b2, t_r, ("W2",), NCK)
                for c in range(NC):
                    s = slice(64 * c, 64 * c + 64)
                    prev = st_pp[(c + 1) % 2]
                    first = c == 0
                    o = begin(f"X{c}", f"S{c - 1}" if 0 < c < NCK else "W3")
                    if c < NCK:
                        end(heads(o[:, 0:64], [(t_bk[:, s], v_t[:, s])] + ([] if first else [(alp[:, s], prev)])))
                    else:
                        end(heads(o[:, 0:64], [(t_bk[:, s], v_t[:, s])] + [(alm[:, b, :], s0t[:, b, :]) for b in range(NB)]))
                    o = begin(f"SA{c}", f"X{c}")
                    end(heads(o[:, 0:64], [(t_r[:, s], xs_)]))
                    o = begin(f"S{c}", f"SA{c}")
                    if c < NCK:
                        end(heads(o[:, 0:64], [(be_t[:, s], sa_), (ka_t[:, s], v_t[:, s])]))
                        if first:
                            wait("y_out", i)
                        heads(bank[6][:, s], [(sa_, t_cb[:, s]), (v_t[:, s], t_ck[:, s])] + ([] if first else [(prev, rh[:, s])]))
                    else:
                        wait("sam_ready", i + 1)
                        end(heads(o[:, :], [(be_t[:, s], sam.rearrange("p b v -> p (b v)")),
                                            (ka_t[:, s], vtm.rearrange("p b v -> p (b v)"))]))
                        heads(bank[6][:, s], [(sa_, t_cb[:, s]), (v_t[:, s], t_ck[:, s])], stop=False, skip_group_check=True)
                        for b in range(NB):
                            w = slice(TP + 8 * b, TP + 8 * b + 8)
                            last = heads(bank[6][:, w], [(s0t[:, b, :], rh[:, w])], start=False, stop=b == NB - 1,
                                         skip_group_check=True)
                        last.then_inc(S("y_ps"), 1)
                for n in range(2):
                    o = begin(f"tr{n}", "S4")
                    for b in range(4):
                        last = pe.transpose(o[0:64, 128 * b:128 * b + 128], sam[:, 4 * n + b, :], ident[:, :])
                    end(last)
                o = begin("trp", "S3")
                end(pe.transpose(o[0:64, 0:128], st_pp[1], ident[:, :]))
                o = begin("mean")
                pe.wait_ge(S("y_out"), i + 1)
                end(pe.matmul(o[:, 0:T], blk[:, :], alp, start=True, stop=True))
                o = begin("var")
                pe.wait_ge(S("ym_sq"), i + 1)
                end(pe.matmul(o[:, 0:T], blk[:, :], ka, start=True, stop=True))

        gu = wk[:, 0:2560].rearrange("p (k t) -> p k t", k=KW)
        gv = wk[:, 2560:5120].rearrange("p (k t) -> p k t", k=KW)

        def guq_pe(pe):
            with pe.Fori(0, 6) as i:
                for g in range(2):
                    pe_group(pe, U_GUQ + 2 * g, T_GUQ + 2 * g, ah, al_, 2, 4, 4, i)

        def guq_act(act):
            act.wait_ge(S("pair_done"), KW)
            act.wait_ge(S("stored"), 48)
            act.wait_ge(S("state_stored"), 48 * KW)
            for n, dst in enumerate((gu, gv, q)):
                with act.Fori(2 * n, 2 * n + 2) as i:
                    for g in range(2):
                        for h in range(2):
                            hi_unit(act, U_GUQ + 2 * g + 2 + h, 4, i)
                        for c in range(2):
                            t = T_GUQ + 2 * g + c
                            tile_ready(act, U_GUQ + 2 * g + 1, 8, i, c + 1)
                            o = dst[:, ds(4 * i - 8 * n + 2 * g + c, 1), 0:T].rearrange("p k t -> p (k t)")
                            act.activation(o, bank[t % 4][:, 0:T], ACT.Copy if n == 2 else ACT.Gelu_apprx_tanh)\
                                .then_inc(S(f"tile_out{t % 4}"), 1)

        def guq_dve(dve, vv):
            vv.do(dve.memset(q[:, :, T:XT_], 0.0), "q_pad")
            with dve.Fori(0, 6) as i:
                for h in range(4):
                    lo_unit(dve, U_GUQ + 2 + h, 4, i)

        sq_v = mixf[:, 0:2560]
        vtok = mixf[:, 0:3072].rearrange("p (t c) -> p t c", t=3)
        ws_raw = mixf[:, 3072:4096].rearrange("p (g s) -> p g s", g=8)
        ws_t = mixf[:, 4096:5120].rearrange("p (g t) -> p g t", g=8)
        ws_s = zz[0:TS, 0:512].rearrange("p (g t) -> p g t", g=8)
        v_mu, v_rs = zz[:, 640:960], zz[:, 960:1280]
        bs_row = wk[0:1, 2560:5120].rearrange("p (g t) -> p g t", g=8)

        def sgu_pool(pool):
            pool.wait_ge(S("pair_done"), KW)
            pool.dma_start(ws_raw, A["w_s"].rearrange("g t s -> t g s")).then_inc(S("ws_in"), 16)
            pool.wait_ge(S("vt_out"), 6)
            pool.dma_start(O["sgu_v"], vtok[0:TS, 2, :]).then_inc(S("sguv_stored"), 16)
            b_s = A["b_s"].rearrange("(o g) t -> o g t", o=1)
            for c in range(2):
                pool.dma_start(bs_row[:, :, 128 * c:128 * c + 128], b_s).then_inc(S("bs_in"), 16)
            for b in range(NB):
                pool.dma_start(bs_row[:, :, TP + 8 * b:TP + 8 * b + 8], b_s[:, :, 0:8]).then_inc(S("bs_in"), 16)

        def sgu_dve(dve, vv):
            for t in range(4):
                dve.wait_ge(S(f"tile_out{t}"), 14 if t >= 2 else 15)
            gvt = gv.rearrange("p k t -> p t k")
            vv.do(dve.tensor_reduce(v_mu, gvt, AX_X, ALU.add), "v_sum")
            dve.wait_ge(S("sgu_ps"), 1)
            vv.do(dve.tensor_scalar(v_mu, bank[4][:, 0:T], -1.0 / W, None, ALU.mult))
            vv.do(dve.tensor_tensor(gv, gv, bmid(v_mu, KW), ALU.add), "v_centred")
            dve.wait_ge(S("v_squares"), 1)
            vv.do(dve.tensor_reduce(v_rs, sq_v.rearrange("p (k t) -> p t k", k=KW), AX_X, ALU.add), "v_sum")
            dve.wait_ge(S("sgu_ps"), 2)
            vv.do(dve.tensor_scalar(v_rs, bank[5][:, 0:T], 1.0 / W, LN_EPS, ALU.mult, ALU.add), "v_var")
            dve.wait_ge(S("v_std"), 1)
            vv.do(dve.reciprocal(v_rs, v_rs))
            vv.do(dve.tensor_tensor(gv, gv, bmid(v_rs, KW), ALU.mult))
            for k in range(KW):
                vv.do(dve.tensor_scalar(gv[:, k, :], gv[:, k, :], pcol("sgu_g", k), pcol("sgu_b", k), ALU.mult, ALU.add), "v_normed")
            for n in range(2):
                dve.wait_ge(S("sgu_ps"), 9 + n)
                vv.do(dve.tensor_tensor(ws_t[:, 4 * n:4 * n + 4, :], bank[6 + n][:, :].rearrange("p (g t) -> p g t", g=4),
                                        bmid(m_u[:, :], 4), ALU.mult), "ws_out")
            dve.wait_ge(S("sgu_ps"), 11)
            for g in range(8):
                vv.do(dve.tensor_tensor(ws_s[:, g, :].rearrange("p (b t) -> p b t", b=NB), bmid(bank[4][0:TS, 8 * g:8 * g + 8], NB),
                                        bc(m_e8[0:TS, :], 8), ALU.mult), "wss_out")
            for g in range(8):
                dve.wait_ge(S("sgu_ps"), 12 + g)
                vv.do(dve.tensor_tensor(gu[:, g, :], gu[:, g, :], bank[4 + g % 4][:, 0:T], ALU.mult), "gated")
            dve.wait_ge(S("bh_ready"), 1)
            vv.do(dve.tensor_tensor(bl[:, :, :], gu, bh[:, :, :], ALU.subtract), "bl_ready")

        def sgu_act(act, aa):
            act.wait_ge(S("v_centred"), 1)
            aa.do(act.activation(sq_v, wk[:, 2560:5120], ACT.Square), "v_squares")
            act.wait_ge(S("v_var"), 1)
            aa.do(act.activation(v_rs, v_rs, ACT.Sqrt), "v_std")
            for f in range(6):
                act.wait_ge(S("sgu_ps"), 3 + f)
                m = TS if f >= 4 else P
                aa.do(act.activation(vtok[0:m, f // 2, 512 * (f % 2):512 * (f % 2) + 512], bank[4 + f % 4][0:m, :], ACT.Copy), "vt_out")
            act.wait_ge(S("gated"), 8)
            aa.do(act.activation(bh[:, :, :], gu, ACT.Copy), "bh_ready")

        def sgu_pe(pe):
            def end(ins):
                ins.then_inc(S("sgu_ps"), 1)
            pe.wait_ge(S("v_sum"), 1)
            end(pe.matmul(bank[4][:, 0:T], ones[:, :], v_mu, start=True, stop=True))
            pe.wait_ge(S("v_sum"), 2)
            end(pe.matmul(bank[5][:, 0:T], ones[:, :], v_rs, start=True, stop=True))
            for f in range(6):
                pe.wait_ge(S("v_normed"), KW)
                if f >= 4:
                    pe.wait_ge(S("vt_out"), f - 3)
                m, t0 = (TS, TP) if f >= 4 else (P, 128 * (f // 2))
                for k in range(4):
                    last = pe.transpose(bank[4 + f % 4][0:m, 128 * k:128 * k + 128], gv[:, 4 * (f % 2) + k, t0:t0 + m], ident[:, :])
                end(last)
            pe.wait_ge(S("ws_in"), 16)
            for n in range(2):
                pe.wait_ge(S("vt_out"), 3 + n)
                for k in range(4):
                    last = pe.transpose(bank[6 + n][:, 128 * k:128 * k + 128], ws_raw[:, 4 * n + k, :], ident[:, :])
                end(last)
            pe.wait_ge(S("vt_out"), 6)
            pe.wait_ge(S("ws_out"), 2)
            end(pe.matmul(bank[4][0:TS, 0:64], rep8[:, :], ws_t[0:8, :, 0:8], start=True, stop=True))
            pe.wait_ge(S("bs_in"), 160)
            pe.wait_ge(S("wss_out"), 8)
            for g in range(8):
                if g >= 4:
                    pe.wait_ge(S("gated"), g - 3)
                o, c = bank[4 + g % 4], slice(128 * g, 128 * g + 128)
                pe.matmul(o[:, 0:T], ones[0:1, :], bs_row[:, g, :], start=True, stop=False, skip_group_check=True)
                for t in range(2):
                    pe.matmul(o[:, 128 * t:128 * t + 128], vtok[:, t, c], ws_t[:, g, :], start=False, stop=False, skip_group_check=True)
                end(pe.matmul(o[:, TP:T], vtok[0:TS, 2, c], ws_s[:, g, :], start=False, stop=True, skip_group_check=True))

        kb = wk[:, 0:2048].rearrange("p (m c) -> p m c", m=2)
        vb = wk[:, 2048:4096].rearrange("p (m c) -> p m c", m=2)
        kt = mixf[:, 0:2048].rearrange("p (d m) -> p d m", d=KW)
        pr_, pr_t = zz[:, 0:256], zz[:, 256:512]
        qb = zz[:, 512:768].rearrange("p (k t) -> p k t", k=KW)
        o_tok = zz[:, 768:1024]
        mx, nmx, rsum, rinv = [zz[:, 1300 + n:1301 + n] for n in range(4)]
        XSCALE = float(W // XH) ** -0.5
        SAMPLE_FILLS = 8

        def attn_pool(pool):
            for b in range(NB + 1):
                if b == 0:
                    pool.wait_ge(S("bl_ready"), 1)
                if b == NB:
                    for t in range(4):
                        pool.wait_ge(S(f"mem_stored{t}"), 32)
                for n, (dst, cache, mem, sem) in enumerate(((kb, "cache_mem_k", "mem_k", "k_in"), (vb, "cache_mem_v", "mem_v", "v_in"))):
                    if b:
                        pool.wait_ge(S("at_ps"), SAMPLE_FILLS * (b - 1) + (7 if n else 4))
                    src = A[cache][b].rearrange("(m p) h d -> p m (h d)", p=P) if b < NB else \
                        O[mem].rearrange("(m p) c -> p m c", p=P)
                    pool.dma_start(dst, src).then_inc(S(sem), 16)

        def softmax_dve(dve, vv, n, n_ps):
            dve.wait_ge(S("at_ps"), n_ps)
            vv.do(dve.tensor_reduce(mx, bank[4][:, 0:MEM], AX_X, ALU.max))
            vv.do(dve.tensor_scalar(nmx, mx, -XSCALE, None, ALU.mult), "nmax")
            dve.wait_ge(S("exp_done"), n + 1)
            vv.do(dve.reciprocal(rinv, rsum))
            vv.do(dve.tensor_scalar(pr_, pr_, rinv, None, ALU.mult), "p_ready")

        def attn_dve(dve, vv):
            for b in range(NB):
                base = SAMPLE_FILLS * b
                vv.do(dve.tensor_copy(qb, q[:, :, TP + 8 * b:TP + 8 * b + 32]), "qb")
                softmax_dve(dve, vv, b, base + 5)
                dve.wait_ge(S("at_ps"), base + 6)
                vv.do(dve.tensor_copy(pr_t, bank[5][:, 0:MEM]), "at_v")
                dve.wait_ge(S("at_ps"), base + 7)
                vv.do(dve.tensor_copy(o_tok, bank[6][:, 0:MEM]), "at_v")
                dve.wait_ge(S("at_ps"), base + 8)
                o = bank[7][:, 0:256].rearrange("p (d h t) -> p h d t", d=2, h=4)[:, :, :, 0:8]
                vv.do(dve.tensor_copy(q[:, :, TP + 8 * b:TP + 8 * b + 8].rearrange("p (h d) t -> p h d t", d=2), o), "at_v")
            base = SAMPLE_FILLS * NB + 4
            for n in range(8):
                h, t = n // 2, n % 2
                softmax_dve(dve, vv, NB + n, base + 3 * n + 1)
                dve.wait_ge(S("at_ps"), base + 3 * n + 2)
                vv.do(dve.tensor_copy(pr_t, bank[5][:, 0:MEM]), "at_v")
                dve.wait_ge(S("at_ps"), base + 3 * n + 3)
                vv.do(dve.tensor_copy(q[:, 2 * h:2 * h + 2, 128 * t:128 * t + 128],
                                      bank[6][:, 0:256].rearrange("p (d t) -> p d t", d=2)), "at_v")

        def attn_act(act, aa):
            def kts(base):
                for f in range(4):
                    act.wait_ge(S("at_ps"), base + f + 1)
                    aa.do(act.activation(kt[:, 2 * f:2 * f + 2, :], bank[4 + f][:, :].rearrange("p (d m) -> p d m", d=2), ACT.Copy), "kt_out")

            def exps(n):
                act.wait_ge(S("nmax"), n + 1)
                aa.do(act.activation(pr_, bank[4][:, 0:MEM], ACT.Exp, bias=nmx, scale=XSCALE, accum_out=rsum), "exp_done")

            act.wait_ge(S("sguv_stored"), 16)
            for b in range(NB):
                kts(SAMPLE_FILLS * b)
                exps(b)
            kts(SAMPLE_FILLS * NB)
            for n in range(8):
                exps(NB + n)

        def attn_pe(pe):
            def end(ins):
                ins.then_inc(S("at_ps"), 1)

            def transposes(b):
                pe.wait_ge(S("k_in"), 16 * (b + 1))
                if b == 0:
                    pe.wait_ge(S("gated"), 8)
                else:
                    pe.wait_ge(S("exp_done"), b)
                    pe.wait_ge(S("at_v"), 3 * b)
                for f in range(4):
                    for a in range(2):
                        for m in range(2):
                            c = 128 * (2 * f + a)
                            last = pe.transpose(bank[4 + f][:, 256 * a + 128 * m:256 * a + 128 * m + 128], kb[:, m, c:c + 128], ident[:, :])
                    end(last)

            def turn_p(n, nv):
                pe.wait_ge(S("p_ready"), n + 1)
                pe.wait_ge(S("at_v"), nv)
                for m in range(2):
                    last = pe.transpose(bank[5][:, 128 * m:128 * m + 128], pr_[:, 128 * m:128 * m + 128], ident[:, :])
                end(last)

            pe.wait_ge(S("q_pad"), 1)
            for b in range(NB):
                transposes(b)
                pe.wait_ge(S("kt_out"), 4 * (b + 1))
                pe.wait_ge(S("qb"), b + 1)
                for h in range(XH):
                    for d in range(2):
                        last = pe.matmul(bank[4][32 * h:32 * h + 32, 0:MEM], qb[:, 2 * h + d, :], kt[:, 2 * h + d, :],
                                         start=d == 0, stop=d == 1)
                end(last)
                turn_p(b, 3 * b)
                pe.wait_ge(S("at_v"), 3 * b + 1)
                pe.wait_ge(S("v_in"), 16 * (b + 1))
                for h in range(XH):
                    for m in range(2):
                        last = pe.matmul(bank[6][32 * h:32 * h + 32, 0:256], pr_t[:, 128 * m + 32 * h:128 * m + 32 * h + 32],
                                         vb[:, m, 256 * h:256 * h + 256], start=m == 0, stop=m == 1)
                end(last)
                pe.wait_ge(S("at_v"), 3 * b + 2)
                for d in range(2):
                    last = pe.transpose(bank[7][:, 128 * d:128 * d + 128], o_tok[:, 128 * d:128 * d + 128], ident[:, :])
                end(last)
            transposes(NB)
            pe.wait_ge(S("kt_out"), 4 * (NB + 1))
            for n in range(8):
                h, t = n // 2, n % 2
                pe.wait_ge(S("exp_done"), NB + n)
                for d in range(2):
                    last = pe.matmul(bank[4][:, 0:MEM], q[:, 2 * h + d, 128 * t:128 * t + 128], kt[:, 2 * h + d, :],
                                     start=d == 0, stop=d == 1)
                end(last)
                turn_p(NB + n, 3 * NB + 2 * n)
                pe.wait_ge(S("at_v"), 3 * NB + 2 * n + 1)
                pe.wait_ge(S("v_in"), 16 * (NB + 1))
                for c in range(2):
                    for m in range(2):
                        last = pe.matmul(bank[6][:, 128 * c:128 * c + 128], vb[:, m, 256 * h + 128 * c:256 * h + 128 * c + 128],
                                         pr_t[:, 128 * m:128 * m + 128], start=m == 0, stop=m == 1)
                end(last)

        def branch_pe(pe):
            for n in range(3):
                pe.wait_ge(S("bl_ready"), n + 1)
                u, t = U_BR[n], T_BR[n]
                with pe.Fori(0, 4) as i:
                    for g in range(2):
                        pe_group(pe, u + 3 * g, t + 4 * g, ah, al_, 2, 6, 8, i)
                        pe_group(pe, u + 3 * g + 2, t + 4 * g + 2, bh, bl, 1, 6, 8, i)

        def branch_src(n):
            return q[:, :, 0:T] if n == 1 else rw[:, 0:KW, 0:T]

        def branch_act(act, aa):
            for n in range(3):
                u, t = U_BR[n], T_BR[n]
                if n:
                    tile_ready(act, u - 1)
                    act.wait_ge(S("at_v"), 3 * NB + 16)
                    aa.do(act.activation(bh[:, :, :], branch_src(n), ACT.Copy), "bh_ready")
                with act.Fori(0, 4) as i:
                    for g in range(2):
                        hi_unit(act, u + 3 * g + 2, 6, i)
                        hi_unit(act, u + 3 * g + 3, 6, i)
                        for c in range(2):
                            tl = t + 4 * g + c
                            tile_ready(act, u + 3 * g + 1, 12, i, c + 1)
                            act.wait_ge(S("gate_free"), 4 * i + 16 * n + 2 * g + c + 1)
                            act.activation(gs[:, 2 * g + c, :], bank[tl % 4][:, 0:T], ACT.Tanh, scale=0.5)\
                                .then_inc(S(f"tile_out{tl % 4}"), 1)
                        hi_unit(act, u + 3 * g + 4, 6, i)

        def branch_dve(dve, vv):
            vv.do(dve.memset(mixf, 0.0))
            for c in range(4):
                vv.do(dve.memset(gs[:, c, :], 0.0), "gate_free")
            for n in range(3):
                u, t = U_BR[n], T_BR[n]
                if n:
                    dve.wait_ge(S("bh_ready"), n + 1)
                    vv.do(dve.tensor_tensor(bl[:, :, :], branch_src(n), bh[:, :, :], ALU.subtract), "bl_ready")
                with vv.loop(0, 4, {"gate_free": 4}) as i:
                    for g in range(2):
                        for h in range(3):
                            lo_unit(dve, u + 3 * g + 2 + h, 6, i)
                        for c in range(2):
                            tg, tb = t + 4 * g + c, t + 4 * g + 2 + c
                            dve.wait_ge(S(f"tile_out{tg % 4}"), 2 * i + tg // 4 + 1)
                            tile_ready(dve, u + 3 * g + 2, 12, i, c + 1)
                            gate = gs[:, 2 * g + c, :]
                            dve.scalar_tensor_tensor(out=gate, in0=gate, scalar=1.0, in1=bank[tb % 4][:, 0:T],
                                                     op0=ALU.add, op1=ALU.mult).then_inc(S(f"tile_out{tb % 4}"), 1)
                            dve.wait_ge(S(f"tile_out{tb % 4}"), 2 * i + tb // 4 + 1)
                            m = mix[:, ds(4 * i + 2 * g + c, 1), :].rearrange("p k t -> p (k t)")
                            vv.do(dve.tensor_tensor(m, m, gate, ALU.add), "gate_free")

        mo = wk[:, 0:5120].rearrange("p (k t) -> p k t", k=KD)

        def out_pe(pe):
            pe.wait_ge(S("mx_lo"), 4)
            with pe.Fori(0, 4) as i:
                for g in range(2):
                    pe_group(pe, U_OUT + 2 * g, T_OUT + 2 * g, ah, al_, 2, 4, 4, i)

        def out_act(act, aa):
            act.wait_ge(S("gate_free"), 52)
            tile_ready(act, U_OUT - 1)
            for c in range(4):
                aa.do(act.activation(ah[:, 4 * c:4 * c + 4, :], mix[:, 4 * c:4 * c + 4, :], ACT.Copy, scale=0.5), "mx_hi")
            with act.Fori(0, 4) as i:
                for g in range(2):
                    for h in range(2):
                        hi_unit(act, U_OUT + 2 * g + 2 + h, 4, i)
                    for c in range(2):
                        t = T_OUT + 2 * g + c
                        tile_ready(act, U_OUT + 2 * g + 1, 8, i, c + 1)
                        act.activation(mo[:, ds(4 * i + 2 * g + c, 1), :].rearrange("p k t -> p (k t)"),
                                       bank[t % 4][:, 0:T], ACT.Copy).then_inc(S(f"tile_out{t % 4}"), 1)

        def out_dve(dve, vv):
            for c in range(4):
                dve.wait_ge(S("mx_hi"), c + 1)
                vv.do(dve.scalar_tensor_tensor(out=al_[:, 4 * c:4 * c + 4, :], in0=mix[:, 4 * c:4 * c + 4, :], scalar=0.5,
                                               in1=ah[:, 4 * c:4 * c + 4, :], op0=ALU.mult, op1=ALU.subtract), "mx_lo")
            with dve.Fori(0, 4) as i:
                for h in range(4):
                    lo_unit(dve, U_OUT + 2 + h, 4, i)

        red, rstd = gs[:, 0, :], gs[:, 1, :]

        def rms_act(act, aa, n, src, sq):
            aa.do(act.activation(sq, src, ACT.Square), "rms_squares")
            act.wait_ge(S("rms_mean"), n + 1)
            aa.do(act.activation(rstd, rstd, ACT.Sqrt), "rms_root")

        def rms_dve(dve, vv, n, sq):
            dve.wait_ge(S("rms_squares"), n + 1)
            vv.do(dve.tensor_reduce(red, sq.rearrange("p (k t) -> p t k", k=KD), AX_X, ALU.add), "rms_sum")
            dve.wait_ge(S("rms_ps"), n + 1)
            vv.do(dve.tensor_scalar(rstd, bank[4][:, 0:T], 1.0 / D, RMS_EPS, ALU.mult, ALU.add), "rms_mean")
            dve.wait_ge(S("rms_root"), n + 1)
            vv.do(dve.reciprocal(rstd, rstd), "rms_ready_t")

        def rms_pe(pe, n):
            pe.wait_ge(S("rms_sum"), n + 1)
            pe.matmul(bank[4][:, 0:T], ones[:, :], red, start=True, stop=True).then_inc(S("rms_ps"), 1)

        x2_tok = [rwr[:, 0:D], rwr[:, D:2 * D], rwr[0:TS, 2 * D:3 * D]]
        cst_raw = qr[:, 0:11 * P]
        cst = rwr[:, 5552:5552 + 16 * 88].rearrange("p (r k) -> p r k", r=16)
        tail = rwr[:, 6960:6960 + 18 * 88].rearrange("p (r k) -> p r k", r=18)

        def res_pool(pool):
            pool.wait_ge(S("bl_ready"), 3)
            for k in range(2):
                pool.dma_start(x2_tok[k], A["x_prompt"][128 * k:128 * k + 128, :]).then_inc(S("x2_in"), 16)
            pool.dma_start(x2_tok[2], A["x_sample"]).then_inc(S("x2_in"), 16)
            pool.dma_start(cst_raw.rearrange("p (j n) -> p j n", n=P),
                           A["state_ffn_conv"].rearrange("b r (k c) -> (b r k) c", c=P).rearrange("(j p) c -> p j c", p=P))\
                .then_inc(S("x2_in"), 16)

        def res_act(act, aa):
            for t in range(4):
                act.wait_ge(S(f"tile_out{t}"), T_FFN // 4 + (1 if t < T_FFN % 4 else 0))
            act.wait_ge(S("mx_lo"), 4)
            rms_act(act, aa, 0, wk[:, 0:5120], mixf)
            act.wait_ge(S("h_ready"), KD)
            rms_act(act, aa, 1, mixf, wk[:, 0:5120])
            for f in range(3):
                act.wait_ge(S("cst_ps"), f + 1)
                w = 512 if f < 2 else 384
                aa.do(act.activation(rwr[:, 5552 + 512 * f:5552 + 512 * f + w], bank[4 + f][:, 0:w], ACT.Copy), "cst_out")
            for c in range(4):
                act.wait_ge(S("hn"), 4 * (c + 1))
                aa.do(act.activation(ah[:, 4 * c:4 * c + 4, :], mo[:, 4 * c:4 * c + 4, :], ACT.Copy), "hn_hi")

        def res_dve(dve, vv):
            rms_dve(dve, vv, 0, mixf)
            for k in range(KD):
                vv.do(dve.scalar_tensor_tensor(out=mo[:, k, :], in0=mo[:, k, :], scalar=pcol("g_post_mix", k), in1=rstd,
                                               op0=ALU.mult, op1=ALU.mult))
                dve.wait_ge(S("res_ps"), k + 1)
                vv.do(dve.tensor_tensor(mix[:, k, :], mo[:, k, :], bank[4 + k % 4][:, 0:T], ALU.add), "h_ready")
            rms_dve(dve, vv, 1, wk[:, 0:5120])
            for c in range(4):
                for k in range(4 * c, 4 * c + 4):
                    vv.do(dve.scalar_tensor_tensor(out=mo[:, k, :], in0=mix[:, k, :], scalar=pcol("g_pre_ffn", k), in1=rstd,
                                                   op0=ALU.mult, op1=ALU.mult), "hn")
            for c in range(4):
                dve.wait_ge(S("hn_hi"), c + 1)
                vv.do(dve.tensor_tensor(al_[:, 4 * c:4 * c + 4, :], mo[:, 4 * c:4 * c + 4, :], ah[:, 4 * c:4 * c + 4, :],
                                        ALU.subtract), "hn_lo")
            vv.do(dve.memset(wk[:, 0:5120], 0.0))
            vv.do(dve.memset(ext[:, :, 0:2], 0.0))
            vv.do(dve.memset(rwr[:, 1352:4056], 0.0), "ext_set")

        def res_pe(pe):
            rms_pe(pe, 0)
            pe.wait_ge(S("x2_in"), 64)
            for k in range(KD):
                if k >= 4:
                    pe.wait_ge(S("h_ready"), k - 3)
                else:
                    pe.wait_ge(S("rms_ready_t"), 1)
                x_transposes(pe, x2_tok, k, bank[4 + k % 4]).then_inc(S("res_ps"), 1)
            pe.wait_ge(S("h_ready"), KD)
            rms_pe(pe, 1)
            pe.wait_ge(S("rms_ready_t"), 2)
            for f in range(3):
                for j in range(4 * f, min(4 * f + 4, 11)):
                    last = pe.transpose(bank[4 + f][:, 128 * (j % 4):128 * (j % 4) + 128], cst_raw[:, 128 * j:128 * j + 128], ident[:, :])
                last.then_inc(S("cst_ps"), 1)

        ext = rwr[:, 0:1352].rearrange("p (k t) -> p k t", k=4)
        cgate = rwr[:, 1352:2704].rearrange("p (k t) -> p k t", k=4)
        cval = rwr[:, 2704:4056].rearrange("p (k t) -> p k t", k=4)
        facc = mo
        UF, TF = U_FFN, T_FFN

        def smp_c(t):
            return t[:, :, TP + 2:CEXT].rearrange("p k (b t) -> p k b t", b=NB)

        def up_pe(pe, u, t, k=0, i=0):
            for g in range(2):
                pe_group(pe, u + 2 * g, t + 2 * g, ah, al_, 2, 12 if k else 0, 24 if k else 0, i)

        def down_pe(pe, u, t, k=0, i=0, c=0):
            pe.wait_ge(S("ff_lo"), lin(c, 2 if k else 0, i))
            for g in range(4):
                pe.wait_ge(S("lo_done"), lin(u + g + 1, 12 if k else 0, i))
                s = (u + g) % NS
                for c4 in range(4):
                    tt = t + 4 * g + c4
                    bank_free(pe, tt, 24 if k else 0, i)
                    for kk in range(4):
                        o = 512 * kk + 128 * c4
                        last = three(pe, bank[tt % 4][:, 0:T], hi[s][:, o:o + P], lo[s][:, o:o + P],
                                     bh[:, kk, :], bl[:, kk, :], kk == 0, kk == 3)
                    last.then_inc(S("parts"), 1)

        def ffn_pe(pe):
            pe.wait_ge(S("hn_lo"), 4)
            up_pe(pe, UF, TF)
            up_pe(pe, UF + 4, TF + 4)
            with pe.Fori(0, NCH - 1) as i:
                up_pe(pe, UF + 8, TF + 8, 1, i)
                down_pe(pe, UF + 12, TF + 12, 1, i, 2)
                up_pe(pe, UF + 16, TF + 28, 1, i)
            down_pe(pe, U_END - 4, T_FFN + 8 + 24 * (NCH - 1), 0, 0, 2 * NCH)

        def ffn_act(act, aa):
            def up(u, t, half, k=0, i=0):
                uk, tk, pk = (12, 24, 32) if k else (0, 0, 0)
                act.wait_ge(S("ext_free"), lin(half, 2 if k else 0, i))
                for g in range(2):
                    for h in range(2):
                        hi_unit(act, u + 2 * g + 2 + h, uk, i, pk)
                    for c in range(2):
                        l, b = 2 * g + c, (t + 2 * g + c) % 4
                        tile_ready(act, u + 2 * g + 1, pk, i, c + 1)
                        act.activation(ext[:, l, 2:2 + TP], bank[b][:, 0:TP], ACT.Copy)
                        act.activation(smp_c(ext)[:, l, :, 2:2 + TB], bank[b][:, TP:T].rearrange("p (b t) -> p b t", b=NB),
                                       ACT.Copy).then_inc(S(f"tile_out{b}"), 1)

            def gate():
                act.wait_ge(S("gate_conv"), aa.value("gate_act") + 1)
                aa.do(act.activation(rwr[:, 1352:2704], rwr[:, 1352:2704], ACT.Gelu_apprx_tanh), "gate_act")

            def split():
                n = aa.value("ff_hi")
                act.wait_ge(S("ff"), aa.value("gate_act"))
                aa.do(act.activation(bh[:, 0:4, 0:TP], cval[:, :, 0:TP], ACT.Copy), "ff_hi")
                for l in range(4):
                    aa.do(act.activation(bh[:, l, TP:T].rearrange("p (b t) -> p b t", b=NB), smp_c(cval)[:, l, :, 0:TB], ACT.Copy),
                          "ff_hi")

            act.wait_ge(S("ext_set"), 1)
            up(UF, TF, 0)
            gate()
            up(UF + 4, TF + 4, 1)
            split()
            with aa.loop(0, NCH - 1, {"gate_act": 1, "ff_hi": 5}) as i:
                up(UF + 8, TF + 8, 2, 1, i)
                gate()
                for g in range(4):
                    hi_unit(act, UF + 12 + g + 2, 12, i, 32)
                up(UF + 16, TF + 28, 3, 1, i)
                split()
            for g in range(2):
                hi_unit(act, U_END - 2 + g)

        def ffn_dve(dve, vv):
            def conv(t, half, dst, k=0, i=0):
                tk = 24 if k else 0
                for l in range(4):
                    dve.wait_ge(S(f"tile_out{(t + l) % 4}"), lin((t + l) // 4 + 1, tk // 4, i))
                tile0 = KF * half + (4 if k else 0)

                def cols(n):
                    c = tile0 + n
                    return ds(4 * i + c, 4) if k else slice(c, c + 4)

                for r in range(2):
                    vv.do(dve.tensor_copy(smp_c(ext)[:, :, :, r],
                                          cst.rearrange("p (b r) k -> p r k b", r=2)[:, r, cols(0), :]))
                for l in range(4):
                    for j in range(3):
                        w = COL["conv_w"] + 88 * j + tile0 + l
                        w = prm[:, ds(4 * i + w, 1)] if k else prm[:, w:w + 1]
                        o, x = dst[:, l, 0:336], ext[:, l, j:j + 336]
                        if j == 0:
                            b = COL["conv_b"] + tile0 + l
                            b = prm[:, ds(4 * i + b, 1)] if k else prm[:, b:b + 1]
                            vv.do(dve.tensor_scalar(o, x, w, b, ALU.mult, ALU.add))
                        else:
                            vv.do(dve.scalar_tensor_tensor(out=o, in0=x, scalar=w, in1=o, op0=ALU.mult, op1=ALU.add),
                                  "gate_conv" if j == 2 and l == 3 and not half else None)
                vv.do(dve.tensor_copy(tail.rearrange("p r k -> p k r")[:, cols(0), 0:2], ext[:, :, TP:TP + 2]))
                for r in range(2):
                    vv.do(dve.tensor_copy(tail[:, 2:18, :].rearrange("p (b r) k -> p r k b", r=2)[:, r, cols(0), :],
                                          smp_c(ext)[:, :, :, TB + r]), "ext_free" if r else None)

            def value():
                dve.wait_ge(S("gate_act"), vv.value("ff") + 1)
                vv.do(dve.tensor_tensor(rwr[:, 2704:4056], rwr[:, 2704:4056], rwr[:, 1352:2704], ALU.mult), "ff")

            def split():
                dve.wait_ge(S("ff_hi"), 5 * vv.value("ff"))
                vv.do(dve.tensor_tensor(bl[:, 0:4, 0:TP], cval[:, :, 0:TP], bh[:, 0:4, 0:TP], ALU.subtract))
                for l in range(4):
                    vv.do(dve.tensor_tensor(bl[:, l, TP:T].rearrange("p (b t) -> p b t", b=NB), smp_c(cval)[:, l, :, 0:TB],
                                            bh[:, l, TP:T].rearrange("p (b t) -> p b t", b=NB), ALU.subtract),
                          "ff_lo" if l >= 2 else None)

            def los(u, n, k=0, i=0):
                for h in range(n):
                    lo_unit(dve, u + h + 2, 12 if k else 0, i, 32 if k else 0)

            def down(u, t, k=0, i=0):
                for g in range(4):
                    for c in range(4):
                        tt = t + 4 * g + c
                        b = tt % 4
                        tile_done = parts_of(u + g) - 3 + c
                        dve.wait_ge(S("parts"), lin(tile_done, 32 if k else 0, i))
                        f = facc[:, 4 * g + c, :]
                        dve.tensor_tensor(f, f, bank[b][:, 0:T], ALU.add).then_inc(S(f"tile_out{b}"), 1)
                        dve.wait_ge(S(f"tile_out{b}"), lin(tt // 4 + 1, 6 if k else 0, i))
                    los(u + g, 1, k, i)

            los(UF, 4)
            conv(TF, 0, cgate)
            los(UF + 4, 4)
            conv(TF + 4, 1, cval)
            value()
            split()
            with vv.loop(0, NCH - 1, PER_F) as i:
                los(UF + 8, 4, 1, i)
                conv(TF + 8, 0, cgate, 1, i)
                down(UF + 12, TF + 12, 1, i)
                los(UF + 16, 4, 1, i)
                conv(TF + 28, 1, cval, 1, i)
                value()
                split()
            down(U_END - 4, T_FFN + 8 + 24 * (NCH - 1))

        PER_F = {"dve": 34, "gate_conv": 1, "ext_free": 2, "ff": 1, "ff_lo": 2}

        y_stage = [rwr[:, 0:D], rwr[:, D:2 * D], rwr[0:TS, 2 * D:3 * D]]
        tail_stage = raw[0]

        def end_act(act, aa):
            for t in range(4):
                act.wait_ge(S(f"tile_out{t}"), 434 // 4 + (1 if t < 434 % 4 else 0))
            rms_act(act, aa, 2, wk[:, 0:5120], rwr[:, 0:5120])
            for f in range(4):
                act.wait_ge(S("tail_ps"), f + 1)
                w = 512 if f < 3 else 128
                aa.do(act.activation(tail_stage[:, 512 * f:512 * f + w], bank[4 + f][:, 0:w], ACT.Copy), "tail_out")
            for f in range(12):
                c, k = f // 3, f % 3
                act.wait_ge(S("y_ps"), KW + f + 1)
                m = TS if k == 2 else P
                aa.do(act.activation(y_stage[k][:, 512 * c:512 * c + 512], bank[4 + f % 4][0:m, :], ACT.Copy), "y_staged")

        def end_dve(dve, vv):
            rms_dve(dve, vv, 2, rwr[:, 0:5120])
            for k in range(KD):
                vv.do(dve.scalar_tensor_tensor(out=facc[:, k, :], in0=facc[:, k, :], scalar=pcol("g_post_ffn", k), in1=rstd,
                                               op0=ALU.mult, op1=ALU.mult))
                vv.do(dve.tensor_tensor(facc[:, k, :], facc[:, k, :], mix[:, k, :], ALU.add), "y_ready")

        def end_pe(pe):
            rms_pe(pe, 2)
            pe.wait_ge(S("rms_ready_t"), 3)
            tails = rwr[:, 6960:6960 + 18 * 88]
            pieces = [(0, 128), (128, 48)] + [(176 + 128 * j, 128) for j in range(11)]
            pe.wait_ge(S("ext_free"), 2 * NCH)
            for n, (at, m) in enumerate(pieces):
                last = pe.transpose(bank[4 + n // 4][0:m, 128 * (n % 4):128 * (n % 4) + 128], tails[:, at:at + m], ident[:, :])
                if n % 4 == 3 or n == len(pieces) - 1:
                    last.then_inc(S("tail_ps"), 1)
            for f in range(12):
                c, k = f // 3, f % 3
                pe.wait_ge(S("y_ready"), 4 * c + 4)
                if f < 4:
                    pe.wait_ge(S("tail_out"), f + 1)
                else:
                    pe.wait_ge(S("y_staged"), f - 3)
                m = TS if k == 2 else P
                for j in range(4):
                    last = pe.transpose(bank[4 + f % 4][0:m, 128 * j:128 * j + 128], facc[:, 4 * c + j, 128 * k:128 * k + m], ident[:, :])
                last.then_inc(S("y_ps"), 1)

        def end_pool(pool):
            pool.wait_ge(S("tail_out"), 4)
            pool.dma_start(O["conv_p"][0:128, :], tail_stage[:, 0:128]).then_inc(S("stored"), 16)
            pool.dma_start(O["conv_p"][128:176, :], tail_stage[0:48, 128:256]).then_inc(S("stored"), 16)
            pool.dma_start(O["conv_s"].rearrange("(j p) n -> p j n", p=P),
                           tail_stage[:, 256:256 + 11 * P].rearrange("p (j n) -> p j n", n=P)).then_inc(S("stored"), 16)
            for k in range(3):
                pool.wait_ge(S("y_staged"), 10 + k)
                pool.dma_start(O["y_p"][128 * k:128 * k + 128, :] if k < 2 else O["y_s"], y_stage[k]).then_inc(S("stored"), 16)
            pool.wait_ge(S("stored"), 16 * 9)
            pool.wait_ge(S("sguv_stored"), 16)
            pool.wait_ge(S("state_stored"), 48 * KW)
            for t in range(4):
                pool.wait_ge(S(f"mem_stored{t}"), 32)

        @block.gpsimd
        def _(pool):
            pp = Prog(pool, S, "pool")
            pool_loads(pool)
            pool_constants(pool, pp)
            mem_pool(pool)
            wkv_pool(pool)
            sgu_pool(pool)
            attn_pool(pool)
            res_pool(pool)
            end_pool(pool)

        @block.sync
        def _(sp):
            for u in range(16):
                g = u // 4
                load_unit(sp, kv(A["w_mem_k"] if g < 2 else A["w_mem_v"], 4 * (u % 4), 512 * (g % 2), 4, 512), u)
            for h in range(2):
                load_unit(sp, kv(A["w_in"], 8 * h, 0), U_RW + h)
            with sp.Fori(0, 12) as i:
                for g in range(2):
                    for h in range(2):
                        load_unit(sp, kv(A["w_in"], 8 * h, 512 * i + 256 * (g + 1)), U_RW + 2 + 2 * g + h, 4, i)
            for n, b in enumerate((1, 2, 0)):
                with sp.Fori(0, 4) as i:
                    for g in range(2):
                        for h in range(2):
                            load_unit(sp, kv(A["w_in"], 8 * h, 512 * i + NSH + 3 * W + D * b + 256 * g), U_BR[n] + 3 * g + h, 6, i)
                        load_unit(sp, kv(A["w_branch"][b], 0, 512 * i + 256 * g), U_BR[n] + 3 * g + 2, 6, i)
            with sp.Fori(0, 4) as i:
                for g in range(2):
                    for h in range(2):
                        load_unit(sp, kv(A["w_out"], 8 * h, 512 * i + 256 * g), U_OUT + 2 * g + h, 4, i)

            def up(half, c, k, i):
                for g in range(2):
                    for h in range(2):
                        n0 = half * DFF + 256 * g + (512 if k else 0)
                        load_unit(sp, kv(A["w_up"], 8 * h, lin(n0, 512 if k else 0, i)), c + 2 * g + h, 12 if k else 0, i)

            def down(rows, c, k, i):
                src = A["w_down"].rearrange("(c kt p) n -> p c kt n", kt=4, p=P)
                for g in range(4):
                    cc = ds(i, 1) if k else slice(rows, rows + 1)
                    load_unit(sp, src[:, cc, :, 512 * g:512 * g + 512].rearrange("p c kt n -> p (c kt) n"), c + g, 12 if k else 0, i)

            up(0, UF, 0, 0)
            up(1, UF + 4, 0, 0)
            with sp.Fori(0, NCH - 1) as i:
                up(0, UF + 8, 1, i)
                down(0, UF + 12, 1, i)
                up(1, UF + 16, 1, i)
            down(NCH - 1, U_END - 4, 0, 0)

        @block.scalar
        def _(act):
            aa = Prog(act, S, "act")
            entry_act(act, aa)
            for u in range(NS):
                hi_unit(act, u)
            mem_act(act)
            split_x_act(act, aa)
            rw_act(act)
            wkv_act(act, aa)
            guq_act(act)
            sgu_act(act, aa)
            attn_act(act, aa)
            branch_act(act, aa)
            out_act(act, aa)
            res_act(act, aa)
            ffn_act(act, aa)
            end_act(act, aa)

        @block.vector
        def _(dve):
            vv = Prog(dve, S, "dve")
            entry_dve(dve, vv)
            for u in range(NS):
                lo_unit(dve, u)
            mem_dve(dve)
            split_x_dve(dve, vv)
            rw_dve(dve)
            wkv_dve(dve, vv)
            guq_dve(dve, vv)
            sgu_dve(dve, vv)
            attn_dve(dve, vv)
            branch_dve(dve, vv)
            out_dve(dve, vv)
            res_dve(dve, vv)
            ffn_dve(dve, vv)
            end_dve(dve, vv)

        @block.tensor
        def _(pe):
            entry_pe(pe)
            mem_pe(pe)
            rw_pe(pe)
            wkv_pe(pe)
            guq_pe(pe)
            sgu_pe(pe)
            attn_pe(pe)
            branch_pe(pe)
            out_pe(pe)
            res_pe(pe)
            ffn_pe(pe)
            end_pe(pe)


_INS = {'x_prompt': (TP, D), 'x_sample': (TS, D), 'mem_prompt': (MEM, D), 'state_wkv': (NB, NH, HD, HD), 'state_shift': (NB, NSH),
        'cache_mem_k': (NB, MEM, XH, W // XH), 'cache_mem_v': (NB, MEM, XH, W // XH), 'state_ffn_conv': (NB, 2, F2),
        'g_pre_mix': (D,), 'w_in': (D, NSH + 3 * W + 3 * D), 'mu_shift': (NSH,), 'w0': (W,), 'w_decay': (64, W), 'a0': (W,),
        'w_aaa': (64, W), 'w_gate': (128, W), 'k_k': (W,), 'k_a': (W,), 'r_k': (W,), 'lnx_w': (W,), 'lnx_b': (W,),
        'sgu_g': (W,), 'sgu_b': (W,), 'w_s': (8, 128, 128), 'b_s': (8, 128), 'g_mem': (D,), 'w_mem_k': (D, W),
        'w_mem_v': (D, W), 'w_branch': (3, W, D), 'w_out': (D, D), 'g_post_mix': (D,), 'g_pre_ffn': (D,), 'w_up': (D, F2),
        'conv_w': (3 * F2,), 'conv_b': (F2,), 'w_down': (DFF, D), 'g_post_ffn': (D,)}
_OUTS = [("y_p", (TP, D), (1, TP, D)), ("y_s", (TS, D), (NB, TB, D)),
         ("wkv_p", (NH, HD, HD), (1, 1, NH, HD, HD)), ("shift_p", (KSH, P), (1, 1, NSH)),
         ("mem_k", (MEM, W), (1, 1, MEM, XH, W // XH)), ("mem_v", (MEM, W), (1, 1, MEM, XH, W // XH)),
         ("conv_p", (2 * F2 // P, P), (1, 1, 2, F2)),
         ("wkv_s", (NB, NH, HD, HD), (1, NB, NH, HD, HD)), ("shift_s", (NB * KSH, P), (1, NB, NSH)),
         ("sgu_v", (TS, W), (1, NB, TB, W)), ("conv_s", (NB * 2 * F2 // P, P), (1, NB, 2, F2))]


def kernel(**inputs):
    import numpy as _np
    import concourse.bacc as _bacc
    from concourse import mybir as _mybir
    from concourse.bass_utils import run_bass_kernel_spmd as _run

    nc = _bacc.Bacc("TRN2", target_bir_lowering=False, num_devices=1)
    arrays, ins, outs = {}, {}, {}
    for name, shape in _INS.items():
        a = _np.ascontiguousarray(_np.asarray(inputs[name])).reshape(shape)
        arrays[f"in_{name}"] = a
        ins[name] = nc.dram_tensor(f"in_{name}", a.shape, _mybir.dt.from_np(a.dtype), kind="ExternalInput").ap()
    for name, shape, _ in _OUTS:
        outs[name] = nc.dram_tensor(f"out_{name}", shape, _mybir.dt.float32, kind="ExternalOutput").ap()
    hybrid_step(nc, ins, outs)
    r = _run(nc, [arrays], core_ids=[0])
    return tuple(_np.asarray(r.results[0][f"out_{name}"]).reshape(shape) for name, _, shape in _OUTS)
```

```python
from contextlib import ExitStack, contextmanager

import concourse.bass as bass
from concourse import mybir

F32 = mybir.dt.float32
F32R = mybir.dt.float32r
ALU = mybir.AluOpType
ACT = mybir.ActivationFunctionType
AX_X = mybir.AxisListType.X
ds = bass.ds

P = 128
D = 2048
KD = D // P
TP, NB, TB = 256, 8, 8
TS = NB * TB
T = TP + TS
W = D // 2
KW = W // P
HD = 64
NH = W // HD
NSH = 3 * W + 64 + 64 + 128
KSH = NSH // P
CH = 64
NCK = TP // CH
NC = NCK + 1
XT_ = T + 24
MEM = 256
XH = 4
DFF = 11 * D // 4
F2 = 2 * DFF
KF = DFF // P
NCH = KF // 4
EXT = TP + 1 + NB * (TB + 1)
CEXT = TP + 2 + NB * (TB + 2)
RMS_EPS, LN_EPS, GN_EPS = 1e-6, 1e-5, 64e-5
C_DECAY = 0.6065306597126334
NS = 2

U_MEM, U_RW, U_GUQ = 0, 16, 42
U_BR = [66, 90, 114]
U_OUT, U_FFN, U_END = 138, 154, 286
T_MEM, T_RW, T_GUQ = 0, 8, 34
T_BR = [58, 90, 122]
T_OUT, T_FFN = 154, 170
PARTS_FFN = 2 * U_FFN

PARAMS = [("g_pre_mix", D), ("mu_shift", NSH), ("w0", W), ("a0", W), ("k_k", W), ("k_a", W), ("r_k", W),
          ("lnx_w", W), ("lnx_b", W), ("sgu_g", W), ("sgu_b", W), ("g_mem", D), ("g_post_mix", D),
          ("g_pre_ffn", D), ("g_post_ffn", D), ("conv_w", 3 * F2), ("conv_b", F2)]
COL = {}
_at = 0
for _name, _n in PARAMS:
    COL[_name] = _at
    _at += _n // P
NPRM = _at


class Prog:

    def __init__(self, eng, sem, own):
        self.eng, self.sem, self.own, self.n, self.k, self.i = eng, sem, own, {}, {}, 0

    def value(self, name):
        k = self.k.get(name, 0)
        n = self.n.get(name, 0)
        return n if not k else k * self.i + n

    def do(self, ins, name=None):
        name = name or self.own
        ins.then_inc(self.sem(name), 1)
        self.n[name] = self.n.get(name, 0) + 1
        self.eng.wait_ge(self.sem(name), self.value(name))

    @contextmanager
    def loop(self, start, end, per):
        with self.eng.Fori(start, end) as i:
            first = {m: self.n.get(m, 0) for m in per}
            self.k, self.i = dict(per), i
            for m in per:
                self.n[m] = first[m] - per[m] * start
            before = dict(self.n)
            yield i
            got = {m: self.n[m] - before.get(m, 0) for m in self.n if self.n[m] != before.get(m, 0)}
            assert got == {m: v for m, v in per.items() if v}, (got, per)
        self.k = {}
        for m in per:
            self.n[m] = first[m] + per[m] * (end - start)


def hybrid_step(nc, A, O):
    ctx = ExitStack()
    with ctx:
        sems = {}

        def S(name):
            if name not in sems:
                sems[name] = ctx.enter_context(nc.semaphore(name))
            return sems[name]

        def sb(name, shape, dt=F32):
            return ctx.enter_context(nc.sbuf_tensor(name, shape, dt))

        raw = [sb(f"raw{i}", [P, 2048]) for i in range(2)]
        hi = [sb(f"hi{i}", [P, 2048], F32R) for i in range(NS)]
        lo = [sb(f"lo{i}", [P, 2048], F32R) for i in range(NS)]
        ah = sb("ah", [P, KD, T], F32R)
        al_ = sb("al", [P, KD, T], F32R)
        bh = sb("bh", [P, KW, T], F32R)
        bl = sb("bl", [P, KW, T], F32R)
        mix = sb("mix", [P, KD, T])
        rwr = sb("rw", [P, KSH * EXT])
        rw = rwr[:, :].rearrange("p (k t) -> p k t", k=KSH)
        qr = sb("q", [P, KW * XT_])
        q = qr[:, :].rearrange("p (k t) -> p k t", k=KW)
        wk = sb("work", [P, 5120])
        zz = sb("small", [P, 1664])
        prm = sb("prm", [P, NPRM])
        ident = sb("ident", [P, P])
        ones = sb("ones", [P, P])
        blk = sb("head_ones", [P, P])
        m_bd = sb("m_bd", [P, CH])
        m_ad = sb("m_ad", [P, CH])
        m_bo = sb("m_bo", [P, CH])
        m_in = sb("m_in", [P, NC, CH])
        m_st = sb("m_st", [P, NC, CH])
        m_e8 = sb("m_e8", [P, NB])
        m_sc = sb("m_scan", [P, T])
        bank = [ctx.enter_context(nc.psum_tensor(f"bank{i}", [P, 512], F32)) for i in range(8)]
        mixf = mix[:, :, :].rearrange("p k t -> p (k t)")
        rep8 = zz[0:NB, 1300:1364]
        gs = zz[:, 0:2 * T].rearrange("p (c t) -> p c t", c=2)

        def mslot(n):
            return mixf[:, T * n:T * (n + 1)]

        def wslot(n):
            return wk[:, T * n:T * (n + 1)]

        def c5(ap):
            return ap.rearrange("p (c t) -> p c t", c=NC)

        def pcol(name, j, n=1):
            c = COL[name] + j
            return prm[:, c:c + n] if isinstance(c, int) else prm[:, ds(c, n)]

        block = ctx.enter_context(nc.Block())

        def parts_of(u):
            if u < U_FFN:
                return 2 * (u + 1)
            v = u - U_FFN
            if v < 8:
                return PARTS_FFN + 2 * (v + 1)
            c, j = divmod(v - 8, 12)
            base = PARTS_FFN + 16 + 32 * c
            if c == NCH - 1:
                return base + 4 * (j + 1)
            return base + (2 * (j + 1) if j < 4 else 8 + 4 * (j - 3) if j < 8 else 24 + 2 * (j - 7))

        def lin(c, k, i):
            return c if not k else k * i + c

        def load_unit(sp, src, c, k=0, i=0):
            if c >= 2 or k:
                count = lin(c - 1, k, i)
                if k:
                    count = sp.to_reg(count)
                    sp.wait_ge(S("hi_done"), 1)
                sp.wait_ge(S("hi_done"), count)
                sp.wait_ge(S("lo_done"), count)
            sp.dma_start(raw[c % 2][:, :].rearrange("p (k n) -> p k n", n=src.shape[2]), src)\
              .then_inc(S(f"raw_loaded{c % 2}"), 16)

        def pe_left(eng, c, k, i, parts_k):
            if c >= NS or k:
                eng.wait_ge(S("parts"), lin(parts_of(c - NS), parts_k, i))

        def hi_unit(act, c, k=0, i=0, pk=None):
            if c >= U_END:
                return
            act.wait_ge(S(f"raw_loaded{c % 2}"), lin(16 * (c // 2 + 1), 8 * k, i))
            pe_left(act, c, k, i, 2 * k if pk is None else pk)
            act.activation(hi[c % NS][:, :], raw[c % 2][:, :], ACT.Copy).then_inc(S("hi_done"), 1)

        def lo_unit(dve, c, k=0, i=0, pk=None):
            if c >= U_END:
                return
            dve.wait_ge(S("hi_done"), lin(c + 1, k, i))
            pe_left(dve, c, k, i, 2 * k if pk is None else pk)
            dve.tensor_tensor(lo[c % NS][:, :], raw[c % 2][:, :], hi[c % NS][:, :], ALU.subtract)\
               .then_inc(S("lo_done"), 1)

        def bank_free(pe, t, k=0, i=0):
            if t >= 4:
                pe.wait_ge(S(f"tile_out{t % 4}"), lin(t // 4, k // 4, i))

        def three(pe, out, a_hi, a_lo, b_hi, b_lo, first, last):
            pe.matmul(out, a_hi, b_hi, start=first, stop=False)
            pe.matmul(out, a_hi, b_lo, start=False, stop=False)
            return pe.matmul(out, a_lo, b_hi, start=False, stop=last)

        def pe_group_steps(pe, u, t, xh, xl, units, uk=0, tk=0, i=0):
            for h in range(units):
                pe.wait_ge(S("lo_done"), lin(u + h + 1, uk, i))
                s = (u + h) % NS
                for c in range(2):
                    if h == 0:
                        bank_free(pe, t + c, tk, i)
                    for k in range(8):
                        o = 256 * k + 128 * c
                        last = three(pe, bank[(t + c) % 4][:, 0:T], hi[s][:, o:o + P], lo[s][:, o:o + P],
                                     xh[:, 8 * h + k, :], xl[:, 8 * h + k, :], h + k == 0, h == units - 1 and k == 7)
                        if k == 7:
                            last.then_inc(S("parts"), 1)
                        if k % 2:
                            yield

        def pe_group(*args):
            for _ in pe_group_steps(*args):
                pass

        def tile_ready(eng, u, pk=0, i=0, part=2):
            eng.wait_ge(S("parts"), lin(parts_of(u) if part == 2 else parts_of(u) - 2 + part, pk, i))

        def kv(w, k0, n0, nk=8, nn=256):
            return w.rearrange("(kt p) n -> p kt n", p=P)[:, k0:k0 + nk, ds(n0, nn) if not isinstance(n0, int) else slice(n0, n0 + nn)]


        x_tok = [wk[:, 896:896 + D], wk[:, 896 + D:896 + 2 * D], qr[0:TS, 0:D]]
        mem_tok = [rwr[:, 0:D], rwr[:, D:2 * D]]
        mkv_stage = [rwr[:, 2 * D + 512 * j:2 * D + 512 * j + 512] for j in range(4)]
        shift_t = zz[:, 0:208]
        ss, rs = zz[:, 220:225], zz[:, 225:230]
        m_u = sb("m_u", [P, P])
        m_id = sb("m_id", [P, CH])
        half_b = sb("half_bias", [P, 2 * KW + 1])

        def pool_constants(pool, pp):
            def full(ap, v):
                pp.do(pool.memset(ap, v))

            def keep(ap, op, base, pattern, cm, fill=0.0, name=None):
                pp.do(pool.affine_select(out=ap, in_=ap, compare_op=op, fill=fill, base=base, pattern=pattern,
                                         channel_multiplier=cm), name)

            full(ident[:, :], 0.0)
            keep(ident[:, :], ALU.not_equal, 0, [[-1, P]], 1, 1.0)
            full(ones[:, :], 1.0)
            full(blk[:, :], 0.0)
            for h in range(2):
                full(blk[64 * h:64 * h + 64, 64 * h:64 * h + 64], 1.0)
            full(m_e8[:, :], 1.0)
            full(m_bd[:, :], 1.0)
            full(m_ad[:, :], 1.0)
            full(m_bo[:, :], 1.0)
            full(m_st[:, :, :], 1.0)
            full(m_in[:, :, :], 1.0)
            full(m_sc[:, :], 1.0)
            full(m_u[:, :], 1.0)
            for h in range(2):
                r = slice(64 * h, 64 * h + 64)
                keep(m_e8[r, :], ALU.is_ge, 0, [[-8, 8]], 1)
                keep(m_e8[r, :], ALU.is_ge, 7, [[8, 8]], -1)
                for m, op, c in ((m_bd, ALU.is_gt, -1), (m_ad, ALU.is_gt, 1)):
                    keep(m[r, :], op, 0, [[-c, 64]], c)
                    mv = m[r, :].rearrange("p (b t) -> p b t", b=8)
                    keep(mv, ALU.is_ge, 0, [[-8, 8], [0, 8]], 1)
                    keep(mv, ALU.is_ge, 7, [[8, 8], [0, 8]], -1)
                keep(m_bo[r, :].rearrange("p (b t) -> p b t", b=8), ALU.is_gt, 0, [[8, 8], [0, 8]], -1)
                keep(m_st[r, 0:NCK, :], ALU.is_gt, 0, [[0, NCK], [1, 64]], -1)
                keep(m_in[r, :, :], ALU.is_ge, 0, [[0, NC], [1, 64]], -1)
                mv = m_in[r, NCK, :].rearrange("p (b t) -> p b t", b=8)
                keep(mv, ALU.is_ge, 0, [[-8, 8], [0, 8]], 1)
                keep(m_st[r, NCK, :], ALU.is_gt, 0, [[1, 64]], -1)
                mv = m_st[r, NCK, :].rearrange("p (b t) -> p b t", b=8)
                keep(mv, ALU.is_ge, 7, [[8, 8], [0, 8]], -1)
                keep(mv, ALU.is_ge, 0, [[-8, 8], [0, 8]], 1)
            keep(m_u[:, :], ALU.is_ge, 0, [[1, P]], -1)
            full(m_sc[:, 0:TP].rearrange("p (c t) -> p c t", c=NCK)[:, :, 0:1], 0.0)
            full(m_sc[:, TP:T].rearrange("p (c t) -> p c t", c=NB)[:, :, 0:1], 0.0)
            full(rep8, 0.0)
            keep(rep8.rearrange("p (b t) -> p b t", b=8), ALU.not_equal, 0, [[0, 8], [-1, 8]], 1, 1.0, "consts")

        def pool_loads(pool):
            for k in range(2):
                pool.dma_start(mem_tok[k], A["mem_prompt"][128 * k:128 * k + 128, :]).then_inc(S("mem_in"), 16)
            row = 0
            for name, n in PARAMS:
                src = A[name].rearrange("(r p) -> r p", p=P)
                k, at = n // P, 0
                while at < k:
                    m = min(k - at, P - row % P)
                    c = 128 * (row // P)
                    pool.dma_start(wk[row % P:row % P + m, c:c + 128], src[at:at + m, :]).then_inc(S("par_in"), 16)
                    par_dmas[0] += 1
                    at += m
                    row += m
            shift = A["state_shift"].rearrange("b (j p) -> (b j) p", p=P)
            pool.dma_start(wk[:, 640:768], shift[0:P, :]).then_inc(S("par_in"), 16)
            pool.dma_start(wk[0:80, 768:896], shift[P:208, :]).then_inc(S("par_in"), 16)
            par_dmas[0] += 2
            for k in range(2):
                pool.dma_start(x_tok[k], A["x_prompt"][128 * k:128 * k + 128, :]).then_inc(S("x_in"), 16)
            pool.dma_start(x_tok[2], A["x_sample"]).then_inc(S("x_in"), 16)

        par_dmas = [0]
        n_par, row = 2, 0
        for name, n in PARAMS:
            at, k = 0, n // P
            while at < k:
                m = min(k - at, P - row % P)
                n_par, at, row = n_par + 1, at + m, row + m

        def entry_act(act, aa):
            for j, (tok, sem, m) in enumerate([(mem_tok[0], "mem_in", P), (mem_tok[1], "mem_in", P), (x_tok[0], "x_in", P),
                                               (x_tok[1], "x_in", P), (x_tok[2], "x_in", TS)]):
                act.wait_ge(S(sem), 32 if sem == "mem_in" else 48)
                if j == 0:
                    act.wait_ge(S("rs_zero"), 1)
                aa.do(act.activation(mixf[0:m, 0:D], tok, ACT.Square, accum_out=ss[0:m, j:j + 1]),
                      "sum_mem" if j == 1 else "sum_x" if j == 4 else None)
            act.wait_ge(S("ms_ready"), 1)
            aa.do(act.activation(rs, ss, ACT.Sqrt), "rms_ready")
            act.wait_ge(S("entry_ps"), 2)
            aa.do(act.activation(prm[:, 0:512], bank[4][:, :], ACT.Copy))
            aa.do(act.activation(prm[:, 512:NPRM], bank[5][:, 0:NPRM - 512], ACT.Copy))
            aa.do(act.activation(shift_t, bank[5][:, 128:336], ACT.Copy), "prm_ready")
            for k in range(8):
                act.wait_ge(S("mem_g"), k + 1)
                aa.do(act.activation(ah[:, 2 * k:2 * k + 2, 0:MEM], memg(k), ACT.Copy), "mem_hi")

        def memg(k):
            return mixf[:, 512 * (k % 2):512 * (k % 2) + 512].rearrange("p (a t) -> p a t", a=2)

        def entry_dve(dve, vv):
            vv.do(dve.memset(ss, 1.0), "rs_zero")
            dve.wait_ge(S("sum_mem"), 1)
            dve.wait_ge(S("sum_x"), 1)
            vv.do(dve.tensor_scalar(ss, ss, 1.0 / D, RMS_EPS, ALU.mult, ALU.add), "ms_ready")
            dve.wait_ge(S("rms_ready"), 1)
            vv.do(dve.reciprocal(rs, rs))
            for j, tok in enumerate(mem_tok + x_tok):
                m = TS if j == 4 else P
                vv.do(dve.tensor_scalar(tok, tok, rs[0:m, j:j + 1], None, ALU.mult), "tok_normed")
            dve.wait_ge(S("prm_ready"), 1)
            vv.do(dve.tensor_scalar(half_b[:, :], prm[:, COL["w0"]:COL["w0"] + 2 * KW + 1], 0.5, None, ALU.mult))
            dve.wait_ge(S("consts"), 1)
            vv.do(dve.tensor_tensor(m_id[:, :], ident[:, 0:64], ident[:, 64:128], ALU.add))
            for k in range(8):
                dve.wait_ge(S("entry_ps"), 3 + k)
                g = bc(pcol("g_mem", 2 * k, 2), MEM)
                vv.do(dve.tensor_tensor(memg(k), bank[4 + k % 4][:, :].rearrange("p (a t) -> p a t", a=2), g, ALU.mult), "mem_g")
                dve.wait_ge(S("mem_hi"), k + 1)
                vv.do(dve.tensor_tensor(al_[:, 2 * k:2 * k + 2, 0:MEM], memg(k), ah[:, 2 * k:2 * k + 2, 0:MEM], ALU.subtract),
                      "mem_lo")
            for k in range(KD):
                dve.wait_ge(S("entry_ps"), 11 + k)
                vv.do(dve.tensor_scalar(mix[:, k, :], bank[4 + k % 4][:, 0:T], pcol("g_pre_mix", k), None, ALU.mult), "x_g")

        def bc(ap, n):
            return ap.rearrange("p (a o) -> p a o", o=1).broadcast_to([ap.shape[0], ap.shape[1], n])

        def entry_pe(pe):
            pe.wait_ge(S("consts"), 1)
            pe.wait_ge(S("par_in"), 16 * n_par)
            for j in range(4):
                last = pe.transpose(bank[4][:, 128 * j:128 * j + 128], wk[:, 128 * j:128 * j + 128], ident[:, :])
            last.then_inc(S("entry_ps"), 1)
            m = NPRM - 512
            pe.transpose(bank[5][:, 0:m], wk[0:m, 512:640], ident[0:m, 0:m])
            pe.transpose(bank[5][:, 128:256], wk[:, 640:768], ident[:, :])
            pe.transpose(bank[5][:, 256:336], wk[0:80, 768:896], ident[0:80, 0:80]).then_inc(S("entry_ps"), 1)
            pe.wait_ge(S("tok_normed"), 2)
            for k in range(8):
                if k < 4:
                    pe.wait_ge(S("prm_ready"), 1)
                else:
                    pe.wait_ge(S("mem_g"), k - 3)
                for a in range(2):
                    for t in range(2):
                        last = pe.transpose(bank[4 + k % 4][:, 256 * a + 128 * t:256 * a + 128 * t + 128],
                                            mem_tok[t][:, 128 * (2 * k + a):128 * (2 * k + a) + 128], ident[:, :])
                last.then_inc(S("entry_ps"), 1)
            pe.wait_ge(S("tok_normed"), 5)
            for k in range(KD):
                if k < 4:
                    pe.wait_ge(S("mem_g"), k + 5)
                else:
                    pe.wait_ge(S("x_g"), k - 3)
                if k == 0:
                    pe.wait_ge(S("mem_lo"), 8)
                x_transposes(pe, x_tok, k, bank[4 + k % 4]).then_inc(S("entry_ps"), 1)

        def x_transposes(pe, toks, k, out):
            for t in range(3):
                m = TS if t == 2 else P
                last = pe.transpose(out[:, 128 * t:128 * t + m], toks[t][:, 128 * k:128 * k + 128], ident[0:m, 0:m])
            return last

        def mem_pe(pe):
            pe.wait_ge(S("mem_lo"), 8)
            for u in range(16):
                g, s = u // 4, u % NS
                pe.wait_ge(S("lo_done"), u + 1)
                for tt in range(2):
                    t = 2 * g + tt
                    if u % 4 == 0:
                        bank_free(pe, t)
                    for k in range(4):
                        kk, r = 4 * (u % 4) + k, slice(128 * tt, 128 * tt + 128)
                        a_h, a_l = ah[:, kk, r], al_[:, kk, r]
                        w_h, w_l = hi[s][:, 512 * k:512 * k + 512], lo[s][:, 512 * k:512 * k + 512]
                        last = three(pe, bank[t % 4][:, :], a_h, a_l, w_h, w_l, kk == 0, kk == KD - 1)
                    last.then_inc(S("parts"), 1)

        def mem_act(act):
            for u in range(16):
                hi_unit(act, u + 2)
                if u % 4 == 3:
                    for t in range(2 * (u // 4), 2 * (u // 4) + 2):
                        tile_ready(act, u, part=t % 2 + 1)
                        if t == 0:
                            act.wait_ge(S("mem_lo"), 8)
                        if t >= 4:
                            act.wait_ge(S(f"mem_stored{t % 4}"), 16)
                        act.activation(mkv_stage[t % 4], bank[t % 4][:, :], ACT.Copy).then_inc(S(f"tile_out{t % 4}"), 1)

        def mem_dve(dve):
            for u in range(16):
                lo_unit(dve, u + 2)

        def mem_pool(pool):
            for t in range(8):
                pool.wait_ge(S(f"tile_out{t % 4}"), t // 4 + 1)
                g, tt = t // 2, t % 2
                dst = O["mem_k"] if g < 2 else O["mem_v"]
                pool.dma_start(dst[128 * tt:128 * tt + 128, 512 * (g % 2):512 * (g % 2) + 512], mkv_stage[t % 4])\
                    .then_inc(S(f"mem_stored{t % 4}"), 16)

        def split_x_act(act, aa):
            act.wait_ge(S("x_g"), KD)
            tile_ready(act, 15)
            for c in range(4):
                aa.do(act.activation(ah[:, 4 * c:4 * c + 4, :], mix[:, 4 * c:4 * c + 4, :], ACT.Copy), "xn_hi")
            for t in range(4):
                act.wait_ge(S(f"mem_stored{t}"), 32)

        def split_x_dve(dve, vv):
            tile_ready(dve, 15)
            for c in range(4):
                dve.wait_ge(S("xn_hi"), c + 1)
                vv.do(dve.tensor_tensor(al_[:, 4 * c:4 * c + 4, :], mix[:, 4 * c:4 * c + 4, :], ah[:, 4 * c:4 * c + 4, :],
                                        ALU.subtract), "xn_lo")
            for t in range(4):
                dve.wait_ge(S(f"mem_stored{t}"), 32)
            vv.do(dve.memset(rw[:, :, 0:1], 0.0))
            vv.do(dve.tensor_copy(smp(rw, KSH)[:, :, :, 0], shift_t.rearrange("p (b k) -> p k b", b=NB)), "shift_set")

        def smp(t, k):
            return t[:, :, TP + 1:EXT].rearrange("p k (b t) -> p k b t", b=NB)

        def rw_pe(pe):
            pe.wait_ge(S("xn_lo"), 4)
            pe_group(pe, U_RW, T_RW, ah, al_, 2)
            with pe.Fori(0, 6) as i:
                for g in range(2):
                    pe_group(pe, U_RW + 2 + 2 * g, T_RW + 2 + 2 * g, ah, al_, 2, 4, 4, i)

        def rw_out(act, k, t, tk=0, i=0):
            kk = ds(k, 1) if tk else slice(k, k + 1)
            b = t % 4
            act.activation(rw[:, kk, 1:1 + TP].rearrange("p k t -> p (k t)"), bank[b][:, 0:TP], ACT.Copy)
            act.activation(rw[:, kk, TP + 1:EXT].rearrange("p k (b t) -> p (k b) t", b=NB)[:, :, 1:1 + TB],
                           bank[b][:, TP:T].rearrange("p (b t) -> p b t", b=NB), ACT.Copy).then_inc(S(f"tile_out{b}"), 1)

        def rw_act(act):
            def group(u, t, k, uk=0, i=0):
                for h in range(2):
                    hi_unit(act, u + 2 + h, uk, i)
                for c in range(2):
                    tile_ready(act, u + 1, 2 * uk, i, c + 1)
                    rw_out(act, k + c, t + c, uk, i)
            act.wait_ge(S("shift_set"), 1)
            group(U_RW, T_RW, 0)
            with act.Fori(0, 6) as i:
                for g in range(2):
                    group(U_RW + 2 + 2 * g, T_RW + 2 + 2 * g, 4 * i + 2 + 2 * g, 4, i)

        def rw_dve(dve):
            for h in range(2):
                lo_unit(dve, U_RW + 2 + h)
            with dve.Fori(0, 6) as i:
                for h in range(4):
                    lo_unit(dve, U_RW + 4 + h, 4, i)

        wa_in, sg = qr[:, 0:T], qr[:, T:2 * T]
        s0t = qr[:, 640:1152].rearrange("p (b v) -> p b v", b=NB)
        alm = qr[:, 1152:1664].rearrange("p (b t) -> p b t", b=NB)
        st_pp = [qr[:, 1664:1728], qr[:, 1728:1792]]
        xs_, sa_ = qr[:, 1792:1856], qr[:, 1856:1920]
        be_t, ka_t, v_, alp, be, ka, rh, t_r, t_ad, t_bd, t_bo, t_rt, t_bk, t_cb, t_ck, bon = [wslot(n) for n in range(16)]
        v_t, t_a2, t_b2 = v_, be, ka
        sam = wk[:, 8 * T:8 * T + 512].rearrange("p (b v) -> p b v", b=NB)
        vtm = wk[:, 8 * T + 512:8 * T + 1024].rearrange("p (b v) -> p b v", b=NB)
        y_, ym, ysq = t_r, t_cb, t_ck
        cum, ldx, pt, tmp = be, ka, t_bk, t_bd
        rk = t_bo
        kkv, av = rw[:, 24, 0:T], rw[:, 25, 0:T]
        sq = qr[:, 2316:2636]
        wlr = qr[:, 1920:2176]
        pend_p, pend_s = qr[:, 2176:2180], qr[:, 2180:2188]
        sp_out = qr[0:64, 2188:2316]
        s_out = zz[0:64, 640:1664]
        s0raw = zz[64:128, 640:1664]
        last_t = qr[:, 0:234]
        sh_stage = qr[:, 256:512]

        RING = (4, 5, 7)
        PR = {}
        for _n in ["s0t", "bonus", "A", "B", "Bk", "Cb", "Ck", "beT", "kaT", "vT", "A2", "B2",
                   "R1", "RT1", "A4", "B4", "R2", "RT2", "Q", "QT", "Q2", "QT2", "QT4", "W1", "W2", "W3", "z", "za",
                   "X0", "SA0", "S0", "ssq"] + \
                [f"{m}{c}" for c in range(1, NCK) for m in ("X", "SA", "S")] + \
                ["X4", "SA4", "S4", "tr0", "tr1", "trp", "mean", "var", "g"]:
            PR[_n] = len(PR)
        NPR = len(PR)
        OUT = {}
        for _n in PR:
            if _n not in ("z", "za", "g"):
                OUT[_n] = len(OUT)
        N_OUT = len(OUT)
        PS0, OUT0 = 3, 2

        def pbank(name):
            return bank[6] if name == "g" else bank[RING[PR[name] % 3]]

        def shift_pool(pool):
            pool.wait_ge(S("shift_stage"), 2)
            pool.dma_start(O["shift_p"], sh_stage[0:KSH, 0:128]).then_inc(S("state_stored"), 16)
            pool.dma_start(O["shift_s"][0:102, :], sh_stage[KSH:128, 0:128]).then_inc(S("state_stored"), 16)
            pool.dma_start(O["shift_s"][102:208, :], sh_stage[0:106, 128:256]).then_inc(S("state_stored"), 16)

        shift_d = zz[:, 640:640 + EXT - 1]

        def wkv_pool(pool):
            def load(j):
                n = slice(128 * j, 128 * j + 128)
                pool.dma_start(wlr[0:64, 0:128], A["w_decay"][:, n]).then_inc(S("pair_in"), 16)
                pool.dma_start(wlr[64:128, 0:128], A["w_aaa"][:, n]).then_inc(S("pair_in"), 16)
                for h in range(2):
                    dst = s0raw.rearrange("v (b h k) -> v b h k", b=NB, h=2)[:, :, h, :]
                    pool.dma_start(dst, A["state_wkv"][:, 2 * j + h].rearrange("b v k -> v b k")).then_inc(S("pair_in"), 16)

            def load_gate(j):
                pool.dma_start(wlr[:, 128:256], A["w_gate"][:, 128 * j:128 * j + 128]).then_inc(S("gate_in"), 16)

            pool.wait_ge(S("at_v"), 3 * NB + 16)
            pool.wait_ge(S("bl_ready"), 2)
            load(0)
            load_gate(0)
            for j in range(KW):
                pool.wait_ge(S("wkv_ps"), PS0 + NPR * j + PR["s0t"] + 1)
                load(min(j + 1, KW - 1))
                pool.wait_ge(S("ring_out"), OUT0 + N_OUT * j + OUT["trp"] + 1)
                for h in range(2):
                    src = s_out.rearrange("v (b h k) -> v b h k", b=NB, h=2)[:, :, h, :]
                    pool.dma_start(O["wkv_s"][:, 2 * j + h].rearrange("b v k -> v b k"), src).then_inc(S("state_stored"), 16)
                pool.dma_start(O["wkv_p"][2 * j:2 * j + 2].rearrange("h v k -> v h k"),
                               sp_out.rearrange("v (h k) -> v h k", h=2)).then_inc(S("state_stored"), 16)
                if j + 1 < KW:
                    pool.wait_ge(S("wkv_ps"), PS0 + NPR * (j + 1))
                    load_gate(j + 1)
                if j == 3:
                    pool.wait_ge(S("parts"), parts_of(U_BR[1] - 1))
                    for n, dst in enumerate((bh, bl)):
                        pool.dma_start(dst[:, :, :].rearrange("p k t -> p (k t)"), A["sgu_parts"][n]).then_inc(S("sgu_back"), 16)

        def row_(tile):
            return rw[:, slice(tile, tile + 1) if isinstance(tile, int) else ds(tile, 1), 0:T].rearrange("p k t -> p (k t)")

        def mix_shift(dve, vv, dst, tile, mu):
            d = shift_d
            tt = slice(tile, tile + 1) if isinstance(tile, int) else ds(tile, 1)
            row = rw[:, tt, :].rearrange("p k t -> p (k t)")
            vv.do(dve.tensor_tensor(d, row[:, 0:EXT - 1], row[:, 1:EXT], ALU.subtract))
            vv.do(dve.scalar_tensor_tensor(out=dst[:, 0:TP], in0=d[:, 0:TP], scalar=mu, in1=row[:, 1:1 + TP],
                                           op0=ALU.mult, op1=ALU.add))
            ds8 = zz[:, 640 + TP + 1:640 + EXT].rearrange("p (b t) -> p b t", b=NB)[:, :, 0:TB]
            vv.do(dve.scalar_tensor_tensor(out=dst[:, TP:T].rearrange("p (b t) -> p b t", b=NB), in0=ds8, scalar=mu,
                                           in1=row[:, TP + 1:EXT].rearrange("p (b t) -> p b t", b=NB)[:, :, 1:],
                                           op0=ALU.mult, op1=ALU.add))

        def shift_dve(dve, vv):
            for t in range(4):
                dve.wait_ge(S(f"tile_out{t}"), 8 if t >= 2 else 9)
            vv.do(dve.tensor_copy(last_t[:, 0:KSH], rw[:, :, TP]))
            vv.do(dve.tensor_copy(last_t[:, KSH:].rearrange("p (b k) -> p k b", b=NB), smp(rw, KSH)[:, :, :, TB]), "last_rows")

        def prepare_kk(dve, vv, j):
            vv.do(dve.tensor_scalar(kkv, row_(j + 8), pcol("k_k", j), None, ALU.mult))
            vv.do(dve.tensor_tensor(sq, kkv, kkv, ALU.mult), "kk_sq")

        def prepare_logs(dve, vv, j):
            dve.wait_ge(S("low_out"), 2 * j + 2)
            vv.do(dve.tensor_scalar(ldx, ldx, -0.5 * C_DECAY, -0.5 * C_DECAY, ALU.mult, ALU.add))
            vv.do(dve.tensor_tensor_scan(cum, m_sc[:, :], ldx, 0.0, ALU.mult, ALU.add))
            vv.do(dve.tensor_tensor(ldx, cum, ldx, ALU.subtract), "logs")
            vv.do(dve.tensor_scalar(av, av, 0.5, 0.5, ALU.mult, ALU.add))

        def prepare_k(dve, vv, j):
            vv.do(dve.tensor_scalar(tmp, av, -1.0, pcol("k_a", j), ALU.add, ALU.mult))
            vv.do(dve.scalar_tensor_tensor(out=row_(j + 8), in0=tmp, scalar=1.0, in1=row_(j + 8), op0=ALU.add, op1=ALU.mult))

        def prepare_norm(dve, vv, j):
            dve.wait_ge(S("kk_root"), j + 1)
            vv.do(dve.reciprocal(sq, sq))
            vv.do(dve.tensor_tensor(kkv, kkv, sq, ALU.mult))
            vv.do(dve.tensor_tensor(av, kkv, av, ALU.mult))

        def prepare_al(dve, vv, j):
            dve.wait_ge(S("exps"), 3 * (j + 1))
            vv.do(dve.scalar_tensor_tensor(out=alp, in0=kkv, scalar=-1.0, in1=ldx, op0=ALU.mult, op1=ALU.mult))
            vv.do(dve.tensor_copy(alm_own, alp[:, TP:T].rearrange("p (b t) -> p b t", b=NB)))

        def prepare_ops(dve, vv, j):
            vv.do(dve.tensor_tensor(ka, row_(j + 8), cum, ALU.mult))
            vv.do(dve.tensor_tensor(be, av, cum, ALU.mult))
            vv.do(dve.tensor_tensor(rh, row_(j), pt, ALU.mult), "ops_ready")

        def prepare_rest(dve, vv, j):
            vv.do(dve.scalar_tensor_tensor(out=rk, in0=row_(j), scalar=pcol("r_k", j), in1=row_(j + 8), op0=ALU.mult,
                                           op1=ALU.mult), "rk_ready")
            vv.do(dve.tensor_copy(pend_p, pt[:, 0:TP].rearrange("p (c t) -> p c t", c=NCK)[:, :, CH - 1]))
            vv.do(dve.tensor_copy(pend_s, pt[:, TP:T].rearrange("p (b t) -> p b t", b=NB)[:, :, TB - 1]))

        alm_own = qr[:, 1152:1152 + 72 * NB].rearrange("p (b t) -> p b t", b=NB)[:, :, 0:TB]

        def wkv_start_dve(dve, vv):
            vv.do(dve.memset(alm, 0.0), "low_in")
            vv.do(dve.memset(xs_, 0.0), "ring_out")
            vv.do(dve.memset(sa_, 0.0), "gated_out")
            dve.wait_ge(S("sig_g"), 3)
            vv.do(dve.tensor_scalar(sg, sg, 0.5, 0.5, ALU.mult, ALU.add), "low_ready")
            prepare_kk(dve, vv, 0)
            dve.wait_ge(S("wkv_ps"), 3)
            vv.do(dve.tensor_scalar(sq, pbank("ssq")[:, 0:T], 1e-24, None, ALU.max), "ring_out")
            prepare_logs(dve, vv, 0)
            prepare_k(dve, vv, 0)
            prepare_norm(dve, vv, 0)
            prepare_al(dve, vv, 0)
            prepare_ops(dve, vv, 0)
            prepare_rest(dve, vv, 0)
            for c in range(2):
                vv.do(dve.memset(gs[:, c, :], 0.0), "gate_free")

        STEPS = dict(enumerate([1, 2, 1, 4, 1, 0, 0, 1, 0, 0, 1, 1, 4, 0, 1, 2, 0, 1, 1, 0, 1, 2, 3, 2, 0, 0, 0, 0, 0, 0, 0, 1, 0, 0, 1, 1, 1, 1, 1, 1, 2, 0, 0, 2, 2, 0, 2, 2, 2, 0]))
        assert sum(STEPS.values()) == 48, sum(STEPS.values())
        UNIT_END = [next(p for p in range(NPR) if sum(STEPS.get(x, 0) for x in range(p + 1)) >= 8 * (j + 1)) for j in range(6)]

        def wkv_dve(dve, vv, n):
            u = U_BR[n]
            with vv.loop(4 * n, 4 * n + 4, PER_V) as i:
                units = [0]

                def stream(p):
                    while units[0] < 6 and UNIT_END[units[0]] < p:
                        j = units[0]
                        lo_unit(dve, u - 24 * n + j + 2, 6, i)
                        if j % 3 == 2:
                            for c in range(2):
                                add_branch(dve, vv, n, j // 3, c, i)
                        units[0] += 1

                def ps(name, units_first=True):
                    if units_first:
                        stream(PR[name])
                    dve.wait_ge(S("wkv_ps"), PS0 + NPR * i + PR[name] + 1)

                def tt(o, a, b, op, sem=None):
                    vv.do(dve.tensor_tensor(o, a, b, op), sem)

                def masked(o, name, m, sem="ring_out"):
                    ps(name)
                    m = m[:, :, :] if len(m.shape) == 3 else bmid(m[:, :], NC)
                    tt(c5(o), c5(pbank(name)[:, 0:T]), m, ALU.mult, sem)

                def plain(o, name, n=T):
                    ps(name)
                    vv.do(dve.tensor_copy(o[:, 0:n], pbank(name)[:, 0:n]), "ring_out")

                def plus(o, name, n=T):
                    ps(name)
                    tt(o[:, 0:n], o[:, 0:n], pbank(name)[:, 0:n], ALU.add, "ring_out")

                ps("s0t")
                vv.do(dve.tensor_copy(qr[:, 640:1152], pbank("s0t")[:, :]), "ring_out")
                ps("bonus")
                tt(bon, pbank("bonus")[:, 0:T], row_(i + 16), ALU.mult, "ring_out")
                masked(t_ad, "A", m_ad)
                masked(t_bd, "B", m_bd, None)
                tt(c5(t_bo)[:, 0:NCK], c5(pbank("B")[:, 0:T])[:, 0:NCK], bmid(m_bo[:, :], NCK), ALU.mult, "ring_out")
                masked(t_bk, "Bk", m_st)
                masked(t_cb, "Cb", m_in)
                masked(t_ck, "Ck", m_in)
                plain(be_t, "beT")
                plain(ka_t, "kaT")
                plain(v_t, "vT")
                tt(c5(t_r), c5(t_bd), bmid(m_id[:, :], NC), ALU.add)
                tt(c5(t_rt), c5(t_ad), bmid(m_id[:, :], NC), ALU.add, "r_ready")
                plain(t_a2, "A2")
                plain(t_b2, "B2")
                plus(t_r, "R1")
                plus(t_rt, "RT1")
                plain(t_ad, "A4")
                plain(t_bd, "B4")
                plus(t_r, "R2")
                plus(t_rt, "RT2")
                plain(t_a2, "Q", TP)
                plain(t_b2, "QT", TP)
                plain(t_ad, "Q2", TP)
                plain(t_bd, "QT2", TP)
                plain(t_rt, "QT4", TP)
                plus(t_r, "W1", TP)
                prepare_kk(dve, vv, i + 1)
                plus(t_r, "W2", TP)
                plus(t_r, "W3", TP)
                for c in range(NCK):
                    plain(xs_, f"X{c}", 64)
                    plain(sa_, f"SA{c}", 64)
                    ps(f"S{c}")
                    pend = pend_p[:, c:c + 1]
                    src = pbank(f"S{c}")[:, 0:64]
                    if c:
                        tt(st_pp[c % 2], src, st_pp[(c + 1) % 2], ALU.add)
                        src = st_pp[c % 2]
                    vv.do(dve.tensor_scalar(st_pp[c % 2], src, pend, None, ALU.mult), "ring_out")
                    if c == 0:
                        ps("ssq")
                        vv.do(dve.tensor_scalar(sq, pbank("ssq")[:, 0:T], 1e-24, None, ALU.max), "ring_out")
                    elif c == 1:
                        prepare_logs(dve, vv, i + 1)
                    elif c == 2:
                        prepare_k(dve, vv, i + 1)
                plain(xs_, "X4", 64)
                ps("SA4")
                vv.do(dve.tensor_copy(sa_, pbank("SA4")[:, 0:64]), "ring_out")
                tt(sam, bmid(sa_, NB), bc(m_e8[:, :], HD), ALU.mult)
                tt(vtm, bmid(v_t[:, TP:T], NB), bc(m_e8[:, :], HD), ALU.mult, "sam_ready")
                prepare_norm(dve, vv, i + 1)
                ps("S4")
                tt(sam, pbank("S4")[:, :].rearrange("p (b v) -> p b v", b=NB), s0t, ALU.add)
                tt(sam, sam, bc(pend_s, HD), ALU.mult, "ring_out")
                dve.wait_ge(S("y_ps"), i + 1)
                vv.do(dve.tensor_copy(y_, bank[6][:, 0:T]), "y_out")
                prepare_al(dve, vv, i + 1)
                dve.wait_ge(S("state_stored"), 48 * (i + 1))
                for m in range(2):
                    ps(f"tr{m}", False)
                    vv.do(dve.tensor_copy(s_out[:, 512 * m:512 * m + 512], pbank(f"tr{m}")[0:64, :]), "ring_out")
                ps("trp", False)
                vv.do(dve.tensor_copy(sp_out, pbank("trp")[0:64, 0:128]), "ring_out")
                ps("mean", False)
                vv.do(dve.scalar_tensor_tensor(out=ym, in0=pbank("mean")[:, 0:T], scalar=-1.0 / HD, in1=y_,
                                               op0=ALU.mult, op1=ALU.add), "ring_out")
                tt(ysq, ym, ym, ALU.mult, "ym_sq")
                prepare_ops(dve, vv, i + 1)
                ps("var", False)
                vv.do(dve.tensor_scalar(ysq, pbank("var")[:, 0:T], 1.0 / HD, GN_EPS, ALU.mult, ALU.add), "ring_out")
                prepare_rest(dve, vv, i + 1)
                stream(PR["g"])
                dve.wait_ge(S("gn_sqrt"), i + 1)
                vv.do(dve.reciprocal(ysq, ysq))
                tt(ym, ym, ysq, ALU.mult)
                vv.do(dve.tensor_scalar(ym, ym, pcol("lnx_w", i), pcol("lnx_b", i), ALU.mult, ALU.add))
                tt(ym, ym, bon, ALU.add)
                ps("g")
                tt(row_(i), ym, bank[6][:, 0:T], ALU.mult, "gated_out")
                stream(NPR)

        def bmid(ap, n):
            return ap.rearrange("p (o t) -> p o t", o=1).broadcast_to([ap.shape[0], n, ap.shape[1]])

        PER_V = {"dve": 26, "kk_sq": 1, "logs": 1, "ring_out": N_OUT, "rk_ready": 1, "ops_ready": 1, "r_ready": 1,
                 "sam_ready": 1, "y_out": 1, "ym_sq": 1, "gated_out": 1, "gate_free": 4}

        def shift_act(act, aa):
            for n in range(2):
                act.wait_ge(S("last_ps"), n + 1)
                m = 128 if n == 0 else 106
                aa.do(act.activation(sh_stage[0:m, 128 * n:128 * n + 128], bank[4 + n][0:m, 0:128], ACT.Copy), "shift_stage")

        def wkv_start_act(act, aa):
            act.wait_ge(S("low_in"), 1)
            aa.do(act.activation(wa_in[0:64, :], rw[0:64, 24, 0:T], ACT.Tanh), "sig_g")
            aa.do(act.activation(wa_in[64:128, :], rw[64:128, 24, 0:T], ACT.Copy), "sig_g")
            aa.do(act.activation(sg, rw[:, 25, 0:T], ACT.Tanh, scale=0.5), "sig_g")

        def prepare_act(act, aa, j, ps=None):
            if ps:
                ps("z")
            else:
                act.wait_ge(S("wkv_ps"), 1)
            aa.do(act.activation(ldx, pbank("z")[:, 0:T], ACT.Tanh, scale=0.5,
                                 bias=half_b[:, ds(j, 1) if ps else slice(0, 1)]), "low_out")
            if ps:
                ps("za")
            else:
                act.wait_ge(S("wkv_ps"), 2)
            aa.do(act.activation(av, pbank("za")[:, 0:T], ACT.Tanh, scale=0.5,
                                 bias=half_b[:, ds(j + 8, 1) if ps else slice(8, 9)]), "low_out")
            if ps:
                ps("X4")
            act.wait_ge(S("logs"), j + 1)
            aa.do(act.activation(pt, cum, ACT.Exp), "exps")
            aa.do(act.activation(cum, cum, ACT.Exp, scale=-1.0), "exps")
            aa.do(act.activation(ldx, ldx, ACT.Exp), "exps")
            if ps:
                act.wait_ge(S("ring_out"), OUT0 + N_OUT * (j - 1) + OUT["ssq"] + 1)
            else:
                act.wait_ge(S("ring_out"), 2)
            aa.do(act.activation(sq, sq, ACT.Sqrt), "kk_root")
            if ps:
                ps("mean")
            act.wait_ge(S("ops_ready"), j + 1)
            aa.do(act.activation(v_, row_(j + 16), ACT.Copy), "v_copied")

        def wkv_act(act, aa, n):
            with aa.loop(4 * n, 4 * n + 4, {"low_out": 2, "exps": 3, "kk_root": 1, "v_copied": 1, "gn_sqrt": 1}) as i:
                units = [0]

                def stream(p):
                    while units[0] < 6 and UNIT_END[units[0]] < p:
                        branch_act_unit(act, units[0], i)
                        units[0] += 1

                def ps(name):
                    stream(PR[name])
                    act.wait_ge(S("wkv_ps"), PS0 + NPR * i + PR[name] + 1)

                prepare_act(act, aa, i + 1, ps)
                ps("var")
                act.wait_ge(S("ring_out"), OUT0 + N_OUT * (i + 1))
                aa.do(act.activation(ysq, ysq, ACT.Sqrt), "gn_sqrt")
                stream(NPR)

        def shift_pe(pe):
            pe.wait_ge(S("last_rows"), 1)
            pe.transpose(bank[4][:, 0:128], last_t[:, 0:128], ident[:, :]).then_inc(S("last_ps"), 1)
            pe.transpose(bank[5][0:106, 0:128], last_t[:, 128:234], ident[:, :]).then_inc(S("last_ps"), 1)
            pe.wait_ge(S("shift_stage"), 2)

        def wkv_start_pe(pe):
            pe.wait_ge(S("low_ready"), 1)
            pe.wait_ge(S("pair_in"), 64)
            for h, name in enumerate(("z", "za")):
                r = slice(64 * h, 64 * h + 64)
                pe.matmul(pbank(name)[:, 0:T], wlr[r, 0:128], wa_in[r, :], start=True, stop=True).then_inc(S("wkv_ps"), 1)
            pe.wait_ge(S("kk_sq"), 1)
            pe.matmul(pbank("ssq")[:, 0:T], blk[:, :], sq, start=True, stop=True).then_inc(S("wkv_ps"), 1)
            pe.wait_ge(S("low_out"), 2)

        def wkv_pe(pe, n):
            u, t = U_BR[n], T_BR[n]
            with pe.Fori(4 * n, 4 * n + 4) as i:
                done = [0]

                def stream():
                    for g in range(2):
                        cu, ct = u - 24 * n + 3 * g, t - 32 * n + 4 * g
                        yield from pe_group_steps(pe, cu, ct, ah, al_, 2, 6, 8, i)
                        if n == 0:
                            pe.wait_ge(S("bl_ready"), 2)
                        else:
                            pe.wait_ge(S("sgu_back"), 32)
                        yield from pe_group_steps(pe, cu + 2, ct + 2, bh, bl, 1, 6, 8, i)

                steps = stream()

                def wait(name, value):
                    value = pe.to_reg(value)
                    pe.wait_ge(S("low_ready"), 1)
                    pe.wait_ge(S(name), value)

                def begin(name, *needs):
                    p = PR[name]
                    assert p == done[0], name
                    for _ in range(STEPS.get(p, 0)):
                        next(steps, None)
                    if p < 3:
                        wait("ring_out", OUT0 + N_OUT * i)
                    need = [OUT[m] for m in needs]
                    if p >= 3 and name != "g":
                        before = list(PR)[p - 3]
                        if before in OUT:
                            need.append(OUT[before])
                        else:
                            wait("low_out", 2 * i + 3 + (before == "za"))
                    if need:
                        wait("ring_out", OUT0 + N_OUT * i + 1 + max(need))
                    return pbank(name)

                def end(ins):
                    ins.then_inc(S("wkv_ps"), 1)
                    done[0] += 1

                def heads(out, pairs, start=True, stop=True, **kw):
                    for h in range(2):
                        r = slice(64 * h, 64 * h + 64)
                        for n, (a, b) in enumerate(pairs):
                            last = pe.matmul(out[r, :], a[r, :], b[r, :], start=start and n == 0,
                                             stop=stop and n == len(pairs) - 1, **kw)
                    return last

                def each(name, a, b, needs=(), n=NC):
                    o = begin(name, *needs)
                    for c in range(n):
                        s = slice(64 * c, 64 * c + 64)
                        last = heads(o[:, s], [(a[:, s], b[:, s])])
                    end(last)

                o = begin("s0t")
                for b in range(NB):
                    last = pe.transpose(o[:, 64 * b:64 * b + 64], s0raw[:, 128 * b:128 * b + 128], ident[64:128, 64:128])
                end(last)
                o = begin("bonus")
                wait("rk_ready", i + 1)
                end(pe.matmul(o[:, 0:T], blk[:, :], rk, start=True, stop=True))
                o = begin("A")
                wait("ops_ready", i + 1)
                for c in range(NC):
                    s = slice(64 * c, 64 * c + 64)
                    last = heads(o[:, s], [(alp[:, s], be[:, s])])
                end(last)
                each("B", be, alp)
                each("Bk", ka, alp)
                each("Cb", be, rh)
                each("Ck", ka, rh)
                for name, src in (("beT", be), ("kaT", ka), ("vT", v_)):
                    o = begin(name)
                    if name == "vT":
                        wait("v_copied", i + 1)
                    for c in range(NC):
                        s = slice(64 * c, 64 * c + 64)
                        last = heads(o[:, s], [(src[:, s], m_id[:, :])])
                    end(last)
                each("A2", t_bd, t_ad, ("B",))
                each("B2", t_ad, t_bd)
                wait("r_ready", i + 1)
                each("R1", t_a2, t_r, ("A2",))
                each("RT1", t_b2, t_rt, ("B2",))
                each("A4", t_b2, t_a2)
                each("B4", t_a2, t_b2)
                each("R2", t_ad, t_r, ("A4", "R1"))
                each("RT2", t_bd, t_rt, ("B4", "RT1"))
                each("Q", t_rt, t_bo, ("RT2",), NCK)
                each("QT", t_bo, t_rt, (), NCK)
                each("Q2", t_b2, t_a2, ("QT",), NCK)
                each("QT2", t_a2, t_b2, (), NCK)
                each("QT4", t_ad, t_bd, ("QT2",), NCK)
                each("W1", t_rt, t_r, ("QT4", "R2"), NCK)
                each("W2", t_bd, t_r, ("W1",), NCK)
                each("W3", t_b2, t_r, ("W2",), NCK)
                o = begin("z")
                wait("pair_in", 64 * i + 128)
                end(pe.matmul(o[:, 0:T], wlr[0:64, 0:128], wa_in[0:64, :], start=True, stop=True))
                o = begin("za")
                end(pe.matmul(o[:, 0:T], wlr[64:128, 0:128], wa_in[64:128, :], start=True, stop=True))
                for c in range(NC):
                    s = slice(64 * c, 64 * c + 64)
                    prev = st_pp[(c + 1) % 2]
                    first = c == 0
                    o = begin(f"X{c}", f"S{c - 1}" if 0 < c < NCK else "W3")
                    if c < NCK:
                        end(heads(o[:, 0:64], [(t_bk[:, s], v_t[:, s])] + ([] if first else [(alp[:, s], prev)])))
                    else:
                        end(heads(o[:, 0:64], [(t_bk[:, s], v_t[:, s])] + [(alm[:, b, :], s0t[:, b, :]) for b in range(NB)]))
                    o = begin(f"SA{c}", f"X{c}")
                    end(heads(o[:, 0:64], [(t_r[:, s], xs_)]))
                    o = begin(f"S{c}", f"SA{c}")
                    if c < NCK:
                        end(heads(o[:, 0:64], [(be_t[:, s], sa_), (ka_t[:, s], v_t[:, s])]))
                        if first:
                            wait("gated_out", i + 1)
                        heads(bank[6][:, s], [(sa_, t_cb[:, s]), (v_t[:, s], t_ck[:, s])] + ([] if first else [(prev, rh[:, s])]))
                    else:
                        wait("sam_ready", i + 1)
                        end(heads(o[:, :], [(be_t[:, s], sam.rearrange("p b v -> p (b v)")),
                                            (ka_t[:, s], vtm.rearrange("p b v -> p (b v)"))]))
                        heads(bank[6][:, s], [(sa_, t_cb[:, s]), (v_t[:, s], t_ck[:, s])], stop=False, skip_group_check=True)
                        for b in range(NB):
                            w = slice(TP + 8 * b, TP + 8 * b + 8)
                            last = heads(bank[6][:, w], [(s0t[:, b, :], rh[:, w])], start=False, stop=b == NB - 1,
                                         skip_group_check=True)
                        last.then_inc(S("y_ps"), 1)
                    if first:
                        o = begin("ssq")
                        wait("kk_sq", i + 2)
                        end(pe.matmul(o[:, 0:T], blk[:, :], sq, start=True, stop=True))
                for m in range(2):
                    o = begin(f"tr{m}", "S4")
                    for b in range(4):
                        last = pe.transpose(o[0:64, 128 * b:128 * b + 128], sam[:, 4 * m + b, :], ident[:, :])
                    end(last)
                o = begin("trp", "S3")
                end(pe.transpose(o[0:64, 0:128], st_pp[1], ident[:, :]))
                o = begin("mean")
                wait("y_out", i + 1)
                end(pe.matmul(o[:, 0:T], blk[:, :], y_, start=True, stop=True))
                o = begin("var")
                wait("ym_sq", i + 1)
                end(pe.matmul(o[:, 0:T], blk[:, :], ysq, start=True, stop=True))
                o = begin("g")
                wait("gate_in", 16 * i + 16)
                end(pe.matmul(o[:, 0:T], wlr[:, 128:256], sg, start=True, stop=True))
                assert next(steps, 0) == 0

        gu = wk[:, 0:2560].rearrange("p (k t) -> p k t", k=KW)
        gv = wk[:, 2560:5120].rearrange("p (k t) -> p k t", k=KW)

        def guq_pe(pe):
            with pe.Fori(0, 6) as i:
                for g in range(2):
                    pe_group(pe, U_GUQ + 2 * g, T_GUQ + 2 * g, ah, al_, 2, 4, 4, i)

        def guq_act(act):
            act.wait_ge(S("state_stored"), 48)
            for n, dst in enumerate((gu, gv, q)):
                with act.Fori(2 * n, 2 * n + 2) as i:
                    for g in range(2):
                        for h in range(2):
                            hi_unit(act, U_GUQ + 2 * g + 2 + h, 4, i)
                        for c in range(2):
                            t = T_GUQ + 2 * g + c
                            tile_ready(act, U_GUQ + 2 * g + 1, 8, i, c + 1)
                            o = dst[:, ds(4 * i - 8 * n + 2 * g + c, 1), 0:T].rearrange("p k t -> p (k t)")
                            act.activation(o, bank[t % 4][:, 0:T], ACT.Copy if n == 2 else ACT.Gelu_apprx_tanh)\
                                .then_inc(S(f"tile_out{t % 4}"), 1)

        def guq_dve(dve, vv):
            dve.wait_ge(S("shift_stage"), 2)
            dve.wait_ge(S("state_stored"), 48)
            vv.do(dve.memset(q[:, :, T:XT_], 0.0), "q_pad")
            for k in (24, 25):
                mix_shift(dve, vv, row_(k), k, pcol("mu_shift", k))
            with vv.loop(0, 6, {"dve": 12}) as i:
                for h in range(4):
                    lo_unit(dve, U_GUQ + 2 + h, 4, i)
                    mix_shift(dve, vv, row_(4 * i + h), 4 * i + h, pcol("mu_shift", 4 * i + h))

        sq_v = mixf[:, 0:2560]
        vtok = mixf[:, 0:3072].rearrange("p (t c) -> p t c", t=3)
        ws_raw = mixf[:, 3072:4096].rearrange("p (g s) -> p g s", g=8)
        ws_t = mixf[:, 4096:5120].rearrange("p (g t) -> p g t", g=8)
        ws_s = zz[0:TS, 0:512].rearrange("p (g t) -> p g t", g=8)
        v_mu, v_rs = zz[:, 640:960], zz[:, 960:1280]
        bs_row = wk[0:1, 2560:5120].rearrange("p (g t) -> p g t", g=8)

        def sgu_pool(pool):
            pool.wait_ge(S("xn_lo"), 4)
            pool.dma_start(ws_raw, A["w_s"].rearrange("g t s -> t g s")).then_inc(S("ws_in"), 16)
            pool.wait_ge(S("vt_out"), 6)
            pool.dma_start(O["sgu_v"], vtok[0:TS, 2, :]).then_inc(S("sguv_stored"), 16)
            b_s = A["b_s"].rearrange("(o g) t -> o g t", o=1)
            for c in range(2):
                pool.dma_start(bs_row[:, :, 128 * c:128 * c + 128], b_s).then_inc(S("bs_in"), 16)
            for b in range(NB):
                pool.dma_start(bs_row[:, :, TP + 8 * b:TP + 8 * b + 8], b_s[:, :, 0:8]).then_inc(S("bs_in"), 16)
            pool.wait_ge(S("bl_ready"), 1)
            for n, src in enumerate((bh, bl)):
                pool.dma_start(A["sgu_parts"][n], src[:, :, :].rearrange("p k t -> p (k t)")).then_inc(S("sgu_away"), 16)

        def sgu_dve(dve, vv):
            for t in range(4):
                dve.wait_ge(S(f"tile_out{t}"), 14 if t >= 2 else 15)
            gvt = gv.rearrange("p k t -> p t k")
            vv.do(dve.tensor_reduce(v_mu, gvt, AX_X, ALU.add), "v_sum")
            dve.wait_ge(S("sgu_ps"), 1)
            vv.do(dve.tensor_scalar(v_mu, bank[4][:, 0:T], -1.0 / W, None, ALU.mult))
            vv.do(dve.tensor_tensor(gv, gv, bmid(v_mu, KW), ALU.add), "v_centred")
            dve.wait_ge(S("v_squares"), 1)
            vv.do(dve.tensor_reduce(v_rs, sq_v.rearrange("p (k t) -> p t k", k=KW), AX_X, ALU.add), "v_sum")
            dve.wait_ge(S("sgu_ps"), 2)
            vv.do(dve.tensor_scalar(v_rs, bank[5][:, 0:T], 1.0 / W, LN_EPS, ALU.mult, ALU.add), "v_var")
            dve.wait_ge(S("v_std"), 1)
            vv.do(dve.reciprocal(v_rs, v_rs))
            vv.do(dve.tensor_tensor(gv, gv, bmid(v_rs, KW), ALU.mult))
            for k in range(KW):
                vv.do(dve.tensor_scalar(gv[:, k, :], gv[:, k, :], pcol("sgu_g", k), pcol("sgu_b", k), ALU.mult, ALU.add), "v_normed")
            for n in range(2):
                dve.wait_ge(S("sgu_ps"), 9 + n)
                vv.do(dve.tensor_tensor(ws_t[:, 4 * n:4 * n + 4, :], bank[6 + n][:, :].rearrange("p (g t) -> p g t", g=4),
                                        bmid(m_u[:, :], 4), ALU.mult), "ws_out")
            dve.wait_ge(S("sgu_ps"), 11)
            for g in range(8):
                vv.do(dve.tensor_tensor(ws_s[:, g, :].rearrange("p (b t) -> p b t", b=NB), bmid(bank[4][0:TS, 8 * g:8 * g + 8], NB),
                                        bc(m_e8[0:TS, :], 8), ALU.mult), "wss_out")
            for g in range(8):
                dve.wait_ge(S("sgu_ps"), 12 + g)
                vv.do(dve.tensor_tensor(gu[:, g, :], gu[:, g, :], bank[4 + g % 4][:, 0:T], ALU.mult), "gated")
            dve.wait_ge(S("bh_ready"), 1)
            vv.do(dve.tensor_tensor(bl[:, :, :], gu, bh[:, :, :], ALU.subtract), "bl_ready")

        def sgu_act(act, aa):
            act.wait_ge(S("v_centred"), 1)
            aa.do(act.activation(sq_v, wk[:, 2560:5120], ACT.Square), "v_squares")
            act.wait_ge(S("v_var"), 1)
            aa.do(act.activation(v_rs, v_rs, ACT.Sqrt), "v_std")
            for f in range(6):
                act.wait_ge(S("sgu_ps"), 3 + f)
                m = TS if f >= 4 else P
                aa.do(act.activation(vtok[0:m, f // 2, 512 * (f % 2):512 * (f % 2) + 512], bank[4 + f % 4][0:m, :], ACT.Copy), "vt_out")
            act.wait_ge(S("gated"), 8)
            aa.do(act.activation(bh[:, :, :], gu, ACT.Copy), "bh_ready")

        def sgu_pe(pe):
            def end(ins):
                ins.then_inc(S("sgu_ps"), 1)
            pe.wait_ge(S("v_sum"), 1)
            end(pe.matmul(bank[4][:, 0:T], ones[:, :], v_mu, start=True, stop=True))
            pe.wait_ge(S("v_sum"), 2)
            end(pe.matmul(bank[5][:, 0:T], ones[:, :], v_rs, start=True, stop=True))
            for f in range(6):
                pe.wait_ge(S("v_normed"), KW)
                if f >= 4:
                    pe.wait_ge(S("vt_out"), f - 3)
                m, t0 = (TS, TP) if f >= 4 else (P, 128 * (f // 2))
                for k in range(4):
                    last = pe.transpose(bank[4 + f % 4][0:m, 128 * k:128 * k + 128], gv[:, 4 * (f % 2) + k, t0:t0 + m], ident[:, :])
                end(last)
            pe.wait_ge(S("ws_in"), 16)
            for n in range(2):
                pe.wait_ge(S("vt_out"), 3 + n)
                for k in range(4):
                    last = pe.transpose(bank[6 + n][:, 128 * k:128 * k + 128], ws_raw[:, 4 * n + k, :], ident[:, :])
                end(last)
            pe.wait_ge(S("vt_out"), 6)
            pe.wait_ge(S("ws_out"), 2)
            end(pe.matmul(bank[4][0:TS, 0:64], rep8, ws_t[0:8, :, 0:8], start=True, stop=True))
            pe.wait_ge(S("bs_in"), 160)
            pe.wait_ge(S("wss_out"), 8)
            for g in range(8):
                if g >= 4:
                    pe.wait_ge(S("gated"), g - 3)
                o, c = bank[4 + g % 4], slice(128 * g, 128 * g + 128)
                pe.matmul(o[:, 0:T], ones[0:1, :], bs_row[:, g, :], start=True, stop=False, skip_group_check=True)
                for t in range(2):
                    pe.matmul(o[:, 128 * t:128 * t + 128], vtok[:, t, c], ws_t[:, g, :], start=False, stop=False, skip_group_check=True)
                end(pe.matmul(o[:, TP:T], vtok[0:TS, 2, c], ws_s[:, g, :], start=False, stop=True, skip_group_check=True))

        kb = wk[:, 0:2048].rearrange("p (m c) -> p m c", m=2)
        vb = wk[:, 2048:4096].rearrange("p (m c) -> p m c", m=2)
        kt = mixf[:, 0:2048].rearrange("p (d m) -> p d m", d=KW)
        pr_, pr_t = zz[:, 0:256], zz[:, 256:512]
        qb = zz[:, 512:768].rearrange("p (k t) -> p k t", k=KW)
        o_tok = zz[:, 768:1024]
        mx, nmx, rsum, rinv = [zz[:, 1300 + n:1301 + n] for n in range(4)]
        XSCALE = float(W // XH) ** -0.5
        SAMPLE_FILLS = 8

        def attn_pool(pool):
            for b in range(NB + 1):
                if b == 0:
                    pool.wait_ge(S("bl_ready"), 1)
                if b == NB:
                    for t in range(4):
                        pool.wait_ge(S(f"mem_stored{t}"), 32)
                for n, (dst, cache, mem, sem) in enumerate(((kb, "cache_mem_k", "mem_k", "k_in"), (vb, "cache_mem_v", "mem_v", "v_in"))):
                    if b:
                        pool.wait_ge(S("at_ps"), SAMPLE_FILLS * (b - 1) + (7 if n else 4))
                    src = A[cache][b].rearrange("(m p) h d -> p m (h d)", p=P) if b < NB else \
                        O[mem].rearrange("(m p) c -> p m c", p=P)
                    pool.dma_start(dst, src).then_inc(S(sem), 16)

        def softmax_dve(dve, vv, n, n_ps):
            dve.wait_ge(S("at_ps"), n_ps)
            vv.do(dve.tensor_reduce(mx, bank[4][:, 0:MEM], AX_X, ALU.max))
            vv.do(dve.tensor_scalar(nmx, mx, -XSCALE, None, ALU.mult), "nmax")
            dve.wait_ge(S("exp_done"), n + 1)
            vv.do(dve.reciprocal(rinv, rsum))
            vv.do(dve.tensor_scalar(pr_, pr_, rinv, None, ALU.mult), "p_ready")

        def attn_dve(dve, vv):
            for b in range(NB):
                base = SAMPLE_FILLS * b
                vv.do(dve.tensor_copy(qb, q[:, :, TP + 8 * b:TP + 8 * b + 32]), "qb")
                softmax_dve(dve, vv, b, base + 5)
                dve.wait_ge(S("at_ps"), base + 6)
                vv.do(dve.tensor_copy(pr_t, bank[5][:, 0:MEM]), "at_v")
                dve.wait_ge(S("at_ps"), base + 7)
                vv.do(dve.tensor_copy(o_tok, bank[6][:, 0:MEM]), "at_v")
                dve.wait_ge(S("at_ps"), base + 8)
                o = bank[7][:, 0:256].rearrange("p (d h t) -> p h d t", d=2, h=4)[:, :, :, 0:8]
                vv.do(dve.tensor_copy(q[:, :, TP + 8 * b:TP + 8 * b + 8].rearrange("p (h d) t -> p h d t", d=2), o), "at_v")
            base = SAMPLE_FILLS * NB + 4
            for n in range(8):
                h, t = n // 2, n % 2
                softmax_dve(dve, vv, NB + n, base + 3 * n + 1)
                dve.wait_ge(S("at_ps"), base + 3 * n + 2)
                vv.do(dve.tensor_copy(pr_t, bank[5][:, 0:MEM]), "at_v")
                dve.wait_ge(S("at_ps"), base + 3 * n + 3)
                vv.do(dve.tensor_copy(q[:, 2 * h:2 * h + 2, 128 * t:128 * t + 128],
                                      bank[6][:, 0:256].rearrange("p (d t) -> p d t", d=2)), "at_v")

        def attn_act(act, aa):
            def kts(base):
                for f in range(4):
                    act.wait_ge(S("at_ps"), base + f + 1)
                    aa.do(act.activation(kt[:, 2 * f:2 * f + 2, :], bank[4 + f][:, :].rearrange("p (d m) -> p d m", d=2), ACT.Copy), "kt_out")

            def exps(n):
                act.wait_ge(S("nmax"), n + 1)
                aa.do(act.activation(pr_, bank[4][:, 0:MEM], ACT.Exp, bias=nmx, scale=XSCALE, accum_out=rsum), "exp_done")

            act.wait_ge(S("sguv_stored"), 16)
            for b in range(NB):
                kts(SAMPLE_FILLS * b)
                exps(b)
            kts(SAMPLE_FILLS * NB)
            for n in range(8):
                exps(NB + n)

        def attn_pe(pe):
            def end(ins):
                ins.then_inc(S("at_ps"), 1)

            def transposes(b):
                pe.wait_ge(S("k_in"), 16 * (b + 1))
                if b == 0:
                    pe.wait_ge(S("gated"), 8)
                else:
                    pe.wait_ge(S("exp_done"), b)
                    pe.wait_ge(S("at_v"), 3 * b)
                for f in range(4):
                    for a in range(2):
                        for m in range(2):
                            c = 128 * (2 * f + a)
                            last = pe.transpose(bank[4 + f][:, 256 * a + 128 * m:256 * a + 128 * m + 128], kb[:, m, c:c + 128], ident[:, :])
                    end(last)

            def turn_p(n, nv):
                pe.wait_ge(S("p_ready"), n + 1)
                pe.wait_ge(S("at_v"), nv)
                for m in range(2):
                    last = pe.transpose(bank[5][:, 128 * m:128 * m + 128], pr_[:, 128 * m:128 * m + 128], ident[:, :])
                end(last)

            pe.wait_ge(S("q_pad"), 1)
            for b in range(NB):
                transposes(b)
                pe.wait_ge(S("kt_out"), 4 * (b + 1))
                pe.wait_ge(S("qb"), b + 1)
                for h in range(XH):
                    for d in range(2):
                        last = pe.matmul(bank[4][32 * h:32 * h + 32, 0:MEM], qb[:, 2 * h + d, :], kt[:, 2 * h + d, :],
                                         start=d == 0, stop=d == 1)
                end(last)
                turn_p(b, 3 * b)
                pe.wait_ge(S("at_v"), 3 * b + 1)
                pe.wait_ge(S("v_in"), 16 * (b + 1))
                for h in range(XH):
                    for m in range(2):
                        last = pe.matmul(bank[6][32 * h:32 * h + 32, 0:256], pr_t[:, 128 * m + 32 * h:128 * m + 32 * h + 32],
                                         vb[:, m, 256 * h:256 * h + 256], start=m == 0, stop=m == 1)
                end(last)
                pe.wait_ge(S("at_v"), 3 * b + 2)
                for d in range(2):
                    last = pe.transpose(bank[7][:, 128 * d:128 * d + 128], o_tok[:, 128 * d:128 * d + 128], ident[:, :])
                end(last)
            transposes(NB)
            pe.wait_ge(S("kt_out"), 4 * (NB + 1))
            for n in range(8):
                h, t = n // 2, n % 2
                pe.wait_ge(S("exp_done"), NB + n)
                for d in range(2):
                    last = pe.matmul(bank[4][:, 0:MEM], q[:, 2 * h + d, 128 * t:128 * t + 128], kt[:, 2 * h + d, :],
                                     start=d == 0, stop=d == 1)
                end(last)
                turn_p(NB + n, 3 * NB + 2 * n)
                pe.wait_ge(S("at_v"), 3 * NB + 2 * n + 1)
                pe.wait_ge(S("v_in"), 16 * (NB + 1))
                for c in range(2):
                    for m in range(2):
                        last = pe.matmul(bank[6][:, 128 * c:128 * c + 128], vb[:, m, 256 * h + 128 * c:256 * h + 128 * c + 128],
                                         pr_t[:, 128 * m:128 * m + 128], start=m == 0, stop=m == 1)
                end(last)

        def attn_split_act(act, aa):
            act.wait_ge(S("at_v"), 3 * NB + 16)
            act.wait_ge(S("sgu_away"), 32)
            aa.do(act.activation(bh[:, :, :], q[:, :, 0:T], ACT.Copy), "bh_ready")

        def attn_split_dve(dve, vv):
            dve.wait_ge(S("bh_ready"), 2)
            dve.wait_ge(S("sgu_away"), 32)
            vv.do(dve.tensor_tensor(bl[:, :, :], q[:, :, 0:T], bh[:, :, :], ALU.subtract), "bl_ready")
            vv.do(dve.memset(mixf, 0.0))

        def branch_act_unit(act, j, i):
            hi_unit(act, U_BR[0] + j + 2, 6, i)
            if j % 3 == 1:
                for c in range(2):
                    t = T_BR[0] + 4 * (j // 3) + c
                    tile_ready(act, U_BR[0] + j, 12, i, c + 1)
                    act.wait_ge(S("gate_free"), 4 * i + 2 * (j // 3) + c + 1)
                    act.activation(gs[:, c, :], bank[t % 4][:, 0:T], ACT.Tanh, scale=0.5).then_inc(S(f"tile_out{t % 4}"), 1)

        def add_branch(dve, vv, n, g, c, i):
            tg = T_BR[0] + 4 * g + c
            tb = tg + 2
            dve.wait_ge(S(f"tile_out{tg % 4}"), 2 * i + tg // 4 + 1)
            tile_ready(dve, U_BR[0] + 3 * g + 2, 12, i, c + 1)
            gate = gs[:, c, :]
            dve.scalar_tensor_tensor(out=gate, in0=gate, scalar=1.0, in1=bank[tb % 4][:, 0:T],
                                     op0=ALU.add, op1=ALU.mult).then_inc(S(f"tile_out{tb % 4}"), 1)
            dve.wait_ge(S(f"tile_out{tb % 4}"), 2 * i + tb // 4 + 1)
            m = mix[:, ds(4 * i - 16 * n + 2 * g + c, 1), :].rearrange("p k t -> p (k t)")
            vv.do(dve.tensor_tensor(m, m, gate, ALU.add), "gate_free")

        def branch_pe(pe):
            with pe.Fori(8, 12) as i:
                for g in range(2):
                    pe_group(pe, U_BR[0] + 3 * g, T_BR[0] + 4 * g, ah, al_, 2, 6, 8, i)
                    pe.wait_ge(S("bl_ready"), 3)
                    pe_group(pe, U_BR[0] + 3 * g + 2, T_BR[0] + 4 * g + 2, bh, bl, 1, 6, 8, i)

        def branch_act(act, aa):
            tile_ready(act, U_BR[2] - 1)
            act.wait_ge(S("gated_out"), KW + 1)
            aa.do(act.activation(bh[:, :, :], rw[:, 0:KW, 0:T], ACT.Copy), "bh_ready")
            with act.Fori(8, 12) as i:
                for j in range(6):
                    branch_act_unit(act, j, i)

        def branch_dve(dve, vv):
            dve.wait_ge(S("bh_ready"), 3)
            vv.do(dve.tensor_tensor(bl[:, :, :], rw[:, 0:KW, 0:T], bh[:, :, :], ALU.subtract), "bl_ready")
            with vv.loop(8, 12, {"gate_free": 4}) as i:
                for g in range(2):
                    for h in range(3):
                        lo_unit(dve, U_BR[0] + 3 * g + 2 + h, 6, i)
                    for c in range(2):
                        add_branch(dve, vv, 2, g, c, i)

        mo = wk[:, 0:5120].rearrange("p (k t) -> p k t", k=KD)

        def out_pe(pe):
            pe.wait_ge(S("mx_lo"), 4)
            with pe.Fori(0, 4) as i:
                for g in range(2):
                    pe_group(pe, U_OUT + 2 * g, T_OUT + 2 * g, ah, al_, 2, 4, 4, i)

        def out_act(act, aa):
            act.wait_ge(S("gate_free"), 50)
            tile_ready(act, U_OUT - 1)
            for c in range(4):
                aa.do(act.activation(ah[:, 4 * c:4 * c + 4, :], mix[:, 4 * c:4 * c + 4, :], ACT.Copy, scale=0.5), "mx_hi")
            with act.Fori(0, 4) as i:
                for g in range(2):
                    for h in range(2):
                        hi_unit(act, U_OUT + 2 * g + 2 + h, 4, i)
                    for c in range(2):
                        t = T_OUT + 2 * g + c
                        tile_ready(act, U_OUT + 2 * g + 1, 8, i, c + 1)
                        act.activation(mo[:, ds(4 * i + 2 * g + c, 1), :].rearrange("p k t -> p (k t)"),
                                       bank[t % 4][:, 0:T], ACT.Copy).then_inc(S(f"tile_out{t % 4}"), 1)

        def out_dve(dve, vv):
            for c in range(4):
                dve.wait_ge(S("mx_hi"), c + 1)
                vv.do(dve.scalar_tensor_tensor(out=al_[:, 4 * c:4 * c + 4, :], in0=mix[:, 4 * c:4 * c + 4, :], scalar=0.5,
                                               in1=ah[:, 4 * c:4 * c + 4, :], op0=ALU.mult, op1=ALU.subtract), "mx_lo")
            with dve.Fori(0, 4) as i:
                for h in range(4):
                    lo_unit(dve, U_OUT + 2 + h, 4, i)

        red, rstd = gs[:, 0, :], gs[:, 1, :]

        def rms_act(act, aa, n, src, sq):
            aa.do(act.activation(sq, src, ACT.Square), "rms_squares")
            act.wait_ge(S("rms_mean"), n + 1)
            aa.do(act.activation(rstd, rstd, ACT.Sqrt), "rms_root")

        def rms_dve(dve, vv, n, sq):
            dve.wait_ge(S("rms_squares"), n + 1)
            vv.do(dve.tensor_reduce(red, sq.rearrange("p (k t) -> p t k", k=KD), AX_X, ALU.add), "rms_sum")
            dve.wait_ge(S("rms_ps"), n + 1)
            vv.do(dve.tensor_scalar(rstd, bank[4][:, 0:T], 1.0 / D, RMS_EPS, ALU.mult, ALU.add), "rms_mean")
            dve.wait_ge(S("rms_root"), n + 1)
            vv.do(dve.reciprocal(rstd, rstd), "rms_ready_t")

        def rms_pe(pe, n):
            pe.wait_ge(S("rms_sum"), n + 1)
            pe.matmul(bank[4][:, 0:T], ones[:, :], red, start=True, stop=True).then_inc(S("rms_ps"), 1)

        x2_tok = [rwr[:, 0:D], rwr[:, D:2 * D], rwr[0:TS, 2 * D:3 * D]]
        cst_raw = qr[:, 0:11 * P]
        cst = rwr[:, 5552:5552 + 16 * 88].rearrange("p (r k) -> p r k", r=16)
        tail = rwr[:, 6960:6960 + 18 * 88].rearrange("p (r k) -> p r k", r=18)

        def res_pool(pool):
            pool.wait_ge(S("bl_ready"), 3)
            for k in range(2):
                pool.dma_start(x2_tok[k], A["x_prompt"][128 * k:128 * k + 128, :]).then_inc(S("x2_in"), 16)
            pool.dma_start(x2_tok[2], A["x_sample"]).then_inc(S("x2_in"), 16)
            pool.dma_start(cst_raw.rearrange("p (j n) -> p j n", n=P),
                           A["state_ffn_conv"].rearrange("b r (k c) -> (b r k) c", c=P).rearrange("(j p) c -> p j c", p=P))\
                .then_inc(S("x2_in"), 16)

        def res_act(act, aa):
            for t in range(4):
                act.wait_ge(S(f"tile_out{t}"), T_FFN // 4 + (1 if t < T_FFN % 4 else 0))
            act.wait_ge(S("mx_lo"), 4)
            rms_act(act, aa, 0, wk[:, 0:5120], mixf)
            act.wait_ge(S("h_ready"), KD)
            rms_act(act, aa, 1, mixf, wk[:, 0:5120])
            for f in range(3):
                act.wait_ge(S("cst_ps"), f + 1)
                w = 512 if f < 2 else 384
                aa.do(act.activation(rwr[:, 5552 + 512 * f:5552 + 512 * f + w], bank[4 + f][:, 0:w], ACT.Copy), "cst_out")
            for c in range(4):
                act.wait_ge(S("hn"), 4 * (c + 1))
                aa.do(act.activation(ah[:, 4 * c:4 * c + 4, :], mo[:, 4 * c:4 * c + 4, :], ACT.Copy), "hn_hi")

        def res_dve(dve, vv):
            rms_dve(dve, vv, 0, mixf)
            for k in range(KD):
                vv.do(dve.scalar_tensor_tensor(out=mo[:, k, :], in0=mo[:, k, :], scalar=pcol("g_post_mix", k), in1=rstd,
                                               op0=ALU.mult, op1=ALU.mult))
                dve.wait_ge(S("res_ps"), k + 1)
                vv.do(dve.tensor_tensor(mix[:, k, :], mo[:, k, :], bank[4 + k % 4][:, 0:T], ALU.add), "h_ready")
            rms_dve(dve, vv, 1, wk[:, 0:5120])
            for c in range(4):
                for k in range(4 * c, 4 * c + 4):
                    vv.do(dve.scalar_tensor_tensor(out=mo[:, k, :], in0=mix[:, k, :], scalar=pcol("g_pre_ffn", k), in1=rstd,
                                                   op0=ALU.mult, op1=ALU.mult), "hn")
            for c in range(4):
                dve.wait_ge(S("hn_hi"), c + 1)
                vv.do(dve.tensor_tensor(al_[:, 4 * c:4 * c + 4, :], mo[:, 4 * c:4 * c + 4, :], ah[:, 4 * c:4 * c + 4, :],
                                        ALU.subtract), "hn_lo")
            vv.do(dve.memset(wk[:, 0:5120], 0.0))
            vv.do(dve.memset(ext[:, :, 0:2], 0.0))
            vv.do(dve.memset(rwr[:, 1352:4056], 0.0), "ext_set")

        def res_pe(pe):
            rms_pe(pe, 0)
            pe.wait_ge(S("x2_in"), 64)
            for k in range(KD):
                if k >= 4:
                    pe.wait_ge(S("h_ready"), k - 3)
                else:
                    pe.wait_ge(S("rms_ready_t"), 1)
                x_transposes(pe, x2_tok, k, bank[4 + k % 4]).then_inc(S("res_ps"), 1)
            pe.wait_ge(S("h_ready"), KD)
            rms_pe(pe, 1)
            pe.wait_ge(S("rms_ready_t"), 2)
            for f in range(3):
                for j in range(4 * f, min(4 * f + 4, 11)):
                    last = pe.transpose(bank[4 + f][:, 128 * (j % 4):128 * (j % 4) + 128], cst_raw[:, 128 * j:128 * j + 128], ident[:, :])
                last.then_inc(S("cst_ps"), 1)

        ext = rwr[:, 0:1352].rearrange("p (k t) -> p k t", k=4)
        cgate = rwr[:, 1352:2704].rearrange("p (k t) -> p k t", k=4)
        cval = rwr[:, 2704:4056].rearrange("p (k t) -> p k t", k=4)
        facc = mo
        UF, TF = U_FFN, T_FFN

        def smp_c(t):
            return t[:, :, TP + 2:CEXT].rearrange("p k (b t) -> p k b t", b=NB)

        def up_pe(pe, u, t, k=0, i=0):
            for g in range(2):
                pe_group(pe, u + 2 * g, t + 2 * g, ah, al_, 2, 12 if k else 0, 24 if k else 0, i)

        def down_pe(pe, u, t, k=0, i=0, c=0):
            pe.wait_ge(S("ff_lo"), lin(c, 2 if k else 0, i))
            for g in range(4):
                pe.wait_ge(S("lo_done"), lin(u + g + 1, 12 if k else 0, i))
                s = (u + g) % NS
                for c4 in range(4):
                    tt = t + 4 * g + c4
                    bank_free(pe, tt, 24 if k else 0, i)
                    for kk in range(4):
                        o = 512 * kk + 128 * c4
                        last = three(pe, bank[tt % 4][:, 0:T], hi[s][:, o:o + P], lo[s][:, o:o + P],
                                     bh[:, kk, :], bl[:, kk, :], kk == 0, kk == 3)
                    last.then_inc(S("parts"), 1)

        def ffn_pe(pe):
            pe.wait_ge(S("hn_lo"), 4)
            up_pe(pe, UF, TF)
            up_pe(pe, UF + 4, TF + 4)
            with pe.Fori(0, NCH - 1) as i:
                up_pe(pe, UF + 8, TF + 8, 1, i)
                down_pe(pe, UF + 12, TF + 12, 1, i, 2)
                up_pe(pe, UF + 16, TF + 28, 1, i)
            down_pe(pe, U_END - 4, T_FFN + 8 + 24 * (NCH - 1), 0, 0, 2 * NCH)

        def ffn_act(act, aa):
            def rows(u, t, q, g, k=0, i=0):
                tk, pk = (24, 32) if k else (0, 0)
                for c in range(2):
                    l, b = 2 * g + c, (t + c) % 4
                    if q >= 4:
                        act.wait_ge(S("ext_free"), lin(q + c - 3, 8 if k else 0, i))
                    tile_ready(act, u, pk, i, c + 1)
                    act.activation(ext[:, l, 2:2 + TP], bank[b][:, 0:TP], ACT.Copy)
                    act.activation(smp_c(ext)[:, l, :, 2:2 + TB], bank[b][:, TP:T].rearrange("p (b t) -> p b t", b=NB),
                                   ACT.Copy).then_inc(S(f"tile_out{b}"), 1)

            def his(u, n, k=0, i=0):
                for h in range(n):
                    hi_unit(act, u + h + 2, 12 if k else 0, i, 32 if k else 0)

            def gate():
                act.wait_ge(S("gate_conv"), aa.value("gate_act") + 1)
                aa.do(act.activation(rwr[:, 1352:2704], rwr[:, 1352:2704], ACT.Gelu_apprx_tanh), "gate_act")

            def split(turn):
                act.wait_ge(S("ff"), turn + 1)
                aa.do(act.activation(bh[:, 0:4, 0:TP], cval[:, :, 0:TP], ACT.Copy), "ff_hi")
                aa.do(act.activation(bh[:, 0:4, TP:T].rearrange("p k (b t) -> p k b t", b=NB), smp_c(cval)[:, :, :, 0:TB], ACT.Copy),
                      "ff_hi")

            act.wait_ge(S("ext_set"), 1)
            for half in range(2):
                u, t = UF + 4 * half, TF + 4 * half
                his(u, 2)
                rows(u + 1, t, 4 * half, 0)
                his(u + 2, 2)
                rows(u + 3, t + 2, 4 * half + 2, 1)
                if half == 0:
                    gate()
            with aa.loop(0, NCH - 1, {"gate_act": 1, "ff_hi": 2}) as i:
                his(UF + 8, 2, 1, i)
                rows(UF + 9, TF + 8, 8, 0, 1, i)
                his(UF + 10, 1, 1, i)
                split(i)
                his(UF + 11, 1, 1, i)
                rows(UF + 11, TF + 10, 10, 1, 1, i)
                his(UF + 12, 6, 1, i)
                gate()
                rows(UF + 17, TF + 28, 12, 0, 1, i)
                his(UF + 18, 2, 1, i)
                rows(UF + 19, TF + 30, 14, 1, 1, i)
            split(NCH - 1)
            for g in range(2):
                hi_unit(act, U_END - 2 + g)

        def ffn_dve(dve, vv):
            def conv(t, q, k=0, i=0):
                l, half = q % 4, q // 4 % 2
                dst = cval if half else cgate
                dve.wait_ge(S(f"tile_out{t % 4}"), lin(t // 4 + 1, 6 if k else 0, i))
                tile = KF * half + 4 * (q // 8) + l

                def col(c):
                    return ds(4 * i + c, 1) if k else slice(c, c + 1)

                vv.do(dve.tensor_copy(smp_c(ext)[:, l, :, 0:2],
                                      cst.rearrange("p (b r) k -> p b r k", r=2)[:, :, :, col(tile)].rearrange("p b r k -> p b (r k)")))
                for j in range(3):
                    w = prm[:, col(COL["conv_w"] + 88 * j + tile)]
                    o, x = dst[:, l, 0:336], ext[:, l, j:j + 336]
                    if j == 0:
                        vv.do(dve.tensor_scalar(o, x, w, prm[:, col(COL["conv_b"] + tile)], ALU.mult, ALU.add))
                    else:
                        vv.do(dve.scalar_tensor_tensor(out=o, in0=x, scalar=w, in1=o, op0=ALU.mult, op1=ALU.add),
                              "gate_conv" if j == 2 and q % 8 == 3 else None)
                vv.do(dve.tensor_copy(tail[:, 0:2, col(tile)].rearrange("p r k -> p (r k)"), ext[:, l, TP:TP + 2]))
                vv.do(dve.tensor_copy(tail[:, 2:18, :].rearrange("p (b r) k -> p b r k", r=2)[:, :, :, col(tile)]
                                      .rearrange("p b r k -> p b (r k)"), smp_c(ext)[:, l, :, TB:TB + 2]), "ext_free")

            def value(turn):
                dve.wait_ge(S("gate_act"), turn + 1)
                vv.do(dve.tensor_tensor(rwr[:, 2704:4056], rwr[:, 2704:4056], rwr[:, 1352:2704], ALU.mult), "ff")

            def split(turn):
                dve.wait_ge(S("ff_hi"), 2 * turn + 2)
                vv.do(dve.tensor_tensor(bl[:, 0:4, 0:TP], cval[:, :, 0:TP], bh[:, 0:4, 0:TP], ALU.subtract), "ff_lo")
                vv.do(dve.tensor_tensor(bl[:, 0:4, TP:T].rearrange("p k (b t) -> p k b t", b=NB), smp_c(cval)[:, :, :, 0:TB],
                                        bh[:, 0:4, TP:T].rearrange("p k (b t) -> p k b t", b=NB), ALU.subtract), "ff_lo")

            def lo(u, k=0, i=0):
                lo_unit(dve, u + 2, 12 if k else 0, i, 32 if k else 0)

            def down(u, t, g, k=0, i=0):
                for c in range(4):
                    tt = t + 4 * g + c
                    b = tt % 4
                    dve.wait_ge(S("parts"), lin(parts_of(u + g) - 3 + c, 32 if k else 0, i))
                    f = facc[:, 4 * g + c, :]
                    dve.tensor_tensor(f, f, bank[b][:, 0:T], ALU.add).then_inc(S(f"tile_out{b}"), 1)
                    dve.wait_ge(S(f"tile_out{b}"), lin(tt // 4 + 1, 6 if k else 0, i))

            for u in range(8):
                lo(UF + u)
                if u in (1, 3, 5):
                    conv(TF + u - 1, u - 1)
                    conv(TF + u, u)
            with vv.loop(0, NCH - 1, PER_F) as i:
                lo(UF + 8, 1, i)
                conv(TF + 6, 6, 1, i)
                lo(UF + 9, 1, i)
                conv(TF + 7, 7, 1, i)
                value(i)
                lo(UF + 10, 1, i)
                split(i)
                conv(TF + 8, 8, 1, i)
                lo(UF + 11, 1, i)
                for g in range(4):
                    down(UF + 12, TF + 12, g, 1, i)
                    lo(UF + 12 + g, 1, i)
                lo(UF + 16, 1, i)
                conv(TF + 9, 9, 1, i)
                conv(TF + 10, 10, 1, i)
                lo(UF + 17, 1, i)
                conv(TF + 11, 11, 1, i)
                lo(UF + 18, 1, i)
                conv(TF + 28, 12, 1, i)
                lo(UF + 19, 1, i)
                conv(TF + 29, 13, 1, i)
            for q in (6, 7):
                conv(TF + q + 24 * (NCH - 1), 8 * (NCH - 1) + q)
            value(NCH - 1)
            split(NCH - 1)
            for g in range(4):
                down(U_END - 4, T_FFN + 8 + 24 * (NCH - 1), g)
                lo(U_END - 4 + g)

        PER_F = {"dve": 39, "gate_conv": 1, "ext_free": 8, "ff": 1, "ff_lo": 2}

        y_stage = [rwr[:, 0:D], rwr[:, D:2 * D], rwr[0:TS, 2 * D:3 * D]]
        tail_stage = raw[0]

        def end_act(act, aa):
            for t in range(4):
                act.wait_ge(S(f"tile_out{t}"), 434 // 4 + (1 if t < 434 % 4 else 0))
            rms_act(act, aa, 2, wk[:, 0:5120], rwr[:, 0:5120])
            for f in range(4):
                act.wait_ge(S("tail_ps"), f + 1)
                w = 512 if f < 3 else 128
                aa.do(act.activation(tail_stage[:, 512 * f:512 * f + w], bank[4 + f][:, 0:w], ACT.Copy), "tail_out")
            for f in range(12):
                c, k = f // 3, f % 3
                act.wait_ge(S("y_ps"), KW + f + 1)
                m = TS if k == 2 else P
                aa.do(act.activation(y_stage[k][:, 512 * c:512 * c + 512], bank[4 + f % 4][0:m, :], ACT.Copy), "y_staged")

        def end_dve(dve, vv):
            rms_dve(dve, vv, 2, rwr[:, 0:5120])
            for k in range(KD):
                vv.do(dve.scalar_tensor_tensor(out=facc[:, k, :], in0=facc[:, k, :], scalar=pcol("g_post_ffn", k), in1=rstd,
                                               op0=ALU.mult, op1=ALU.mult))
                vv.do(dve.tensor_tensor(facc[:, k, :], facc[:, k, :], mix[:, k, :], ALU.add), "y_ready")

        def end_pe(pe):
            rms_pe(pe, 2)
            pe.wait_ge(S("rms_ready_t"), 3)
            tails = rwr[:, 6960:6960 + 18 * 88]
            pieces = [(0, 128), (128, 48)] + [(176 + 128 * j, 128) for j in range(11)]
            pe.wait_ge(S("ext_free"), 8 * NCH)
            for n, (at, m) in enumerate(pieces):
                last = pe.transpose(bank[4 + n // 4][0:m, 128 * (n % 4):128 * (n % 4) + 128], tails[:, at:at + m], ident[:, :])
                if n % 4 == 3 or n == len(pieces) - 1:
                    last.then_inc(S("tail_ps"), 1)
            for f in range(12):
                c, k = f // 3, f % 3
                pe.wait_ge(S("y_ready"), 4 * c + 4)
                if f < 4:
                    pe.wait_ge(S("tail_out"), f + 1)
                else:
                    pe.wait_ge(S("y_staged"), f - 3)
                m = TS if k == 2 else P
                for j in range(4):
                    last = pe.transpose(bank[4 + f % 4][0:m, 128 * j:128 * j + 128], facc[:, 4 * c + j, 128 * k:128 * k + m], ident[:, :])
                last.then_inc(S("y_ps"), 1)

        def end_pool(pool):
            pool.wait_ge(S("tail_out"), 4)
            pool.dma_start(O["conv_p"][0:128, :], tail_stage[:, 0:128]).then_inc(S("stored"), 16)
            pool.dma_start(O["conv_p"][128:176, :], tail_stage[0:48, 128:256]).then_inc(S("stored"), 16)
            pool.dma_start(O["conv_s"].rearrange("(j p) n -> p j n", p=P),
                           tail_stage[:, 256:256 + 11 * P].rearrange("p (j n) -> p j n", n=P)).then_inc(S("stored"), 16)
            for k in range(3):
                pool.wait_ge(S("y_staged"), 10 + k)
                pool.dma_start(O["y_p"][128 * k:128 * k + 128, :] if k < 2 else O["y_s"], y_stage[k]).then_inc(S("stored"), 16)
            pool.wait_ge(S("stored"), 16 * 6)
            pool.wait_ge(S("sguv_stored"), 16)
            pool.wait_ge(S("state_stored"), 48 * (KW + 1))
            for t in range(4):
                pool.wait_ge(S(f"mem_stored{t}"), 32)

        @block.gpsimd
        def _(pool):
            pp = Prog(pool, S, "pool")
            pool_loads(pool)
            pool_constants(pool, pp)
            mem_pool(pool)
            shift_pool(pool)
            sgu_pool(pool)
            attn_pool(pool)
            wkv_pool(pool)
            res_pool(pool)
            end_pool(pool)

        @block.sync
        def _(sp):
            for u in range(16):
                g = u // 4
                load_unit(sp, kv(A["w_mem_k"] if g < 2 else A["w_mem_v"], 4 * (u % 4), 512 * (g % 2), 4, 512), u)
            for h in range(2):
                load_unit(sp, kv(A["w_in"], 8 * h, 0), U_RW + h)
            with sp.Fori(0, 12) as i:
                for g in range(2):
                    for h in range(2):
                        load_unit(sp, kv(A["w_in"], 8 * h, 512 * i + 256 * (g + 1)), U_RW + 2 + 2 * g + h, 4, i)
            for n, b in enumerate((2, 1, 0)):
                with sp.Fori(0, 4) as i:
                    for g in range(2):
                        for h in range(2):
                            load_unit(sp, kv(A["w_in"], 8 * h, 512 * i + NSH + 3 * W + D * b + 256 * g), U_BR[n] + 3 * g + h, 6, i)
                        load_unit(sp, kv(A["w_branch"][b], 0, 512 * i + 256 * g), U_BR[n] + 3 * g + 2, 6, i)
            with sp.Fori(0, 4) as i:
                for g in range(2):
                    for h in range(2):
                        load_unit(sp, kv(A["w_out"], 8 * h, 512 * i + 256 * g), U_OUT + 2 * g + h, 4, i)

            def up(half, c, k, i):
                for g in range(2):
                    for h in range(2):
                        n0 = half * DFF + 256 * g + (512 if k else 0)
                        load_unit(sp, kv(A["w_up"], 8 * h, lin(n0, 512 if k else 0, i)), c + 2 * g + h, 12 if k else 0, i)

            def down(rows, c, k, i):
                src = A["w_down"].rearrange("(c kt p) n -> p c kt n", kt=4, p=P)
                for g in range(4):
                    cc = ds(i, 1) if k else slice(rows, rows + 1)
                    load_unit(sp, src[:, cc, :, 512 * g:512 * g + 512].rearrange("p c kt n -> p (c kt) n"), c + g, 12 if k else 0, i)

            up(0, UF, 0, 0)
            up(1, UF + 4, 0, 0)
            with sp.Fori(0, NCH - 1) as i:
                up(0, UF + 8, 1, i)
                down(0, UF + 12, 1, i)
                up(1, UF + 16, 1, i)
            down(NCH - 1, U_END - 4, 0, 0)

        @block.scalar
        def _(act):
            aa = Prog(act, S, "act")
            entry_act(act, aa)
            for u in range(NS):
                hi_unit(act, u)
            mem_act(act)
            split_x_act(act, aa)
            rw_act(act)
            shift_act(act, aa)
            guq_act(act)
            sgu_act(act, aa)
            attn_act(act, aa)
            attn_split_act(act, aa)
            wkv_start_act(act, aa)
            prepare_act(act, aa, 0)
            for n in range(2):
                wkv_act(act, aa, n)
            branch_act(act, aa)
            out_act(act, aa)
            res_act(act, aa)
            ffn_act(act, aa)
            end_act(act, aa)

        @block.vector
        def _(dve):
            vv = Prog(dve, S, "dve")
            entry_dve(dve, vv)
            for u in range(NS):
                lo_unit(dve, u)
            mem_dve(dve)
            split_x_dve(dve, vv)
            rw_dve(dve)
            shift_dve(dve, vv)
            guq_dve(dve, vv)
            sgu_dve(dve, vv)
            attn_dve(dve, vv)
            attn_split_dve(dve, vv)
            wkv_start_dve(dve, vv)
            for n in range(2):
                wkv_dve(dve, vv, n)
            branch_dve(dve, vv)
            out_dve(dve, vv)
            res_dve(dve, vv)
            ffn_dve(dve, vv)
            end_dve(dve, vv)

        @block.tensor
        def _(pe):
            entry_pe(pe)
            mem_pe(pe)
            rw_pe(pe)
            shift_pe(pe)
            guq_pe(pe)
            sgu_pe(pe)
            attn_pe(pe)
            wkv_start_pe(pe)
            for n in range(2):
                wkv_pe(pe, n)
            branch_pe(pe)
            out_pe(pe)
            res_pe(pe)
            ffn_pe(pe)
            end_pe(pe)


_INS = {'x_prompt': (TP, D), 'x_sample': (TS, D), 'mem_prompt': (MEM, D), 'state_wkv': (NB, NH, HD, HD), 'state_shift': (NB, NSH),
        'cache_mem_k': (NB, MEM, XH, W // XH), 'cache_mem_v': (NB, MEM, XH, W // XH), 'state_ffn_conv': (NB, 2, F2),
        'g_pre_mix': (D,), 'w_in': (D, NSH + 3 * W + 3 * D), 'mu_shift': (NSH,), 'w0': (W,), 'w_decay': (64, W), 'a0': (W,),
        'w_aaa': (64, W), 'w_gate': (128, W), 'k_k': (W,), 'k_a': (W,), 'r_k': (W,), 'lnx_w': (W,), 'lnx_b': (W,),
        'sgu_g': (W,), 'sgu_b': (W,), 'w_s': (8, 128, 128), 'b_s': (8, 128), 'g_mem': (D,), 'w_mem_k': (D, W),
        'w_mem_v': (D, W), 'w_branch': (3, W, D), 'w_out': (D, D), 'g_post_mix': (D,), 'g_pre_ffn': (D,), 'w_up': (D, F2),
        'conv_w': (3 * F2,), 'conv_b': (F2,), 'w_down': (DFF, D), 'g_post_ffn': (D,)}
_OUTS = [("y_p", (TP, D), (1, TP, D)), ("y_s", (TS, D), (NB, TB, D)),
         ("wkv_p", (NH, HD, HD), (1, 1, NH, HD, HD)), ("shift_p", (KSH, P), (1, 1, NSH)),
         ("mem_k", (MEM, W), (1, 1, MEM, XH, W // XH)), ("mem_v", (MEM, W), (1, 1, MEM, XH, W // XH)),
         ("conv_p", (2 * F2 // P, P), (1, 1, 2, F2)),
         ("wkv_s", (NB, NH, HD, HD), (1, NB, NH, HD, HD)), ("shift_s", (NB * KSH, P), (1, NB, NSH)),
         ("sgu_v", (TS, W), (1, NB, TB, W)), ("conv_s", (NB * 2 * F2 // P, P), (1, NB, 2, F2))]


def kernel(**inputs):
    import numpy as _np
    import concourse.bacc as _bacc
    from concourse import mybir as _mybir
    from concourse.bass_utils import run_bass_kernel_spmd as _run

    nc = _bacc.Bacc("TRN2", target_bir_lowering=False, num_devices=1)
    arrays, ins, outs = {}, {}, {}
    for name, shape in _INS.items():
        a = _np.ascontiguousarray(_np.asarray(inputs[name])).reshape(shape)
        arrays[f"in_{name}"] = a
        ins[name] = nc.dram_tensor(f"in_{name}", a.shape, _mybir.dt.from_np(a.dtype), kind="ExternalInput").ap()
    for name, shape, _ in _OUTS:
        outs[name] = nc.dram_tensor(f"out_{name}", shape, _mybir.dt.float32, kind="ExternalOutput").ap()
    ins["sgu_parts"] = nc.dram_tensor("sgu_parts", (2, P, KW * T), F32R, kind="Internal").ap()
    hybrid_step(nc, ins, outs)
    r = _run(nc, [arrays], core_ids=[0])
    return tuple(_np.asarray(r.results[0][f"out_{name}"]).reshape(shape) for name, _, shape in _OUTS)
```

```python
from contextlib import ExitStack, contextmanager

import concourse.bass as bass
from concourse import mybir

F32 = mybir.dt.float32
F32R = mybir.dt.float32r
ALU = mybir.AluOpType
ACT = mybir.ActivationFunctionType
AX_X = mybir.AxisListType.X
ds = bass.ds

P = 128
D = 2048
KD = D // P
TP, NB, TB = 256, 8, 8
TS = NB * TB
T = TP + TS
W = D // 2
KW = W // P
HD = 64
NH = W // HD
NSH = 3 * W + 64 + 64 + 128
KSH = NSH // P
CH = 64
NCK = TP // CH
NC = NCK + 1
XT_ = T + 24
MEM = 256
XH = 4
DFF = 11 * D // 4
F2 = 2 * DFF
KF = DFF // P
NCH = KF // 4
EXT = TP + 1 + NB * (TB + 1)
CEXT = TP + 2 + NB * (TB + 2)
RMS_EPS, LN_EPS, GN_EPS = 1e-6, 1e-5, 64e-5
C_DECAY = 0.6065306597126334
NS = 2

U_MEM, U_RW, U_GUQ = 0, 16, 42
U_BR = [66, 90, 114]
U_OUT, U_FFN, U_END = 138, 154, 286
T_MEM, T_RW, T_GUQ = 0, 8, 34
T_BR = [58, 90, 122]
T_OUT, T_FFN = 154, 170
PARTS_FFN = 2 * U_FFN

PARAMS = [("g_pre_mix", D), ("mu_shift", NSH), ("w0", W), ("a0", W), ("k_k", W), ("k_a", W), ("r_k", W),
          ("lnx_w", W), ("lnx_b", W), ("sgu_g", W), ("sgu_b", W), ("g_mem", D), ("g_post_mix", D),
          ("g_pre_ffn", D), ("g_post_ffn", D), ("conv_w", 3 * F2), ("conv_b", F2)]
COL = {}
_at = 0
for _name, _n in PARAMS:
    COL[_name] = _at
    _at += _n // P
NPRM = _at


class Prog:

    def __init__(self, eng, sem, own):
        self.eng, self.sem, self.own, self.n, self.k, self.i = eng, sem, own, {}, {}, 0

    def value(self, name):
        k = self.k.get(name, 0)
        n = self.n.get(name, 0)
        return n if not k else k * self.i + n

    def do(self, ins, name=None):
        name = name or self.own
        ins.then_inc(self.sem(name), 1)
        self.n[name] = self.n.get(name, 0) + 1
        self.eng.wait_ge(self.sem(name), self.value(name))

    @contextmanager
    def loop(self, start, end, per):
        with self.eng.Fori(start, end) as i:
            first = {m: self.n.get(m, 0) for m in per}
            self.k, self.i = dict(per), i
            for m in per:
                self.n[m] = first[m] - per[m] * start
            before = dict(self.n)
            yield i
            got = {m: self.n[m] - before.get(m, 0) for m in self.n if self.n[m] != before.get(m, 0)}
            assert got == {m: v for m, v in per.items() if v}, (got, per)
        self.k = {}
        for m in per:
            self.n[m] = first[m] + per[m] * (end - start)


def hybrid_step(nc, A, O):
    ctx = ExitStack()
    with ctx:
        sems = {}

        def S(name):
            if name not in sems:
                sems[name] = ctx.enter_context(nc.semaphore(name))
            return sems[name]

        def sb(name, shape, dt=F32):
            return ctx.enter_context(nc.sbuf_tensor(name, shape, dt))

        raw = [sb(f"raw{i}", [P, 2048]) for i in range(2)]
        hi = [sb(f"hi{i}", [P, 2048], F32R) for i in range(NS)]
        lo = [sb(f"lo{i}", [P, 2048], F32R) for i in range(NS)]
        ah = sb("ah", [P, KD, T], F32R)
        al_ = sb("al", [P, KD, T], F32R)
        bh = sb("bh", [P, KW, T], F32R)
        bl = sb("bl", [P, KW, T], F32R)
        mix = sb("mix", [P, KD, T])
        rwr = sb("rw", [P, KSH * EXT])
        rw = rwr[:, :].rearrange("p (k t) -> p k t", k=KSH)
        qr = sb("q", [P, KW * XT_])
        q = qr[:, :].rearrange("p (k t) -> p k t", k=KW)
        wk = sb("work", [P, 5120])
        zz = sb("small", [P, 1664])
        prm = sb("prm", [P, NPRM])
        ident = sb("ident", [P, P])
        ones = sb("ones", [P, P])
        blk = sb("head_ones", [P, P])
        m_bd = sb("m_bd", [P, CH])
        m_ad = sb("m_ad", [P, CH])
        m_bo = sb("m_bo", [P, CH])
        m_in = sb("m_in", [P, NC, CH])
        m_st = sb("m_st", [P, NC, CH])
        m_e8 = sb("m_e8", [P, NB])
        m_sc = sb("m_scan", [P, T])
        bank = [ctx.enter_context(nc.psum_tensor(f"bank{i}", [P, 512], F32)) for i in range(8)]
        mixf = mix[:, :, :].rearrange("p k t -> p (k t)")
        rep8 = zz[0:NB, 1300:1364]
        gs = zz[:, 0:2 * T].rearrange("p (c t) -> p c t", c=2)

        def mslot(n):
            return mixf[:, T * n:T * (n + 1)]

        def wslot(n):
            return wk[:, T * n:T * (n + 1)]

        def c5(ap):
            return ap.rearrange("p (c t) -> p c t", c=NC)

        def pcol(name, j, n=1):
            c = COL[name] + j
            return prm[:, c:c + n] if isinstance(c, int) else prm[:, ds(c, n)]

        block = ctx.enter_context(nc.Block())

        def parts_of(u):
            if u < U_FFN:
                return 2 * (u + 1)
            v = u - U_FFN
            if v < 8:
                return PARTS_FFN + 2 * (v + 1)
            c, j = divmod(v - 8, 12)
            base = PARTS_FFN + 16 + 32 * c
            if c == NCH - 1:
                return base + 4 * (j + 1)
            return base + (2 * (j + 1) if j < 4 else 8 + 4 * (j - 3) if j < 8 else 24 + 2 * (j - 7))

        def lin(c, k, i):
            return c if not k else k * i + c

        def load_unit(sp, src, c, k=0, i=0):
            if c >= 2 or k:
                count = lin(c - 1, k, i)
                if k:
                    count = sp.to_reg(count)
                    sp.wait_ge(S("hi_done"), 1)
                sp.wait_ge(S("hi_done"), count)
                sp.wait_ge(S("lo_done"), count)
            sp.dma_start(raw[c % 2][:, :].rearrange("p (k n) -> p k n", n=src.shape[2]), src)\
              .then_inc(S(f"raw_loaded{c % 2}"), 16)

        def pe_left(eng, c, k, i, parts_k):
            if c >= NS or k:
                eng.wait_ge(S("parts"), lin(parts_of(c - NS), parts_k, i))

        def hi_unit(act, c, k=0, i=0, pk=None):
            if c >= U_END:
                return
            act.wait_ge(S(f"raw_loaded{c % 2}"), lin(16 * (c // 2 + 1), 8 * k, i))
            pe_left(act, c, k, i, 2 * k if pk is None else pk)
            act.activation(hi[c % NS][:, :], raw[c % 2][:, :], ACT.Copy).then_inc(S("hi_done"), 1)

        def lo_unit(dve, c, k=0, i=0, pk=None):
            if c >= U_END:
                return
            dve.wait_ge(S("hi_done"), lin(c + 1, k, i))
            pe_left(dve, c, k, i, 2 * k if pk is None else pk)
            dve.tensor_tensor(lo[c % NS][:, :], raw[c % 2][:, :], hi[c % NS][:, :], ALU.subtract)\
               .then_inc(S("lo_done"), 1)

        def bank_free(pe, t, k=0, i=0):
            if t >= 4:
                pe.wait_ge(S(f"tile_out{t % 4}"), lin(t // 4, k // 4, i))

        def three(pe, out, a_hi, a_lo, b_hi, b_lo, first, last):
            pe.matmul(out, a_hi, b_hi, start=first, stop=False)
            pe.matmul(out, a_hi, b_lo, start=False, stop=False)
            return pe.matmul(out, a_lo, b_hi, start=False, stop=last)

        def pe_group_steps(pe, u, t, xh, xl, units, uk=0, tk=0, i=0, chunks=None):
            for h in range(units):
                pe.wait_ge(S("lo_done"), lin(u + h + 1, uk, i))
                s = (u + h) % NS
                for c in range(2):
                    if h == 0:
                        bank_free(pe, t + c, tk, i)
                    for k in range(8):
                        if chunks and c == 0 and k % 4 == 0:
                            pe.wait_ge(S(chunks), 2 * h + k // 4 + 1)
                        o = 256 * k + 128 * c
                        last = three(pe, bank[(t + c) % 4][:, 0:T], hi[s][:, o:o + P], lo[s][:, o:o + P],
                                     xh[:, 8 * h + k, :], xl[:, 8 * h + k, :], h + k == 0, h == units - 1 and k == 7)
                        if k == 7:
                            last.then_inc(S("parts"), 1)
                        if k % 2:
                            yield

        def pe_group(*args):
            for _ in pe_group_steps(*args):
                pass

        def tile_ready(eng, u, pk=0, i=0, part=2):
            eng.wait_ge(S("parts"), lin(parts_of(u) if part == 2 else parts_of(u) - 2 + part, pk, i))

        def kv(w, k0, n0, nk=8, nn=256):
            return w.rearrange("(kt p) n -> p kt n", p=P)[:, k0:k0 + nk, ds(n0, nn) if not isinstance(n0, int) else slice(n0, n0 + nn)]


        x_tok = [wk[:, 896:896 + D], wk[:, 896 + D:896 + 2 * D], qr[0:TS, 0:D]]
        mem_tok = [rwr[:, 0:D], rwr[:, D:2 * D]]
        mkv_stage = [rwr[:, 2 * D + 512 * j:2 * D + 512 * j + 512] for j in range(4)]
        shift_t = zz[:, 0:208]
        ss, rs = zz[:, 220:225], zz[:, 225:230]
        m_u = sb("m_u", [P, P])
        m_id = sb("m_id", [P, CH])
        half_b = sb("half_bias", [P, 2 * KW + 1])

        def pool_constants(pool, pp):
            def full(ap, v):
                pp.do(pool.memset(ap, v))

            def keep(ap, op, base, pattern, cm, fill=0.0, name=None):
                pp.do(pool.affine_select(out=ap, in_=ap, compare_op=op, fill=fill, base=base, pattern=pattern,
                                         channel_multiplier=cm), name)

            full(ident[:, :], 0.0)
            keep(ident[:, :], ALU.not_equal, 0, [[-1, P]], 1, 1.0)
            full(ones[:, :], 1.0)
            full(blk[:, :], 0.0)
            for h in range(2):
                full(blk[64 * h:64 * h + 64, 64 * h:64 * h + 64], 1.0)
            full(m_e8[:, :], 1.0)
            full(m_bd[:, :], 1.0)
            full(m_ad[:, :], 1.0)
            full(m_bo[:, :], 1.0)
            full(m_st[:, :, :], 1.0)
            full(m_in[:, :, :], 1.0)
            full(m_sc[:, :], 1.0)
            full(m_u[:, :], 1.0)
            for h in range(2):
                r = slice(64 * h, 64 * h + 64)
                keep(m_e8[r, :], ALU.is_ge, 0, [[-8, 8]], 1)
                keep(m_e8[r, :], ALU.is_ge, 7, [[8, 8]], -1)
                for m, op, c in ((m_bd, ALU.is_gt, -1), (m_ad, ALU.is_gt, 1)):
                    keep(m[r, :], op, 0, [[-c, 64]], c)
                    mv = m[r, :].rearrange("p (b t) -> p b t", b=8)
                    keep(mv, ALU.is_ge, 0, [[-8, 8], [0, 8]], 1)
                    keep(mv, ALU.is_ge, 7, [[8, 8], [0, 8]], -1)
                keep(m_bo[r, :].rearrange("p (b t) -> p b t", b=8), ALU.is_gt, 0, [[8, 8], [0, 8]], -1)
                keep(m_st[r, 0:NCK, :], ALU.is_gt, 0, [[0, NCK], [1, 64]], -1)
                keep(m_in[r, :, :], ALU.is_ge, 0, [[0, NC], [1, 64]], -1)
                mv = m_in[r, NCK, :].rearrange("p (b t) -> p b t", b=8)
                keep(mv, ALU.is_ge, 0, [[-8, 8], [0, 8]], 1)
                keep(m_st[r, NCK, :], ALU.is_gt, 0, [[1, 64]], -1)
                mv = m_st[r, NCK, :].rearrange("p (b t) -> p b t", b=8)
                keep(mv, ALU.is_ge, 7, [[8, 8], [0, 8]], -1)
                keep(mv, ALU.is_ge, 0, [[-8, 8], [0, 8]], 1)
            keep(m_u[:, :], ALU.is_ge, 0, [[1, P]], -1)
            full(m_sc[:, 0:TP].rearrange("p (c t) -> p c t", c=NCK)[:, :, 0:1], 0.0)
            full(m_sc[:, TP:T].rearrange("p (c t) -> p c t", c=NB)[:, :, 0:1], 0.0)
            full(rep8, 0.0)
            keep(rep8.rearrange("p (b t) -> p b t", b=8), ALU.not_equal, 0, [[0, 8], [-1, 8]], 1, 1.0, "consts")

        def sp_memory(sp):
            for k in range(2):
                sp.dma_start(mem_tok[k], A["mem_prompt"][128 * k:128 * k + 128, :]).then_inc(S("mem_in"), 16)

        def sp_parameters_and_x(sp):
            row = 0
            for name, n in PARAMS:
                src = A[name].rearrange("(r p) -> r p", p=P)
                k, at = n // P, 0
                while at < k:
                    m = min(k - at, P - row % P)
                    c = 128 * (row // P)
                    sp.dma_start(wk[row % P:row % P + m, c:c + 128], src[at:at + m, :]).then_inc(S("par_in"), 16)
                    at += m
                    row += m
            shift = A["state_shift"].rearrange("b (j p) -> (b j) p", p=P)
            sp.dma_start(wk[:, 640:768], shift[0:P, :]).then_inc(S("par_in"), 16)
            sp.dma_start(wk[0:80, 768:896], shift[P:208, :]).then_inc(S("par_in"), 16)
            for k in range(2):
                sp.dma_start(x_tok[k], A["x_prompt"][128 * k:128 * k + 128, :]).then_inc(S("x_in"), 16)
            sp.dma_start(x_tok[2], A["x_sample"]).then_inc(S("x_in"), 16)

        n_par, row = 2, 0
        for name, n in PARAMS:
            at, k = 0, n // P
            while at < k:
                m = min(k - at, P - row % P)
                n_par, at, row = n_par + 1, at + m, row + m

        def entry_act(act, aa):
            for k in range(2):
                act.wait_ge(S("mem_in"), 32)
                if k == 0:
                    act.wait_ge(S("rs_zero"), 1)
                aa.do(act.activation(mixf[:, 0:D], mem_tok[k], ACT.Square, accum_out=ss[:, k:k + 1]), "sum_mem" if k else None)
            act.wait_ge(S("ms_ready"), 1)
            aa.do(act.activation(rs[:, 0:2], ss[:, 0:2], ACT.Sqrt), "rms_ready")
            act.wait_ge(S("entry_ps"), 2)
            aa.do(act.activation(prm[:, 0:512], bank[4][:, :], ACT.Copy))
            aa.do(act.activation(prm[:, 512:NPRM], bank[5][:, 0:NPRM - 512], ACT.Copy))
            aa.do(act.activation(shift_t, bank[5][:, 128:336], ACT.Copy), "prm_ready")
            for k in range(8):
                act.wait_ge(S("mem_g"), k + 1)
                aa.do(act.activation(ah[:, 2 * k:2 * k + 2, 0:MEM], memg(k), ACT.Copy), "mem_hi")

        def memg(k):
            return mixf[:, 512 * (k % 2):512 * (k % 2) + 512].rearrange("p (a t) -> p a t", a=2)

        def entry_dve(dve, vv):
            vv.do(dve.memset(ss, 1.0), "rs_zero")
            dve.wait_ge(S("sum_mem"), 1)
            vv.do(dve.tensor_scalar(ss[:, 0:2], ss[:, 0:2], 1.0 / D, RMS_EPS, ALU.mult, ALU.add), "ms_ready")
            dve.wait_ge(S("rms_ready"), 1)
            vv.do(dve.reciprocal(rs[:, 0:2], rs[:, 0:2]))
            for j, tok in enumerate(mem_tok):
                vv.do(dve.tensor_scalar(tok, tok, rs[:, j:j + 1], None, ALU.mult), "tok_normed")
            dve.wait_ge(S("prm_ready"), 1)
            vv.do(dve.tensor_scalar(half_b[:, :], prm[:, COL["w0"]:COL["w0"] + 2 * KW + 1], 0.5, None, ALU.mult))
            dve.wait_ge(S("consts"), 1)
            vv.do(dve.tensor_tensor(m_id[:, :], ident[:, 0:64], ident[:, 64:128], ALU.add))
            for k in range(9):
                if k < 8:
                    dve.wait_ge(S("entry_ps"), 3 + k)
                    g = bc(pcol("g_mem", 2 * k, 2), MEM)
                    vv.do(dve.tensor_tensor(memg(k), bank[4 + k % 4][:, :].rearrange("p (a t) -> p a t", a=2), g, ALU.mult), "mem_g")
                if k:
                    n = k - 1
                    dve.wait_ge(S("mem_hi"), n + 1)
                    vv.do(dve.tensor_tensor(al_[:, 2 * n:2 * n + 2, 0:MEM], memg(n), ah[:, 2 * n:2 * n + 2, 0:MEM], ALU.subtract),
                          "mem_lo")

        def bc(ap, n):
            return ap.rearrange("p (a o) -> p a o", o=1).broadcast_to([ap.shape[0], ap.shape[1], n])

        def entry_pe(pe):
            pe.wait_ge(S("consts"), 1)
            pe.wait_ge(S("par_in"), 16 * n_par)
            for j in range(4):
                last = pe.transpose(bank[4][:, 128 * j:128 * j + 128], wk[:, 128 * j:128 * j + 128], ident[:, :])
            last.then_inc(S("entry_ps"), 1)
            m = NPRM - 512
            pe.transpose(bank[5][:, 0:m], wk[0:m, 512:640], ident[0:m, 0:m])
            pe.transpose(bank[5][:, 128:256], wk[:, 640:768], ident[:, :])
            pe.transpose(bank[5][:, 256:336], wk[0:80, 768:896], ident[0:80, 0:80]).then_inc(S("entry_ps"), 1)
            pe.wait_ge(S("tok_normed"), 2)
            for k in range(8):
                if k < 4:
                    pe.wait_ge(S("prm_ready"), 1)
                else:
                    pe.wait_ge(S("mem_g"), k - 3)
                for a in range(2):
                    for t in range(2):
                        last = pe.transpose(bank[4 + k % 4][:, 256 * a + 128 * t:256 * a + 128 * t + 128],
                                            mem_tok[t][:, 128 * (2 * k + a):128 * (2 * k + a) + 128], ident[:, :])
                last.then_inc(S("entry_ps"), 1)

        def x_transposes(pe, toks, k, out):
            for t in range(3):
                m = TS if t == 2 else P
                last = pe.transpose(out[:, 128 * t:128 * t + m], toks[t][:, 128 * k:128 * k + 128], ident[0:m, 0:m])
            return last

        def mem_pe(pe):
            pe.wait_ge(S("mem_lo"), 8)
            for u in range(16):
                g, s = u // 4, u % NS
                if 7 <= u < 15:
                    for k in (2 * (u - 7), 2 * (u - 7) + 1):
                        if k >= 4:
                            pe.wait_ge(S("x_g"), k - 3)
                        else:
                            pe.wait_ge(S("tok_normed"), 5)
                        x_transposes(pe, x_tok, k, bank[4 + k % 4]).then_inc(S("entry_ps"), 1)
                pe.wait_ge(S("lo_done"), u + 1)
                for tt in range(2):
                    t = 2 * g + tt
                    if u % 4 == 0:
                        bank_free(pe, t)
                    for k in range(4):
                        kk, r = 4 * (u % 4) + k, slice(128 * tt, 128 * tt + 128)
                        a_h, a_l = ah[:, kk, r], al_[:, kk, r]
                        w_h, w_l = hi[s][:, 512 * k:512 * k + 512], lo[s][:, 512 * k:512 * k + 512]
                        last = three(pe, bank[t % 4][:, :], a_h, a_l, w_h, w_l, kk == 0, kk == KD - 1)
                    last.then_inc(S("parts"), 1)

        def mem_act(act, aa):
            for u in range(16):
                hi_unit(act, u + 2)
                if 1 <= u <= 3:
                    j, m = u + 1, TS if u == 3 else P
                    act.wait_ge(S("x_in"), 48)
                    act.wait_ge(S("mem_lo"), 8)
                    aa.do(act.activation(mixf[0:m, 0:D], x_tok[u - 1], ACT.Square, accum_out=ss[0:m, j:j + 1]),
                          "sum_x" if u == 3 else None)
                if u % 4 == 3:
                    for t in range(2 * (u // 4), 2 * (u // 4) + 2):
                        tile_ready(act, u, part=t % 2 + 1)
                        if t == 0:
                            act.wait_ge(S("mem_lo"), 8)
                        if t >= 4:
                            act.wait_ge(S(f"mem_stored{t % 4}"), 16)
                        act.activation(mkv_stage[t % 4], bank[t % 4][:, :], ACT.Copy).then_inc(S(f"tile_out{t % 4}"), 1)
                if u == 3:
                    act.wait_ge(S("ms_ready"), 2)
                    aa.do(act.activation(rs[:, 2:5], ss[:, 2:5], ACT.Sqrt), "rms_ready")

        def mem_dve(dve, vv):
            def norm_x(j):
                m = TS if j == 2 else P
                vv.do(dve.tensor_scalar(x_tok[j], x_tok[j], rs[0:m, 2 + j:3 + j], None, ALU.mult), "tok_normed")

            for u in range(16):
                lo_unit(dve, u + 2)
                if u == 3:
                    dve.wait_ge(S("sum_x"), 1)
                    vv.do(dve.tensor_scalar(ss[:, 2:5], ss[:, 2:5], 1.0 / D, RMS_EPS, ALU.mult, ALU.add), "ms_ready")
                elif u == 4:
                    dve.wait_ge(S("rms_ready"), 2)
                    vv.do(dve.reciprocal(rs[:, 2:5], rs[:, 2:5]))
                    norm_x(0)
                elif u == 5:
                    norm_x(1)
                    norm_x(2)
                elif 7 <= u < 15:
                    for k in (2 * (u - 7), 2 * (u - 7) + 1):
                        dve.wait_ge(S("entry_ps"), 11 + k)
                        vv.do(dve.tensor_scalar(mix[:, k, :], bank[4 + k % 4][:, 0:T], pcol("g_pre_mix", k), None, ALU.mult), "x_g")

        def mem_pool(pool):
            for t in range(8):
                pool.wait_ge(S(f"tile_out{t % 4}"), t // 4 + 1)
                g, tt = t // 2, t % 2
                dst = O["mem_k"] if g < 2 else O["mem_v"]
                pool.dma_start(dst[128 * tt:128 * tt + 128, 512 * (g % 2):512 * (g % 2) + 512], mkv_stage[t % 4])\
                    .then_inc(S(f"mem_stored{t % 4}"), 16)

        def split_x_act(act, aa):
            act.wait_ge(S("x_g"), KD)
            tile_ready(act, 15)
            for c in range(4):
                aa.do(act.activation(ah[:, 4 * c:4 * c + 4, :], mix[:, 4 * c:4 * c + 4, :], ACT.Copy), "xn_hi")
            for t in range(4):
                act.wait_ge(S(f"mem_stored{t}"), 32)

        def split_x_dve(dve, vv):
            tile_ready(dve, 15)
            for c in range(4):
                dve.wait_ge(S("xn_hi"), c + 1)
                vv.do(dve.tensor_tensor(al_[:, 4 * c:4 * c + 4, :], mix[:, 4 * c:4 * c + 4, :], ah[:, 4 * c:4 * c + 4, :],
                                        ALU.subtract), "xn_lo")
            for t in range(4):
                dve.wait_ge(S(f"mem_stored{t}"), 32)
            vv.do(dve.memset(rw[:, :, 0:1], 0.0))
            vv.do(dve.tensor_copy(smp(rw, KSH)[:, :, :, 0], shift_t.rearrange("p (b k) -> p k b", b=NB)), "shift_set")

        def smp(t, k):
            return t[:, :, TP + 1:EXT].rearrange("p k (b t) -> p k b t", b=NB)

        def rw_pe(pe):
            pe_group(pe, U_RW, T_RW, ah, al_, 2, 0, 0, 0, "xn_lo")
            with pe.Fori(0, 6) as i:
                for g in range(2):
                    pe_group(pe, U_RW + 2 + 2 * g, T_RW + 2 + 2 * g, ah, al_, 2, 4, 4, i)

        def rw_out(act, k, t, tk=0, i=0):
            kk = ds(k, 1) if tk else slice(k, k + 1)
            b = t % 4
            act.activation(rw[:, kk, 1:1 + TP].rearrange("p k t -> p (k t)"), bank[b][:, 0:TP], ACT.Copy)
            act.activation(rw[:, kk, TP + 1:EXT].rearrange("p k (b t) -> p (k b) t", b=NB)[:, :, 1:1 + TB],
                           bank[b][:, TP:T].rearrange("p (b t) -> p b t", b=NB), ACT.Copy).then_inc(S(f"tile_out{b}"), 1)

        def rw_act(act):
            def group(u, t, k, uk=0, i=0):
                for h in range(2):
                    hi_unit(act, u + 2 + h, uk, i)
                for c in range(2):
                    tile_ready(act, u + 1, 2 * uk, i, c + 1)
                    rw_out(act, k + c, t + c, uk, i)
            act.wait_ge(S("shift_set"), 1)
            group(U_RW, T_RW, 0)
            with act.Fori(0, 6) as i:
                for g in range(2):
                    group(U_RW + 2 + 2 * g, T_RW + 2 + 2 * g, 4 * i + 2 + 2 * g, 4, i)

        def rw_dve(dve):
            for h in range(2):
                lo_unit(dve, U_RW + 2 + h)
            with dve.Fori(0, 6) as i:
                for h in range(4):
                    lo_unit(dve, U_RW + 4 + h, 4, i)

        wa_in, sg = qr[:, 0:T], qr[:, T:2 * T]
        s0t = qr[:, 640:1152].rearrange("p (b v) -> p b v", b=NB)
        alm = qr[:, 1152:1664].rearrange("p (b t) -> p b t", b=NB)
        st_pp = [qr[:, 1664:1728], qr[:, 1728:1792]]
        xs_, sa_ = qr[:, 1792:1856], qr[:, 1856:1920]
        be_t, ka_t, v_, alp, be, ka, rh, t_r, t_ad, t_bd, t_bo, t_rt, t_bk, t_cb, t_ck, bon = [wslot(n) for n in range(16)]
        v_t, t_a2, t_b2 = v_, be, ka
        sam = wk[:, 8 * T:8 * T + 512].rearrange("p (b v) -> p b v", b=NB)
        vtm = wk[:, 8 * T + 512:8 * T + 1024].rearrange("p (b v) -> p b v", b=NB)
        y_, ym, ysq = t_r, t_cb, t_ck
        cum, ldx, pt, tmp = be, ka, t_bk, t_bd
        rk = t_bo
        kkv, av = rw[:, 24, 0:T], rw[:, 25, 0:T]
        sq = qr[:, 2316:2636]
        wlr = qr[:, 1920:2176]
        pend_p, pend_s = qr[:, 2176:2180], qr[:, 2180:2188]
        sp_out = qr[0:64, 2188:2316]
        s_out = zz[0:64, 640:1664]
        s0raw = zz[64:128, 640:1664]
        last_t = qr[:, 0:234]
        sh_stage = qr[:, 256:512]

        RING = (4, 5, 7)
        PR = {}
        for _n in ["s0t", "bonus", "A", "B", "Bk", "Cb", "Ck", "beT", "kaT", "vT", "A2", "B2",
                   "R1", "RT1", "A4", "B4", "R2", "RT2", "Q", "QT", "Q2", "QT2", "QT4", "W1", "W2", "W3", "z", "za",
                   "X0", "SA0", "S0", "ssq"] + \
                [f"{m}{c}" for c in range(1, NCK) for m in ("X", "SA", "S")] + \
                ["X4", "SA4", "S4", "mean", "tr0", "tr1", "trp", "var", "g"]:
            PR[_n] = len(PR)
        NPR = len(PR)
        OUT = {}
        for _n in PR:
            if _n not in ("z", "za", "g"):
                OUT[_n] = len(OUT)
        N_OUT = len(OUT)
        PS0, OUT0 = 3, 2

        def pbank(name):
            return bank[6] if name == "g" else bank[RING[PR[name] % 3]]

        def shift_pool(pool):
            pool.wait_ge(S("shift_stage"), 2)
            pool.dma_start(O["shift_p"], sh_stage[0:KSH, 0:128]).then_inc(S("state_stored"), 16)
            pool.dma_start(O["shift_s"][0:102, :], sh_stage[KSH:128, 0:128]).then_inc(S("state_stored"), 16)
            pool.dma_start(O["shift_s"][102:208, :], sh_stage[0:106, 128:256]).then_inc(S("state_stored"), 16)

        shift_d = zz[:, 640:640 + EXT - 1]

        def wkv_pool(pool):
            def load(j):
                n = slice(128 * j, 128 * j + 128)
                pool.dma_start(wlr[0:64, 0:128], A["w_decay"][:, n]).then_inc(S("pair_in"), 16)
                pool.dma_start(wlr[64:128, 0:128], A["w_aaa"][:, n]).then_inc(S("pair_in"), 16)
                for h in range(2):
                    dst = s0raw.rearrange("v (b h k) -> v b h k", b=NB, h=2)[:, :, h, :]
                    pool.dma_start(dst, A["state_wkv"][:, 2 * j + h].rearrange("b v k -> v b k")).then_inc(S("pair_in"), 16)

            def load_gate(j):
                pool.dma_start(wlr[:, 128:256], A["w_gate"][:, 128 * j:128 * j + 128]).then_inc(S("gate_in"), 16)

            pool.wait_ge(S("at_v"), 3 * NB + 16)
            pool.wait_ge(S("bl_ready"), 2)
            load(0)
            load_gate(0)
            for j in range(KW):
                pool.wait_ge(S("wkv_ps"), PS0 + NPR * j + PR["s0t"] + 1)
                load(min(j + 1, KW - 1))
                pool.wait_ge(S("ring_out"), OUT0 + N_OUT * j + OUT["trp"] + 1)
                for h in range(2):
                    src = s_out.rearrange("v (b h k) -> v b h k", b=NB, h=2)[:, :, h, :]
                    pool.dma_start(O["wkv_s"][:, 2 * j + h].rearrange("b v k -> v b k"), src).then_inc(S("state_stored"), 16)
                pool.dma_start(O["wkv_p"][2 * j:2 * j + 2].rearrange("h v k -> v h k"),
                               sp_out.rearrange("v (h k) -> v h k", h=2)).then_inc(S("state_stored"), 16)
                if j + 1 < KW:
                    pool.wait_ge(S("wkv_ps"), PS0 + NPR * (j + 1))
                    load_gate(j + 1)
                if j == 3:
                    pool.wait_ge(S("parts"), parts_of(U_BR[1] - 1))
                    for n, dst in enumerate((bh, bl)):
                        pool.dma_start(dst[:, :, :].rearrange("p k t -> p (k t)"), A["sgu_parts"][n]).then_inc(S("sgu_back"), 16)

        def row_(tile):
            return rw[:, slice(tile, tile + 1) if isinstance(tile, int) else ds(tile, 1), 0:T].rearrange("p k t -> p (k t)")

        def mix_shift(dve, vv, dst, tile, mu):
            d = shift_d
            tt = slice(tile, tile + 1) if isinstance(tile, int) else ds(tile, 1)
            row = rw[:, tt, :].rearrange("p k t -> p (k t)")
            vv.do(dve.tensor_tensor(d, row[:, 0:EXT - 1], row[:, 1:EXT], ALU.subtract))
            vv.do(dve.scalar_tensor_tensor(out=dst[:, 0:TP], in0=d[:, 0:TP], scalar=mu, in1=row[:, 1:1 + TP],
                                           op0=ALU.mult, op1=ALU.add))
            ds8 = zz[:, 640 + TP + 1:640 + EXT].rearrange("p (b t) -> p b t", b=NB)[:, :, 0:TB]
            vv.do(dve.scalar_tensor_tensor(out=dst[:, TP:T].rearrange("p (b t) -> p b t", b=NB), in0=ds8, scalar=mu,
                                           in1=row[:, TP + 1:EXT].rearrange("p (b t) -> p b t", b=NB)[:, :, 1:],
                                           op0=ALU.mult, op1=ALU.add))

        def shift_dve(dve, vv):
            for t in range(4):
                dve.wait_ge(S(f"tile_out{t}"), 8 if t >= 2 else 9)
            vv.do(dve.tensor_copy(last_t[:, 0:KSH], rw[:, :, TP]))
            vv.do(dve.tensor_copy(last_t[:, KSH:].rearrange("p (b k) -> p k b", b=NB), smp(rw, KSH)[:, :, :, TB]), "last_rows")

        def prepare_kk(dve, vv, j):
            vv.do(dve.tensor_scalar(kkv, row_(j + 8), pcol("k_k", j), None, ALU.mult))
            vv.do(dve.tensor_tensor(sq, kkv, kkv, ALU.mult), "kk_sq")

        def prepare_logs(dve, vv, j):
            dve.wait_ge(S("low_out"), 2 * j + 2)
            vv.do(dve.tensor_scalar(ldx, ldx, -0.5 * C_DECAY, -0.5 * C_DECAY, ALU.mult, ALU.add))
            vv.do(dve.tensor_tensor_scan(cum, m_sc[:, :], ldx, 0.0, ALU.mult, ALU.add))
            vv.do(dve.tensor_tensor(ldx, cum, ldx, ALU.subtract), "logs")
            vv.do(dve.tensor_scalar(av, av, 0.5, 0.5, ALU.mult, ALU.add))

        def prepare_k(dve, vv, j):
            vv.do(dve.tensor_scalar(tmp, av, -1.0, pcol("k_a", j), ALU.add, ALU.mult))
            vv.do(dve.scalar_tensor_tensor(out=row_(j + 8), in0=tmp, scalar=1.0, in1=row_(j + 8), op0=ALU.add, op1=ALU.mult))

        def prepare_norm(dve, vv, j):
            dve.wait_ge(S("kk_root"), j + 1)
            vv.do(dve.reciprocal(sq, sq))
            vv.do(dve.tensor_tensor(kkv, kkv, sq, ALU.mult))
            vv.do(dve.tensor_tensor(av, kkv, av, ALU.mult))

        def prepare_al(dve, vv, j):
            dve.wait_ge(S("exps"), 3 * (j + 1))
            vv.do(dve.scalar_tensor_tensor(out=alp, in0=kkv, scalar=-1.0, in1=ldx, op0=ALU.mult, op1=ALU.mult))
            vv.do(dve.tensor_copy(alm_own, alp[:, TP:T].rearrange("p (b t) -> p b t", b=NB)))

        def prepare_ops(dve, vv, j):
            vv.do(dve.tensor_tensor(ka, row_(j + 8), cum, ALU.mult))
            vv.do(dve.tensor_tensor(be, av, cum, ALU.mult))
            vv.do(dve.tensor_tensor(rh, row_(j), pt, ALU.mult), "ops_ready")

        def prepare_rest(dve, vv, j):
            vv.do(dve.scalar_tensor_tensor(out=rk, in0=row_(j), scalar=pcol("r_k", j), in1=row_(j + 8), op0=ALU.mult,
                                           op1=ALU.mult), "rk_ready")
            vv.do(dve.tensor_copy(pend_p, pt[:, 0:TP].rearrange("p (c t) -> p c t", c=NCK)[:, :, CH - 1]))
            vv.do(dve.tensor_copy(pend_s, pt[:, TP:T].rearrange("p (b t) -> p b t", b=NB)[:, :, TB - 1]))

        alm_own = qr[:, 1152:1152 + 72 * NB].rearrange("p (b t) -> p b t", b=NB)[:, :, 0:TB]

        def wkv_start_dve(dve, vv):
            vv.do(dve.memset(alm, 0.0), "low_in")
            vv.do(dve.memset(xs_, 0.0), "ring_out")
            vv.do(dve.memset(sa_, 0.0), "gated_out")
            dve.wait_ge(S("sig_g"), 3)
            vv.do(dve.tensor_scalar(sg, sg, 0.5, 0.5, ALU.mult, ALU.add), "low_ready")
            prepare_kk(dve, vv, 0)
            dve.wait_ge(S("wkv_ps"), 3)
            vv.do(dve.tensor_scalar(sq, pbank("ssq")[:, 0:T], 1e-24, None, ALU.max), "ring_out")
            prepare_logs(dve, vv, 0)
            prepare_k(dve, vv, 0)
            prepare_norm(dve, vv, 0)
            prepare_al(dve, vv, 0)
            prepare_ops(dve, vv, 0)
            prepare_rest(dve, vv, 0)
            for c in range(2):
                vv.do(dve.memset(gs[:, c, :], 0.0), "gate_free")

        STEPS = {PR["s0t"]: 1, PR["bonus"]: 2, PR["A"]: 1, PR["B"]: 7, PR["Bk"]: 1, PR["Cb"]: 1, PR["beT"]: 1,
                 PR["kaT"]: 1, PR["R1"]: 1, PR["RT1"]: 1, PR["A4"]: 1, PR["B4"]: 3, PR["Q"]: 1, PR["Q2"]: 1,
                 PR["QT2"]: 2, PR["QT4"]: 3, PR["W1"]: 2, PR["W2"]: 1, PR["S0"]: 1, PR["X1"]: 1, PR["X2"]: 1,
                 PR["SA2"]: 2, PR["SA3"]: 1, PR["S3"]: 1, PR["S4"]: 2, PR["mean"]: 2, PR["tr1"]: 2, PR["var"]: 2,
                 PR["g"]: 2}
        assert sum(STEPS.values()) == 48
        UNIT_END = [next(p for p in range(NPR) if sum(STEPS.get(x, 0) for x in range(p + 1)) >= 8 * (j + 1)) for j in range(6)]

        def wkv_dve(dve, vv, n):
            u = U_BR[n]
            with vv.loop(4 * n, 4 * n + 4, PER_V) as i:
                units = [0]

                def stream(p):
                    while units[0] < 6 and UNIT_END[units[0]] < p:
                        j = units[0]
                        lo_unit(dve, u - 24 * n + j + 2, 6, i)
                        if j % 3 == 2:
                            for c in range(2):
                                add_branch(dve, vv, n, j // 3, c, i)
                        units[0] += 1

                def ps(name, units_first=True):
                    if units_first:
                        stream(PR[name])
                    dve.wait_ge(S("wkv_ps"), PS0 + NPR * i + PR[name] + 1)

                def tt(o, a, b, op, sem=None):
                    vv.do(dve.tensor_tensor(o, a, b, op), sem)

                def masked(o, name, m, sem="ring_out"):
                    ps(name)
                    m = m[:, :, :] if len(m.shape) == 3 else bmid(m[:, :], NC)
                    tt(c5(o), c5(pbank(name)[:, 0:T]), m, ALU.mult, sem)

                def plain(o, name, n=T):
                    ps(name)
                    vv.do(dve.tensor_copy(o[:, 0:n], pbank(name)[:, 0:n]), "ring_out")

                def plus(o, name, n=T):
                    ps(name)
                    tt(o[:, 0:n], o[:, 0:n], pbank(name)[:, 0:n], ALU.add, "ring_out")

                ps("s0t")
                vv.do(dve.tensor_copy(qr[:, 640:1152], pbank("s0t")[:, :]), "ring_out")
                ps("bonus")
                tt(bon, pbank("bonus")[:, 0:T], row_(i + 16), ALU.mult, "ring_out")
                masked(t_ad, "A", m_ad)
                masked(t_bd, "B", m_bd, None)
                tt(c5(t_bo)[:, 0:NCK], c5(pbank("B")[:, 0:T])[:, 0:NCK], bmid(m_bo[:, :], NCK), ALU.mult, "ring_out")
                masked(t_bk, "Bk", m_st)
                masked(t_cb, "Cb", m_in)
                masked(t_ck, "Ck", m_in)
                plain(be_t, "beT")
                plain(ka_t, "kaT")
                plain(v_t, "vT")
                tt(c5(t_r), c5(t_bd), bmid(m_id[:, :], NC), ALU.add)
                tt(c5(t_rt), c5(t_ad), bmid(m_id[:, :], NC), ALU.add, "r_ready")
                plain(t_a2, "A2")
                plain(t_b2, "B2")
                plus(t_r, "R1")
                plus(t_rt, "RT1")
                plain(t_ad, "A4")
                plain(t_bd, "B4")
                plus(t_r, "R2")
                plus(t_rt, "RT2")
                plain(t_a2, "Q", TP)
                plain(t_b2, "QT", TP)
                plain(t_ad, "Q2", TP)
                plain(t_bd, "QT2", TP)
                plain(t_rt, "QT4", TP)
                plus(t_r, "W1", TP)
                prepare_kk(dve, vv, i + 1)
                plus(t_r, "W2", TP)
                plus(t_r, "W3", TP)
                for c in range(NCK):
                    plain(xs_, f"X{c}", 64)
                    plain(sa_, f"SA{c}", 64)
                    ps(f"S{c}")
                    pend = pend_p[:, c:c + 1]
                    src = pbank(f"S{c}")[:, 0:64]
                    if c:
                        tt(st_pp[c % 2], src, st_pp[(c + 1) % 2], ALU.add)
                        src = st_pp[c % 2]
                    vv.do(dve.tensor_scalar(st_pp[c % 2], src, pend, None, ALU.mult), "ring_out")
                    if c == 0:
                        ps("ssq")
                        vv.do(dve.tensor_scalar(sq, pbank("ssq")[:, 0:T], 1e-24, None, ALU.max), "ring_out")
                    elif c == 1:
                        prepare_logs(dve, vv, i + 1)
                    elif c == 2:
                        prepare_k(dve, vv, i + 1)
                plain(xs_, "X4", 64)
                ps("SA4")
                vv.do(dve.tensor_copy(sa_, pbank("SA4")[:, 0:64]), "ring_out")
                tt(sam, bmid(sa_, NB), bc(m_e8[:, :], HD), ALU.mult)
                tt(vtm, bmid(v_t[:, TP:T], NB), bc(m_e8[:, :], HD), ALU.mult, "sam_ready")
                prepare_norm(dve, vv, i + 1)
                ps("S4")
                tt(sam, pbank("S4")[:, :].rearrange("p (b v) -> p b v", b=NB), s0t, ALU.add)
                tt(sam, sam, bc(pend_s, HD), ALU.mult, "ring_out")
                dve.wait_ge(S("y_ps"), i + 1)
                vv.do(dve.tensor_copy(y_, bank[6][:, 0:T]), "y_out")
                prepare_al(dve, vv, i + 1)
                ps("mean", False)
                vv.do(dve.scalar_tensor_tensor(out=ym, in0=pbank("mean")[:, 0:T], scalar=-1.0 / HD, in1=y_,
                                               op0=ALU.mult, op1=ALU.add), "ring_out")
                tt(ysq, ym, ym, ALU.mult, "ym_sq")
                dve.wait_ge(S("state_stored"), 48 * (i + 1))
                for m in range(2):
                    ps(f"tr{m}", False)
                    vv.do(dve.tensor_copy(s_out[:, 512 * m:512 * m + 512], pbank(f"tr{m}")[0:64, :]), "ring_out")
                ps("trp", False)
                vv.do(dve.tensor_copy(sp_out, pbank("trp")[0:64, 0:128]), "ring_out")
                prepare_ops(dve, vv, i + 1)
                ps("var", False)
                vv.do(dve.tensor_scalar(ysq, pbank("var")[:, 0:T], 1.0 / HD, GN_EPS, ALU.mult, ALU.add), "ring_out")
                stream(PR["g"])
                prepare_rest(dve, vv, i + 1)
                dve.wait_ge(S("gn_sqrt"), i + 1)
                vv.do(dve.reciprocal(ysq, ysq))
                tt(ym, ym, ysq, ALU.mult)
                vv.do(dve.tensor_scalar(ym, ym, pcol("lnx_w", i), pcol("lnx_b", i), ALU.mult, ALU.add))
                tt(ym, ym, bon, ALU.add)
                ps("g")
                tt(row_(i), ym, bank[6][:, 0:T], ALU.mult, "gated_out")
                stream(NPR)

        def bmid(ap, n):
            return ap.rearrange("p (o t) -> p o t", o=1).broadcast_to([ap.shape[0], n, ap.shape[1]])

        PER_V = {"dve": 26, "kk_sq": 1, "logs": 1, "ring_out": N_OUT, "rk_ready": 1, "ops_ready": 1, "r_ready": 1,
                 "sam_ready": 1, "y_out": 1, "ym_sq": 1, "gated_out": 1, "gate_free": 4}

        def shift_act(act, aa):
            for n in range(2):
                act.wait_ge(S("last_ps"), n + 1)
                m = 128 if n == 0 else 106
                aa.do(act.activation(sh_stage[0:m, 128 * n:128 * n + 128], bank[4 + n][0:m, 0:128], ACT.Copy), "shift_stage")

        def wkv_start_act(act, aa):
            act.wait_ge(S("low_in"), 1)
            aa.do(act.activation(wa_in[0:64, :], rw[0:64, 24, 0:T], ACT.Tanh), "sig_g")
            aa.do(act.activation(wa_in[64:128, :], rw[64:128, 24, 0:T], ACT.Copy), "sig_g")
            aa.do(act.activation(sg, rw[:, 25, 0:T], ACT.Tanh, scale=0.5), "sig_g")

        def prepare_act(act, aa, j, ps=None):
            if ps:
                ps("z")
            else:
                act.wait_ge(S("wkv_ps"), 1)
            aa.do(act.activation(ldx, pbank("z")[:, 0:T], ACT.Tanh, scale=0.5,
                                 bias=half_b[:, ds(j, 1) if ps else slice(0, 1)]), "low_out")
            if ps:
                ps("za")
            else:
                act.wait_ge(S("wkv_ps"), 2)
            aa.do(act.activation(av, pbank("za")[:, 0:T], ACT.Tanh, scale=0.5,
                                 bias=half_b[:, ds(j + 8, 1) if ps else slice(8, 9)]), "low_out")
            if ps:
                ps("X4")
            act.wait_ge(S("logs"), j + 1)
            aa.do(act.activation(pt, cum, ACT.Exp), "exps")
            aa.do(act.activation(cum, cum, ACT.Exp, scale=-1.0), "exps")
            aa.do(act.activation(ldx, ldx, ACT.Exp), "exps")
            if ps:
                act.wait_ge(S("ring_out"), OUT0 + N_OUT * (j - 1) + OUT["ssq"] + 1)
            else:
                act.wait_ge(S("ring_out"), 2)
            aa.do(act.activation(sq, sq, ACT.Sqrt), "kk_root")
            if ps:
                ps("mean")
            act.wait_ge(S("ops_ready"), j + 1)
            aa.do(act.activation(v_, row_(j + 16), ACT.Copy), "v_copied")

        def wkv_act(act, aa, n):
            with aa.loop(4 * n, 4 * n + 4, {"low_out": 2, "exps": 3, "kk_root": 1, "v_copied": 1, "gn_sqrt": 1}) as i:
                units = [0]

                def stream(p):
                    while units[0] < 6 and UNIT_END[units[0]] < p:
                        branch_act_unit(act, units[0], i)
                        units[0] += 1

                def ps(name):
                    stream(PR[name])
                    act.wait_ge(S("wkv_ps"), PS0 + NPR * i + PR[name] + 1)

                prepare_act(act, aa, i + 1, ps)
                ps("var")
                act.wait_ge(S("ring_out"), OUT0 + N_OUT * (i + 1))
                aa.do(act.activation(ysq, ysq, ACT.Sqrt), "gn_sqrt")
                stream(NPR)

        def shift_pe(pe):
            pe.wait_ge(S("last_rows"), 1)
            pe.transpose(bank[4][:, 0:128], last_t[:, 0:128], ident[:, :]).then_inc(S("last_ps"), 1)
            pe.transpose(bank[5][0:106, 0:128], last_t[:, 128:234], ident[:, :]).then_inc(S("last_ps"), 1)
            pe.wait_ge(S("shift_stage"), 2)

        def wkv_start_pe(pe):
            pe.wait_ge(S("low_ready"), 1)
            pe.wait_ge(S("pair_in"), 64)
            for h, name in enumerate(("z", "za")):
                r = slice(64 * h, 64 * h + 64)
                pe.matmul(pbank(name)[:, 0:T], wlr[r, 0:128], wa_in[r, :], start=True, stop=True).then_inc(S("wkv_ps"), 1)
            pe.wait_ge(S("kk_sq"), 1)
            pe.matmul(pbank("ssq")[:, 0:T], blk[:, :], sq, start=True, stop=True).then_inc(S("wkv_ps"), 1)
            pe.wait_ge(S("low_out"), 2)

        def wkv_pe(pe, n):
            u, t = U_BR[n], T_BR[n]
            with pe.Fori(4 * n, 4 * n + 4) as i:
                done = [0]

                def stream():
                    for g in range(2):
                        cu, ct = u - 24 * n + 3 * g, t - 32 * n + 4 * g
                        yield from pe_group_steps(pe, cu, ct, ah, al_, 2, 6, 8, i)
                        if n == 0:
                            pe.wait_ge(S("bl_ready"), 2)
                        else:
                            pe.wait_ge(S("sgu_back"), 32)
                        yield from pe_group_steps(pe, cu + 2, ct + 2, bh, bl, 1, 6, 8, i)

                steps = stream()

                def wait(name, value):
                    value = pe.to_reg(value)
                    pe.wait_ge(S("low_ready"), 1)
                    pe.wait_ge(S(name), value)

                def begin(name, *needs):
                    p = PR[name]
                    assert p == done[0], name
                    for _ in range(STEPS.get(p, 0)):
                        next(steps, None)
                    if p < 3:
                        wait("ring_out", OUT0 + N_OUT * i)
                    need = [OUT[m] for m in needs]
                    if p >= 3 and name != "g":
                        before = list(PR)[p - 3]
                        if before in OUT:
                            need.append(OUT[before])
                        else:
                            wait("low_out", 2 * i + 3 + (before == "za"))
                    if need:
                        wait("ring_out", OUT0 + N_OUT * i + 1 + max(need))
                    return pbank(name)

                def end(ins):
                    ins.then_inc(S("wkv_ps"), 1)
                    done[0] += 1

                def heads(out, pairs, start=True, stop=True, **kw):
                    for h in range(2):
                        r = slice(64 * h, 64 * h + 64)
                        for n, (a, b) in enumerate(pairs):
                            last = pe.matmul(out[r, :], a[r, :], b[r, :], start=start and n == 0,
                                             stop=stop and n == len(pairs) - 1, **kw)
                    return last

                def each(name, a, b, needs=(), n=NC):
                    o = begin(name, *needs)
                    for c in range(n):
                        s = slice(64 * c, 64 * c + 64)
                        last = heads(o[:, s], [(a[:, s], b[:, s])])
                    end(last)

                o = begin("s0t")
                for b in range(NB):
                    last = pe.transpose(o[:, 64 * b:64 * b + 64], s0raw[:, 128 * b:128 * b + 128], ident[64:128, 64:128])
                end(last)
                o = begin("bonus")
                wait("rk_ready", i + 1)
                end(pe.matmul(o[:, 0:T], blk[:, :], rk, start=True, stop=True))
                o = begin("A")
                wait("ops_ready", i + 1)
                for c in range(NC):
                    s = slice(64 * c, 64 * c + 64)
                    last = heads(o[:, s], [(alp[:, s], be[:, s])])
                end(last)
                each("B", be, alp)
                each("Bk", ka, alp)
                each("Cb", be, rh)
                each("Ck", ka, rh)
                for name, src in (("beT", be), ("kaT", ka), ("vT", v_)):
                    o = begin(name)
                    if name == "vT":
                        wait("v_copied", i + 1)
                    for c in range(NC):
                        s = slice(64 * c, 64 * c + 64)
                        last = heads(o[:, s], [(src[:, s], m_id[:, :])])
                    end(last)
                each("A2", t_bd, t_ad, ("B",))
                each("B2", t_ad, t_bd)
                wait("r_ready", i + 1)
                each("R1", t_a2, t_r, ("A2",))
                each("RT1", t_b2, t_rt, ("B2",))
                each("A4", t_b2, t_a2)
                each("B4", t_a2, t_b2)
                each("R2", t_ad, t_r, ("A4", "R1"))
                each("RT2", t_bd, t_rt, ("B4", "RT1"))
                each("Q", t_rt, t_bo, ("RT2",), NCK)
                each("QT", t_bo, t_rt, (), NCK)
                each("Q2", t_b2, t_a2, ("QT",), NCK)
                each("QT2", t_a2, t_b2, (), NCK)
                each("QT4", t_ad, t_bd, ("QT2",), NCK)
                each("W1", t_rt, t_r, ("QT4", "R2"), NCK)
                each("W2", t_bd, t_r, ("W1",), NCK)
                each("W3", t_b2, t_r, ("W2",), NCK)
                o = begin("z")
                wait("pair_in", 64 * i + 128)
                end(pe.matmul(o[:, 0:T], wlr[0:64, 0:128], wa_in[0:64, :], start=True, stop=True))
                o = begin("za")
                end(pe.matmul(o[:, 0:T], wlr[64:128, 0:128], wa_in[64:128, :], start=True, stop=True))
                for c in range(NC):
                    s = slice(64 * c, 64 * c + 64)
                    prev = st_pp[(c + 1) % 2]
                    first = c == 0
                    o = begin(f"X{c}", f"S{c - 1}" if 0 < c < NCK else "W3")
                    if c < NCK:
                        end(heads(o[:, 0:64], [(t_bk[:, s], v_t[:, s])] + ([] if first else [(alp[:, s], prev)])))
                    else:
                        end(heads(o[:, 0:64], [(t_bk[:, s], v_t[:, s])] + [(alm[:, b, :], s0t[:, b, :]) for b in range(NB)]))
                    o = begin(f"SA{c}", f"X{c}")
                    end(heads(o[:, 0:64], [(t_r[:, s], xs_)]))
                    o = begin(f"S{c}", f"SA{c}")
                    if c < NCK:
                        end(heads(o[:, 0:64], [(be_t[:, s], sa_), (ka_t[:, s], v_t[:, s])]))
                        if first:
                            wait("gated_out", i + 1)
                        heads(bank[6][:, s], [(sa_, t_cb[:, s]), (v_t[:, s], t_ck[:, s])] + ([] if first else [(prev, rh[:, s])]))
                    else:
                        wait("sam_ready", i + 1)
                        end(heads(o[:, :], [(be_t[:, s], sam.rearrange("p b v -> p (b v)")),
                                            (ka_t[:, s], vtm.rearrange("p b v -> p (b v)"))]))
                        heads(bank[6][:, s], [(sa_, t_cb[:, s]), (v_t[:, s], t_ck[:, s])], stop=False, skip_group_check=True)
                        for b in range(NB):
                            w = slice(TP + 8 * b, TP + 8 * b + 8)
                            last = heads(bank[6][:, w], [(s0t[:, b, :], rh[:, w])], start=False, stop=b == NB - 1,
                                         skip_group_check=True)
                        last.then_inc(S("y_ps"), 1)
                    if first:
                        o = begin("ssq")
                        wait("kk_sq", i + 2)
                        end(pe.matmul(o[:, 0:T], blk[:, :], sq, start=True, stop=True))
                o = begin("mean")
                wait("y_out", i + 1)
                end(pe.matmul(o[:, 0:T], blk[:, :], y_, start=True, stop=True))
                for m in range(2):
                    o = begin(f"tr{m}", "S4")
                    for b in range(4):
                        last = pe.transpose(o[0:64, 128 * b:128 * b + 128], sam[:, 4 * m + b, :], ident[:, :])
                    end(last)
                o = begin("trp", "S3")
                end(pe.transpose(o[0:64, 0:128], st_pp[1], ident[:, :]))
                o = begin("var")
                wait("ym_sq", i + 1)
                end(pe.matmul(o[:, 0:T], blk[:, :], ysq, start=True, stop=True))
                o = begin("g")
                wait("gate_in", 16 * i + 16)
                end(pe.matmul(o[:, 0:T], wlr[:, 128:256], sg, start=True, stop=True))
                assert next(steps, 0) == 0

        gu = wk[:, 0:2560].rearrange("p (k t) -> p k t", k=KW)
        gv = wk[:, 2560:5120].rearrange("p (k t) -> p k t", k=KW)

        def guq_pe(pe):
            with pe.Fori(0, 6) as i:
                for g in range(2):
                    pe_group(pe, U_GUQ + 2 * g, T_GUQ + 2 * g, ah, al_, 2, 4, 4, i)

        def guq_act(act):
            act.wait_ge(S("state_stored"), 48)
            for n, dst in enumerate((gu, gv, q)):
                with act.Fori(2 * n, 2 * n + 2) as i:
                    for g in range(2):
                        for h in range(2):
                            hi_unit(act, U_GUQ + 2 * g + 2 + h, 4, i)
                        for c in range(2):
                            t = T_GUQ + 2 * g + c
                            tile_ready(act, U_GUQ + 2 * g + 1, 8, i, c + 1)
                            o = dst[:, ds(4 * i - 8 * n + 2 * g + c, 1), 0:T].rearrange("p k t -> p (k t)")
                            act.activation(o, bank[t % 4][:, 0:T], ACT.Copy if n == 2 else ACT.Gelu_apprx_tanh)\
                                .then_inc(S(f"tile_out{t % 4}"), 1)

        def guq_dve(dve, vv):
            dve.wait_ge(S("shift_stage"), 2)
            dve.wait_ge(S("state_stored"), 48)
            vv.do(dve.memset(q[:, :, T:XT_], 0.0), "q_pad")
            for k in (24, 25):
                mix_shift(dve, vv, row_(k), k, pcol("mu_shift", k))
            with vv.loop(0, 6, {"dve": 12}) as i:
                for h in range(4):
                    lo_unit(dve, U_GUQ + 2 + h, 4, i)
                    mix_shift(dve, vv, row_(4 * i + h), 4 * i + h, pcol("mu_shift", 4 * i + h))

        sq_v = mixf[:, 0:2560]
        vtok = mixf[:, 0:3072].rearrange("p (t c) -> p t c", t=3)
        ws_raw = mixf[:, 3072:4096].rearrange("p (g s) -> p g s", g=8)
        ws_t = mixf[:, 4096:5120].rearrange("p (g t) -> p g t", g=8)
        ws_s = zz[0:TS, 0:512].rearrange("p (g t) -> p g t", g=8)
        v_mu, v_rs = zz[:, 640:960], zz[:, 960:1280]
        bs_row = wk[0:1, 2560:5120].rearrange("p (g t) -> p g t", g=8)

        def sgu_pool(pool):
            pool.wait_ge(S("xn_lo"), 4)
            pool.dma_start(ws_raw, A["w_s"].rearrange("g t s -> t g s")).then_inc(S("ws_in"), 16)
            pool.wait_ge(S("vt_out"), 6)
            pool.dma_start(O["sgu_v"], vtok[0:TS, 2, :]).then_inc(S("sguv_stored"), 16)
            pool.wait_ge(S("bl_ready"), 1)
            for n, src in enumerate((bh, bl)):
                pool.dma_start(A["sgu_parts"][n], src[:, :, :].rearrange("p k t -> p (k t)")).then_inc(S("sgu_away"), 16)

        def sgu_dve(dve, vv):
            for t in range(4):
                dve.wait_ge(S(f"tile_out{t}"), 14 if t >= 2 else 15)
            gvt = gv.rearrange("p k t -> p t k")
            vv.do(dve.tensor_reduce(v_mu, gvt, AX_X, ALU.add), "v_sum")
            dve.wait_ge(S("sgu_ps"), 1)
            vv.do(dve.tensor_scalar(v_mu, bank[4][:, 0:T], -1.0 / W, None, ALU.mult))
            vv.do(dve.tensor_tensor(gv, gv, bmid(v_mu, KW), ALU.add), "v_centred")
            dve.wait_ge(S("v_squares"), 1)
            vv.do(dve.tensor_reduce(v_rs, sq_v.rearrange("p (k t) -> p t k", k=KW), AX_X, ALU.add), "v_sum")
            dve.wait_ge(S("sgu_ps"), 2)
            vv.do(dve.tensor_scalar(v_rs, bank[5][:, 0:T], 1.0 / W, LN_EPS, ALU.mult, ALU.add), "v_var")
            dve.wait_ge(S("v_std"), 1)
            vv.do(dve.reciprocal(v_rs, v_rs))
            vv.do(dve.tensor_tensor(gv, gv, bmid(v_rs, KW), ALU.mult))
            for k in range(KW):
                vv.do(dve.tensor_scalar(gv[:, k, :], gv[:, k, :], pcol("sgu_g", k), pcol("sgu_b", k), ALU.mult, ALU.add), "v_normed")
            for n in range(2):
                dve.wait_ge(S("sgu_ps"), 9 + n)
                vv.do(dve.tensor_tensor(ws_t[:, 4 * n:4 * n + 4, :], bank[6 + n][:, :].rearrange("p (g t) -> p g t", g=4),
                                        bmid(m_u[:, :], 4), ALU.mult), "ws_out")
            dve.wait_ge(S("sgu_ps"), 11)
            for g in range(8):
                vv.do(dve.tensor_tensor(ws_s[:, g, :].rearrange("p (b t) -> p b t", b=NB), bmid(bank[4][0:TS, 8 * g:8 * g + 8], NB),
                                        bc(m_e8[0:TS, :], 8), ALU.mult), "wss_out")
            for g in range(8):
                dve.wait_ge(S("sgu_ps"), 12 + g)
                vv.do(dve.tensor_tensor(gu[:, g, :], gu[:, g, :], bank[4 + g % 4][:, 0:T], ALU.mult), "gated")
            dve.wait_ge(S("bh_ready"), 1)
            vv.do(dve.tensor_tensor(bl[:, :, :], gu, bh[:, :, :], ALU.subtract), "bl_ready")

        def sgu_act(act, aa):
            act.wait_ge(S("v_centred"), 1)
            aa.do(act.activation(sq_v, wk[:, 2560:5120], ACT.Square), "v_squares")
            act.wait_ge(S("v_var"), 1)
            aa.do(act.activation(v_rs, v_rs, ACT.Sqrt), "v_std")
            for f in range(6):
                act.wait_ge(S("sgu_ps"), 3 + f)
                m = TS if f >= 4 else P
                aa.do(act.activation(vtok[0:m, f // 2, 512 * (f % 2):512 * (f % 2) + 512], bank[4 + f % 4][0:m, :], ACT.Copy), "vt_out")
            b_s = A["b_s"].rearrange("(o g) t -> o g t", o=1)
            for c in range(2):
                act.dma_start(bs_row[:, :, 128 * c:128 * c + 128], b_s).then_inc(S("bs_in"), 16)
            act.wait_ge(S("bs_in"), 32)
            aa.do(act.activation(bs_row[:, :, TP:T].rearrange("o g (b t) -> o g b t", b=NB),
                                 bs_row[:, :, 0:64].rearrange("o g (b t) -> o g b t", b=NB)[:, :, 0:1, :].broadcast_to([1, 8, NB, 8]),
                                 ACT.Copy), "bs_samples")
            act.wait_ge(S("gated"), 8)
            aa.do(act.activation(bh[:, :, :], gu, ACT.Copy), "bh_ready")

        def sgu_pe(pe):
            def end(ins):
                ins.then_inc(S("sgu_ps"), 1)
            pe.wait_ge(S("v_sum"), 1)
            end(pe.matmul(bank[4][:, 0:T], ones[:, :], v_mu, start=True, stop=True))
            pe.wait_ge(S("v_sum"), 2)
            end(pe.matmul(bank[5][:, 0:T], ones[:, :], v_rs, start=True, stop=True))
            for f in range(6):
                pe.wait_ge(S("v_normed"), KW)
                if f >= 4:
                    pe.wait_ge(S("vt_out"), f - 3)
                m, t0 = (TS, TP) if f >= 4 else (P, 128 * (f // 2))
                for k in range(4):
                    last = pe.transpose(bank[4 + f % 4][0:m, 128 * k:128 * k + 128], gv[:, 4 * (f % 2) + k, t0:t0 + m], ident[:, :])
                end(last)
            pe.wait_ge(S("ws_in"), 16)
            for n in range(2):
                pe.wait_ge(S("vt_out"), 3 + n)
                for k in range(4):
                    last = pe.transpose(bank[6 + n][:, 128 * k:128 * k + 128], ws_raw[:, 4 * n + k, :], ident[:, :])
                end(last)
            pe.wait_ge(S("vt_out"), 6)
            pe.wait_ge(S("ws_out"), 2)
            end(pe.matmul(bank[4][0:TS, 0:64], rep8, ws_t[0:8, :, 0:8], start=True, stop=True))
            pe.wait_ge(S("bs_in"), 32)
            pe.wait_ge(S("bs_samples"), 1)
            pe.wait_ge(S("wss_out"), 8)
            for g in range(8):
                if g >= 4:
                    pe.wait_ge(S("gated"), g - 3)
                o, c = bank[4 + g % 4], slice(128 * g, 128 * g + 128)
                pe.matmul(o[:, 0:T], ones[0:1, :], bs_row[:, g, :], start=True, stop=False, skip_group_check=True)
                for t in range(2):
                    pe.matmul(o[:, 128 * t:128 * t + 128], vtok[:, t, c], ws_t[:, g, :], start=False, stop=False, skip_group_check=True)
                end(pe.matmul(o[:, TP:T], vtok[0:TS, 2, c], ws_s[:, g, :], start=False, stop=True, skip_group_check=True))

        kb = wk[:, 0:2048].rearrange("p (m c) -> p m c", m=2)
        vb = wk[:, 2048:4096].rearrange("p (m c) -> p m c", m=2)
        kts_ = [mixf[:, 2048 * n:2048 * n + 2048].rearrange("p (d m) -> p d m", d=KW) for n in range(2)]
        pr_, pr_t = zz[:, 0:256], zz[:, 256:512]
        qb = zz[:, 512:768].rearrange("p (k t) -> p k t", k=KW)
        o_tok = zz[:, 768:1024]
        mx, nmx, rsum, rinv = [zz[:, 1300 + n:1301 + n] for n in range(4)]
        XSCALE = float(W // XH) ** -0.5
        FILLS = 8

        def at_base(b):
            return 4 + FILLS * b


        def attn_pool(pool):
            def load(b, dst, cache, mem, sem):
                src = A[cache][b].rearrange("(m p) h d -> p m (h d)", p=P) if b < NB else O[mem].rearrange("(m p) c -> p m c", p=P)
                pool.dma_start(dst, src).then_inc(S(sem), 16)

            def keys(b):
                if b == 1:
                    pool.wait_ge(S("at_ps"), 4)
                elif b > 1:
                    pool.wait_ge(S("at_ps"), at_base(b - 2) + 5)
                load(b, kb, "cache_mem_k", "mem_k", "k_in")

            def values(b):
                if b:
                    pool.wait_ge(S("at_ps"), at_base(b - 1) + 7)
                load(b, vb, "cache_mem_v", "mem_v", "v_in")

            pool.wait_ge(S("bl_ready"), 1)
            for t in range(4):
                pool.wait_ge(S(f"mem_stored{t}"), 32)
            keys(0)
            values(0)
            keys(1)
            for b in range(1, NB + 1):
                if b < NB:
                    keys(b + 1)
                values(b)

        def score_bank(n):
            return bank[7 if n >= NB and (n - NB) % 2 else 4]

        def softmax_max(dve, vv, n, n_ps):
            dve.wait_ge(S("at_ps"), n_ps)
            vv.do(dve.tensor_reduce(mx, score_bank(n)[:, 0:MEM], AX_X, ALU.max))
            vv.do(dve.tensor_scalar(nmx, mx, -XSCALE, None, ALU.mult), "nmax")

        def softmax_scale(dve, vv, n):
            dve.wait_ge(S("exp_done"), n + 1)
            vv.do(dve.reciprocal(rinv, rsum))
            vv.do(dve.tensor_scalar(pr_, pr_, rinv, None, ALU.mult), "p_ready")

        def attn_dve(dve, vv):
            for b in range(NB):
                base = at_base(b)
                vv.do(dve.tensor_copy(qb, q[:, :, TP + 8 * b:TP + 8 * b + 32]), "qb")
                softmax_max(dve, vv, b, base + 1)
                softmax_scale(dve, vv, b)
                dve.wait_ge(S("at_ps"), base + 6)
                vv.do(dve.tensor_copy(pr_t, bank[5][:, 0:MEM]), "at_v")
                dve.wait_ge(S("at_ps"), base + 7)
                vv.do(dve.tensor_copy(o_tok, bank[6][:, 0:MEM]), "at_v")
                dve.wait_ge(S("at_ps"), base + 8)
                o = bank[7][:, 0:256].rearrange("p (d h t) -> p h d t", d=2, h=4)[:, :, :, 0:8]
                vv.do(dve.tensor_copy(q[:, :, TP + 8 * b:TP + 8 * b + 8].rearrange("p (h d) t -> p h d t", d=2), o), "at_v")
            base = at_base(NB)
            softmax_max(dve, vv, NB, base + 1)
            for n in range(8):
                h, t = n // 2, n % 2
                ahead = 1 if n < 7 else 0
                softmax_scale(dve, vv, NB + n)
                dve.wait_ge(S("at_ps"), base + 3 * n + 2 + ahead)
                vv.do(dve.tensor_copy(pr_t, bank[5][:, 0:MEM]), "at_v")
                if ahead:
                    softmax_max(dve, vv, NB + n + 1, base + 3 * n + 2)
                dve.wait_ge(S("at_ps"), base + 3 * n + 3 + ahead)
                vv.do(dve.tensor_copy(q[:, 2 * h:2 * h + 2, 128 * t:128 * t + 128],
                                      bank[6][:, 0:256].rearrange("p (d t) -> p d t", d=2)), "at_v")

        def attn_act(act, aa):
            def kts(b):
                for f in range(4):
                    act.wait_ge(S("at_ps"), at_base(b - 1) + f + 2 if b else f + 1)
                    aa.do(act.activation(kts_[b % 2][:, 2 * f:2 * f + 2, :], bank[f][:, :].rearrange("p (d m) -> p d m", d=2), ACT.Copy), "kt_out")

            def exps(n):
                act.wait_ge(S("nmax"), n + 1)
                aa.do(act.activation(pr_, score_bank(n)[:, 0:MEM], ACT.Exp, bias=nmx, scale=XSCALE, accum_out=rsum), "exp_done")

            act.wait_ge(S("sguv_stored"), 16)
            kts(0)
            for b in range(NB):
                exps(b)
                kts(b + 1)
            for n in range(8):
                exps(NB + n)

        def attn_pe(pe):
            def end(ins):
                ins.then_inc(S("at_ps"), 1)

            def transposes(b):
                pe.wait_ge(S("k_in"), 16 * (b + 1))
                if b:
                    pe.wait_ge(S("kt_out"), 4 * b)
                for f in range(4):
                    for a in range(2):
                        for m in range(2):
                            c = 128 * (2 * f + a)
                            last = pe.transpose(bank[f][:, 256 * a + 128 * m:256 * a + 128 * m + 128], kb[:, m, c:c + 128], ident[:, :])
                    end(last)

            def turn_p(n, nv):
                pe.wait_ge(S("p_ready"), n + 1)
                pe.wait_ge(S("at_v"), nv)
                for m in range(2):
                    last = pe.transpose(bank[5][:, 128 * m:128 * m + 128], pr_[:, 128 * m:128 * m + 128], ident[:, :])
                end(last)

            pe.wait_ge(S("q_pad"), 1)
            pe.wait_ge(S("gated"), 8)
            transposes(0)
            for b in range(NB):
                kt = kts_[b % 2]
                pe.wait_ge(S("kt_out"), 4 * (b + 1))
                if b:
                    pe.wait_ge(S("exp_done"), b)
                pe.wait_ge(S("qb"), b + 1)
                for h in range(XH):
                    for d in range(2):
                        last = pe.matmul(bank[4][32 * h:32 * h + 32, 0:MEM], qb[:, 2 * h + d, :], kt[:, 2 * h + d, :],
                                         start=d == 0, stop=d == 1)
                end(last)
                transposes(b + 1)
                turn_p(b, 3 * b)
                pe.wait_ge(S("at_v"), 3 * b + 1)
                pe.wait_ge(S("v_in"), 16 * (b + 1))
                for h in range(XH):
                    for m in range(2):
                        last = pe.matmul(bank[6][32 * h:32 * h + 32, 0:256], pr_t[:, 128 * m + 32 * h:128 * m + 32 * h + 32],
                                         vb[:, m, 256 * h:256 * h + 256], start=m == 0, stop=m == 1)
                end(last)
                pe.wait_ge(S("at_v"), 3 * b + 2)
                for d in range(2):
                    last = pe.transpose(bank[7][:, 128 * d:128 * d + 128], o_tok[:, 128 * d:128 * d + 128], ident[:, :])
                end(last)
            kt = kts_[NB % 2]
            pe.wait_ge(S("kt_out"), 4 * (NB + 1))

            def scores(n):
                h, t = n // 2, n % 2
                pe.wait_ge(S("exp_done"), NB + max(n - 1, 0))
                if n == 1:
                    pe.wait_ge(S("at_v"), 3 * NB)
                for d in range(2):
                    last = pe.matmul(score_bank(NB + n)[:, 0:MEM], q[:, 2 * h + d, 128 * t:128 * t + 128], kt[:, 2 * h + d, :],
                                     start=d == 0, stop=d == 1)
                end(last)

            scores(0)
            for n in range(8):
                h, t = n // 2, n % 2
                if n < 7:
                    scores(n + 1)
                turn_p(NB + n, 3 * NB + 2 * n)
                pe.wait_ge(S("at_v"), 3 * NB + 2 * n + 1)
                pe.wait_ge(S("v_in"), 16 * (NB + 1))
                for c in range(2):
                    for m in range(2):
                        last = pe.matmul(bank[6][:, 128 * c:128 * c + 128], vb[:, m, 256 * h + 128 * c:256 * h + 128 * c + 128],
                                         pr_t[:, 128 * m:128 * m + 128], start=m == 0, stop=m == 1)
                end(last)

        def attn_split_act(act, aa):
            act.wait_ge(S("at_v"), 3 * NB + 16)
            act.wait_ge(S("sgu_away"), 32)
            aa.do(act.activation(bh[:, :, :], q[:, :, 0:T], ACT.Copy), "bh_ready")

        def attn_split_dve(dve, vv):
            dve.wait_ge(S("bh_ready"), 2)
            dve.wait_ge(S("sgu_away"), 32)
            vv.do(dve.tensor_tensor(bl[:, :, :], q[:, :, 0:T], bh[:, :, :], ALU.subtract), "bl_ready")
            vv.do(dve.memset(mixf, 0.0))

        def branch_act_unit(act, j, i):
            hi_unit(act, U_BR[0] + j + 2, 6, i)
            if j % 3 == 1:
                for c in range(2):
                    t = T_BR[0] + 4 * (j // 3) + c
                    tile_ready(act, U_BR[0] + j, 12, i, c + 1)
                    act.wait_ge(S("gate_free"), 4 * i + 2 * (j // 3) + c + 1)
                    act.activation(gs[:, c, :], bank[t % 4][:, 0:T], ACT.Tanh, scale=0.5).then_inc(S(f"tile_out{t % 4}"), 1)

        def add_branch(dve, vv, n, g, c, i):
            tg = T_BR[0] + 4 * g + c
            tb = tg + 2
            dve.wait_ge(S(f"tile_out{tg % 4}"), 2 * i + tg // 4 + 1)
            tile_ready(dve, U_BR[0] + 3 * g + 2, 12, i, c + 1)
            gate = gs[:, c, :]
            dve.scalar_tensor_tensor(out=gate, in0=gate, scalar=1.0, in1=bank[tb % 4][:, 0:T],
                                     op0=ALU.add, op1=ALU.mult).then_inc(S(f"tile_out{tb % 4}"), 1)
            dve.wait_ge(S(f"tile_out{tb % 4}"), 2 * i + tb // 4 + 1)
            m = mix[:, ds(4 * i - 16 * n + 2 * g + c, 1), :].rearrange("p k t -> p (k t)")
            vv.do(dve.tensor_tensor(m, m, gate, ALU.add), "gate_free")

        def branch_pe(pe):
            with pe.Fori(8, 12) as i:
                for g in range(2):
                    pe_group(pe, U_BR[0] + 3 * g, T_BR[0] + 4 * g, ah, al_, 2, 6, 8, i)
                    pe.wait_ge(S("bl_ready"), 3)
                    pe_group(pe, U_BR[0] + 3 * g + 2, T_BR[0] + 4 * g + 2, bh, bl, 1, 6, 8, i)

        def branch_act(act, aa):
            tile_ready(act, U_BR[2] - 1)
            act.wait_ge(S("gated_out"), KW + 1)
            aa.do(act.activation(bh[:, :, :], rw[:, 0:KW, 0:T], ACT.Copy), "bh_ready")
            with act.Fori(8, 12) as i:
                for j in range(6):
                    branch_act_unit(act, j, i)

        def branch_dve(dve, vv):
            dve.wait_ge(S("bh_ready"), 3)
            vv.do(dve.tensor_tensor(bl[:, :, :], rw[:, 0:KW, 0:T], bh[:, :, :], ALU.subtract), "bl_ready")
            with vv.loop(8, 12, {"gate_free": 4}) as i:
                for g in range(2):
                    for h in range(3):
                        lo_unit(dve, U_BR[0] + 3 * g + 2 + h, 6, i)
                    for c in range(2):
                        add_branch(dve, vv, 2, g, c, i)

        mo = wk[:, 0:5120].rearrange("p (k t) -> p k t", k=KD)
        red, rstd = zz[:, 640:960], zz[:, 960:1280]

        def square_act(act, n, src, k=0, i=0):
            act.wait_ge(S("squares_added"), lin(n + (3 if n >= KD else 1), k, i))
            act.activation(gs[:, n % 2, :], src, ACT.Square).then_inc(S("tile_squares"), 1)

        def add_squares_dve(dve, n, k=0, i=0):
            dve.wait_ge(S("tile_squares"), lin(n + 1, k, i))
            dve.wait_ge(S("squares_added"), lin(n + (4 if n >= KD else 2), k, i))
            dve.tensor_tensor(red, red, gs[:, n % 2, :], ALU.add).then_inc(S("squares_added"), 1)

        def start_squares_dve(dve, before):
            for n in range(2):
                dve.memset(red, 0.0).then_inc(S("squares_added"), 1)
                dve.wait_ge(S("squares_added"), before + n + 1)

        def out_pe(pe):
            with pe.Fori(0, 4) as i:
                for g in range(2):
                    pe_group(pe, U_OUT + 2 * g, T_OUT + 2 * g, ah, al_, 2, 4, 4, i, None if g else "mx_lo")

        def out_act(act, aa):
            tile_ready(act, U_OUT - 2)
            for c in range(4):
                act.wait_ge(S("gate_free"), 38 + 4 * c)
                aa.do(act.activation(ah[:, 4 * c:4 * c + 4, :], mix[:, 4 * c:4 * c + 4, :], ACT.Copy, scale=0.5), "mx_hi")
            with act.Fori(0, 4) as i:
                for g in range(2):
                    for h in range(2):
                        hi_unit(act, U_OUT + 2 * g + 2 + h, 4, i)
                    for c in range(2):
                        t = T_OUT + 2 * g + c
                        tile_ready(act, U_OUT + 2 * g + 1, 8, i, c + 1)
                        square_act(act, 2 * g + c, bank[t % 4][:, 0:T], 4, i)
                        act.activation(mo[:, ds(4 * i + 2 * g + c, 1), :].rearrange("p k t -> p (k t)"),
                                       bank[t % 4][:, 0:T], ACT.Copy).then_inc(S(f"tile_out{t % 4}"), 1)

        def out_dve(dve, vv):
            for c in range(4):
                dve.wait_ge(S("mx_hi"), c + 1)
                vv.do(dve.scalar_tensor_tensor(out=al_[:, 4 * c:4 * c + 4, :], in0=mix[:, 4 * c:4 * c + 4, :], scalar=0.5,
                                               in1=ah[:, 4 * c:4 * c + 4, :], op0=ALU.mult, op1=ALU.subtract), "mx_lo")
            dve.wait_ge(S("state_stored"), 48 * (KW + 1))
            start_squares_dve(dve, 0)
            with dve.Fori(0, 4) as i:
                for g in range(2):
                    for h in range(2):
                        lo_unit(dve, U_OUT + 2 + 2 * g + h, 4, i)
                    for c in range(2):
                        add_squares_dve(dve, 2 * g + c, 4, i)

        red_more = gs[:, 0, :]

        def rms_squares_act(act, aa, src, sq, ready=None):
            for c in range(4):
                if ready:
                    act.wait_ge(S(ready), 4 * (c + 1))
                aa.do(act.activation(sq[:, 1280 * c:1280 * c + 1280], src[:, 1280 * c:1280 * c + 1280], ACT.Square), "rms_squares")

        def rms_root_act(act, aa, n):
            act.wait_ge(S("rms_mean"), n + 1)
            aa.do(act.activation(rstd, rstd, ACT.Sqrt), "rms_root")

        def rms_dve(dve, vv, n, sq):
            for c in range(4):
                dve.wait_ge(S("rms_squares"), c + 1)
                vv.do(dve.tensor_reduce(red_more if c else red, sq[:, 1280 * c:1280 * c + 1280].rearrange("p (k t) -> p t k", k=4),
                                        AX_X, ALU.add), None)
                if c:
                    vv.do(dve.tensor_tensor(red, red, red_more, ALU.add), "rms_sum" if c == 3 else None)
            rms_root_dve(dve, vv, n)

        def rms_root_dve(dve, vv, n):
            dve.wait_ge(S("rms_ps"), n + 1)
            vv.do(dve.tensor_scalar(rstd, bank[4][:, 0:T], 1.0 / D, RMS_EPS, ALU.mult, ALU.add), "rms_mean")
            dve.wait_ge(S("rms_root"), n + 1)
            vv.do(dve.reciprocal(rstd, rstd), "rms_ready_t")

        def rms_pe(pe, n):
            if n == 1:
                pe.wait_ge(S("rms_sum"), 1)
            else:
                pe.wait_ge(S("squares_added"), KD + 2 if n == 0 else 2 * KD + 4)
            pe.matmul(bank[4][:, 0:T], ones[:, :], red, start=True, stop=True).then_inc(S("rms_ps"), 1)

        x2_tok = [rwr[:, 0:D], rwr[:, D:2 * D], rwr[0:TS, 2 * D:3 * D]]
        cst_raw = qr[:, 0:11 * P]
        cst = rwr[:, 5552:5552 + 16 * 88].rearrange("p (r k) -> p r k", r=16)
        tail = rwr[:, 6960:6960 + 18 * 88].rearrange("p (r k) -> p r k", r=18)

        def res_pool(pool, pp):
            pool.wait_ge(S("bl_ready"), 3)
            for k in range(2):
                pool.dma_start(x2_tok[k], A["x_prompt"][128 * k:128 * k + 128, :]).then_inc(S("x2_in"), 16)
            pool.dma_start(x2_tok[2], A["x_sample"]).then_inc(S("x2_in"), 16)
            pool.dma_start(cst_raw.rearrange("p (j n) -> p j n", n=P),
                           A["state_ffn_conv"].rearrange("b r (k c) -> (b r k) c", c=P).rearrange("(j p) c -> p j c", p=P))\
                .then_inc(S("x2_in"), 16)
            pool.wait_ge(S("res_ps"), KD)
            pp.do(pool.memset(ext[:, :, 0:2], 0.0))
            pp.do(pool.memset(rwr[:, 1352:4056], 0.0), "ext_set")
            pool.wait_ge(S("hn_lo"), 4)
            pp.do(pool.memset(wk[:, 0:5120], 0.0), "sum_zero")

        def res_act(act, aa):
            for t in range(4):
                act.wait_ge(S(f"tile_out{t}"), T_FFN // 4 + (1 if t < T_FFN % 4 else 0))
            act.wait_ge(S("mx_lo"), 4)
            rms_root_act(act, aa, 0)
            rms_squares_act(act, aa, mixf, wk[:, 0:5120], "h_ready")
            rms_root_act(act, aa, 1)
            for c in range(4):
                act.wait_ge(S("hn"), 4 * (c + 1))
                aa.do(act.activation(ah[:, 4 * c:4 * c + 4, :], mo[:, 4 * c:4 * c + 4, :], ACT.Copy), "hn_hi")
            for f in range(3):
                act.wait_ge(S("cst_ps"), f + 1)
                w = 512 if f < 2 else 384
                aa.do(act.activation(rwr[:, 5552 + 512 * f:5552 + 512 * f + w], bank[4 + f][:, 0:w], ACT.Copy), "cst_out")

        def res_dve(dve, vv):
            dve.wait_ge(S("squares_added"), KD + 2)
            rms_root_dve(dve, vv, 0)
            for k in range(KD):
                vv.do(dve.scalar_tensor_tensor(out=mo[:, k, :], in0=mo[:, k, :], scalar=pcol("g_post_mix", k), in1=rstd,
                                               op0=ALU.mult, op1=ALU.mult))
                dve.wait_ge(S("res_ps"), k + 1)
                vv.do(dve.tensor_tensor(mix[:, k, :], mo[:, k, :], bank[4 + k % 4][:, 0:T], ALU.add), "h_ready")
            rms_dve(dve, vv, 1, wk[:, 0:5120])

            def lo_parts(c):
                dve.wait_ge(S("hn_hi"), c + 1)
                vv.do(dve.tensor_tensor(al_[:, 4 * c:4 * c + 4, :], mo[:, 4 * c:4 * c + 4, :], ah[:, 4 * c:4 * c + 4, :],
                                        ALU.subtract), "hn_lo")

            for c in range(4):
                for k in range(4 * c, 4 * c + 4):
                    vv.do(dve.scalar_tensor_tensor(out=mo[:, k, :], in0=mix[:, k, :], scalar=pcol("g_pre_ffn", k), in1=rstd,
                                                   op0=ALU.mult, op1=ALU.mult), "hn")
                if c:
                    lo_parts(c - 1)
            lo_parts(3)

        def res_pe(pe):
            rms_pe(pe, 0)
            pe.wait_ge(S("x2_in"), 64)
            for k in range(KD):
                if k >= 4:
                    pe.wait_ge(S("h_ready"), k - 3)
                else:
                    pe.wait_ge(S("rms_ready_t"), 1)
                x_transposes(pe, x2_tok, k, bank[4 + k % 4]).then_inc(S("res_ps"), 1)
            pe.wait_ge(S("h_ready"), KD)
            rms_pe(pe, 1)
            pe.wait_ge(S("rms_ready_t"), 2)
            for f in range(3):
                for j in range(4 * f, min(4 * f + 4, 11)):
                    last = pe.transpose(bank[4 + f][:, 128 * (j % 4):128 * (j % 4) + 128], cst_raw[:, 128 * j:128 * j + 128], ident[:, :])
                last.then_inc(S("cst_ps"), 1)

        ext = rwr[:, 0:1352].rearrange("p (k t) -> p k t", k=4)
        cgate = rwr[:, 1352:2704].rearrange("p (k t) -> p k t", k=4)
        cval = rwr[:, 2704:4056].rearrange("p (k t) -> p k t", k=4)
        facc = mo
        UF, TF = U_FFN, T_FFN

        def smp_c(t):
            return t[:, :, TP + 2:CEXT].rearrange("p k (b t) -> p k b t", b=NB)

        def up_pe(pe, u, t, k=0, i=0, chunks=None):
            for g in range(2):
                pe_group(pe, u + 2 * g, t + 2 * g, ah, al_, 2, 12 if k else 0, 24 if k else 0, i, None if g else chunks)

        def down_pe(pe, u, t, k=0, i=0, c=0):
            pe.wait_ge(S("ff_lo"), lin(c, 2 if k else 0, i))
            for g in range(4):
                pe.wait_ge(S("lo_done"), lin(u + g + 1, 12 if k else 0, i))
                s = (u + g) % NS
                for c4 in range(4):
                    tt = t + 4 * g + c4
                    bank_free(pe, tt, 24 if k else 0, i)
                    for kk in range(4):
                        o = 512 * kk + 128 * c4
                        last = three(pe, bank[tt % 4][:, 0:T], hi[s][:, o:o + P], lo[s][:, o:o + P],
                                     bh[:, kk, :], bl[:, kk, :], kk == 0, kk == 3)
                    last.then_inc(S("parts"), 1)

        def ffn_pe(pe):
            up_pe(pe, UF, TF, 0, 0, "hn_lo")
            up_pe(pe, UF + 4, TF + 4)
            with pe.Fori(0, NCH - 1) as i:
                up_pe(pe, UF + 8, TF + 8, 1, i)
                down_pe(pe, UF + 12, TF + 12, 1, i, 2)
                up_pe(pe, UF + 16, TF + 28, 1, i)
            down_pe(pe, U_END - 4, T_FFN + 8 + 24 * (NCH - 1), 0, 0, 2 * NCH)

        def ffn_act(act, aa):
            def rows(u, t, q, g, k=0, i=0):
                tk, pk = (24, 32) if k else (0, 0)
                for c in range(2):
                    l, b = 2 * g + c, (t + c) % 4
                    if q >= 4:
                        act.wait_ge(S("ext_free"), lin(q + c - 3, 8 if k else 0, i))
                    tile_ready(act, u, pk, i, c + 1)
                    act.activation(ext[:, l, 2:2 + TP], bank[b][:, 0:TP], ACT.Copy)
                    act.activation(smp_c(ext)[:, l, :, 2:2 + TB], bank[b][:, TP:T].rearrange("p (b t) -> p b t", b=NB),
                                   ACT.Copy).then_inc(S(f"tile_out{b}"), 1)

            def his(u, n, k=0, i=0):
                for h in range(n):
                    hi_unit(act, u + h + 2, 12 if k else 0, i, 32 if k else 0)

            def gate():
                act.wait_ge(S("gate_conv"), aa.value("gate_act") + 1)
                aa.do(act.activation(rwr[:, 1352:2704], rwr[:, 1352:2704], ACT.Gelu_apprx_tanh), "gate_act")

            def split(turn):
                act.wait_ge(S("ff"), turn + 1)
                aa.do(act.activation(bh[:, 0:4, 0:TP], cval[:, :, 0:TP], ACT.Copy), "ff_hi")
                aa.do(act.activation(bh[:, 0:4, TP:T].rearrange("p k (b t) -> p k b t", b=NB), smp_c(cval)[:, :, :, 0:TB], ACT.Copy),
                      "ff_hi")

            act.wait_ge(S("ext_set"), 1)
            for half in range(2):
                u, t = UF + 4 * half, TF + 4 * half
                his(u, 2)
                rows(u + 1, t, 4 * half, 0)
                his(u + 2, 2)
                rows(u + 3, t + 2, 4 * half + 2, 1)
                if half == 0:
                    gate()
            with aa.loop(0, NCH - 1, {"gate_act": 1, "ff_hi": 2}) as i:
                his(UF + 8, 2, 1, i)
                rows(UF + 9, TF + 8, 8, 0, 1, i)
                his(UF + 10, 1, 1, i)
                split(i)
                his(UF + 11, 1, 1, i)
                rows(UF + 11, TF + 10, 10, 1, 1, i)
                his(UF + 12, 6, 1, i)
                gate()
                rows(UF + 17, TF + 28, 12, 0, 1, i)
                his(UF + 18, 2, 1, i)
                rows(UF + 19, TF + 30, 14, 1, 1, i)
            split(NCH - 1)
            for g in range(5):
                hi_unit(act, U_END - 2 + g)
                for n in range(4 * g - 4, 4 * g) if g else ():
                    t = T_FFN + 8 + 24 * (NCH - 1) + n
                    act.wait_ge(S(f"tile_out{t % 4}"), t // 4 + 1)
                    square_act(act, KD + n, facc[:, n, :])

        def ffn_dve(dve, vv):
            def conv(t, q, k=0, i=0):
                l, half = q % 4, q // 4 % 2
                dst = cval if half else cgate
                dve.wait_ge(S(f"tile_out{t % 4}"), lin(t // 4 + 1, 6 if k else 0, i))
                tile = KF * half + 4 * (q // 8) + l

                def col(c):
                    return ds(4 * i + c, 1) if k else slice(c, c + 1)

                vv.do(dve.tensor_copy(smp_c(ext)[:, l, :, 0:2],
                                      cst.rearrange("p (b r) k -> p b r k", r=2)[:, :, :, col(tile)].rearrange("p b r k -> p b (r k)")))
                for j in range(3):
                    w = prm[:, col(COL["conv_w"] + 88 * j + tile)]
                    o, x = dst[:, l, 0:336], ext[:, l, j:j + 336]
                    if j == 0:
                        vv.do(dve.tensor_scalar(o, x, w, prm[:, col(COL["conv_b"] + tile)], ALU.mult, ALU.add))
                    else:
                        vv.do(dve.scalar_tensor_tensor(out=o, in0=x, scalar=w, in1=o, op0=ALU.mult, op1=ALU.add),
                              "gate_conv" if j == 2 and q % 8 == 3 else None)
                vv.do(dve.tensor_copy(tail[:, 0:2, col(tile)].rearrange("p r k -> p (r k)"), ext[:, l, TP:TP + 2]))
                vv.do(dve.tensor_copy(tail[:, 2:18, :].rearrange("p (b r) k -> p b r k", r=2)[:, :, :, col(tile)]
                                      .rearrange("p b r k -> p b (r k)"), smp_c(ext)[:, l, :, TB:TB + 2]), "ext_free")

            def value(turn):
                dve.wait_ge(S("gate_act"), turn + 1)
                vv.do(dve.tensor_tensor(rwr[:, 2704:4056], rwr[:, 2704:4056], rwr[:, 1352:2704], ALU.mult), "ff")

            def split(turn):
                dve.wait_ge(S("ff_hi"), 2 * turn + 2)
                vv.do(dve.tensor_tensor(bl[:, 0:4, 0:TP], cval[:, :, 0:TP], bh[:, 0:4, 0:TP], ALU.subtract), "ff_lo")
                vv.do(dve.tensor_tensor(bl[:, 0:4, TP:T].rearrange("p k (b t) -> p k b t", b=NB), smp_c(cval)[:, :, :, 0:TB],
                                        bh[:, 0:4, TP:T].rearrange("p k (b t) -> p k b t", b=NB), ALU.subtract), "ff_lo")

            def lo(u, k=0, i=0):
                lo_unit(dve, u + 2, 12 if k else 0, i, 32 if k else 0)

            def down(u, t, g, k=0, i=0):
                for c in range(4):
                    tt = t + 4 * g + c
                    b = tt % 4
                    dve.wait_ge(S("parts"), lin(parts_of(u + g) - 3 + c, 32 if k else 0, i))
                    f = facc[:, 4 * g + c, :]
                    dve.tensor_tensor(f, f, bank[b][:, 0:T], ALU.add).then_inc(S(f"tile_out{b}"), 1)
                    dve.wait_ge(S(f"tile_out{b}"), lin(tt // 4 + 1, 6 if k else 0, i))

            for u in range(8):
                lo(UF + u)
                if u == 1:
                    dve.wait_ge(S("cst_out"), 3)
                if u in (1, 3, 5):
                    conv(TF + u - 1, u - 1)
                    conv(TF + u, u)
            dve.wait_ge(S("sum_zero"), 1)
            with vv.loop(0, NCH - 1, PER_F) as i:
                lo(UF + 8, 1, i)
                conv(TF + 6, 6, 1, i)
                lo(UF + 9, 1, i)
                conv(TF + 7, 7, 1, i)
                value(i)
                lo(UF + 10, 1, i)
                split(i)
                conv(TF + 8, 8, 1, i)
                lo(UF + 11, 1, i)
                for g in range(4):
                    down(UF + 12, TF + 12, g, 1, i)
                    lo(UF + 12 + g, 1, i)
                lo(UF + 16, 1, i)
                conv(TF + 9, 9, 1, i)
                conv(TF + 10, 10, 1, i)
                lo(UF + 17, 1, i)
                conv(TF + 11, 11, 1, i)
                lo(UF + 18, 1, i)
                conv(TF + 28, 12, 1, i)
                lo(UF + 19, 1, i)
                conv(TF + 29, 13, 1, i)
            for q in (6, 7):
                conv(TF + q + 24 * (NCH - 1), 8 * (NCH - 1) + q)
            value(NCH - 1)
            split(NCH - 1)
            start_squares_dve(dve, KD + 2)
            for g in range(4):
                down(U_END - 4, T_FFN + 8 + 24 * (NCH - 1), g)
                lo(U_END - 4 + g)
                if g:
                    for n in range(4 * g - 4, 4 * g):
                        add_squares_dve(dve, KD + n)
            for n in range(12, 16):
                add_squares_dve(dve, KD + n)

        PER_F = {"dve": 39, "gate_conv": 1, "ext_free": 8, "ff": 1, "ff_lo": 2}

        y_stage = [rwr[:, 0:D], rwr[:, D:2 * D], rwr[0:TS, 2 * D:3 * D]]
        tail_stage = raw[0]

        def end_act(act, aa):
            for t in range(4):
                act.wait_ge(S(f"tile_out{t}"), 434 // 4 + (1 if t < 434 % 4 else 0))
            rms_root_act(act, aa, 2)
            for f in range(4):
                act.wait_ge(S("tail_ps"), f + 1)
                w = 512 if f < 3 else 128
                aa.do(act.activation(tail_stage[:, 512 * f:512 * f + w], bank[4 + f][:, 0:w], ACT.Copy), "tail_out")
            for f in range(12):
                c, k = f // 3, f % 3
                act.wait_ge(S("y_ps"), KW + f + 1)
                m = TS if k == 2 else P
                aa.do(act.activation(y_stage[k][:, 512 * c:512 * c + 512], bank[4 + f % 4][0:m, :], ACT.Copy), "y_staged")

        def end_dve(dve, vv):
            dve.wait_ge(S("squares_added"), 2 * KD + 4)
            rms_root_dve(dve, vv, 2)
            for k in range(KD):
                vv.do(dve.scalar_tensor_tensor(out=facc[:, k, :], in0=facc[:, k, :], scalar=pcol("g_post_ffn", k), in1=rstd,
                                               op0=ALU.mult, op1=ALU.mult), "y_scaled" if k % 2 else None)
                if k % 2 == 0:
                    vv.do(dve.tensor_tensor(facc[:, k, :], facc[:, k, :], mix[:, k, :], ALU.add), "y_ready")

        def end_pe(pe):
            rms_pe(pe, 2)
            pe.wait_ge(S("rms_ready_t"), 3)
            tails = rwr[:, 6960:6960 + 18 * 88]
            pieces = [(0, 128), (128, 48)] + [(176 + 128 * j, 128) for j in range(11)]
            pe.wait_ge(S("ext_free"), 8 * NCH)
            for n, (at, m) in enumerate(pieces):
                last = pe.transpose(bank[4 + n // 4][0:m, 128 * (n % 4):128 * (n % 4) + 128], tails[:, at:at + m], ident[:, :])
                if n % 4 == 3 or n == len(pieces) - 1:
                    last.then_inc(S("tail_ps"), 1)
            for f in range(12):
                c, k = f // 3, f % 3
                pe.wait_ge(S("y_ready"), 2 * c + 2)
                pe.wait_ge(S("y_ready_odd"), 2 * c + 2)
                if f < 4:
                    pe.wait_ge(S("tail_out"), f + 1)
                else:
                    pe.wait_ge(S("y_staged"), f - 3)
                m = TS if k == 2 else P
                for j in range(4):
                    last = pe.transpose(bank[4 + f % 4][0:m, 128 * j:128 * j + 128], facc[:, 4 * c + j, 128 * k:128 * k + m], ident[:, :])
                last.then_inc(S("y_ps"), 1)

        def end_pool(pool, pp):
            for k in range(1, KD, 2):
                pool.wait_ge(S("y_scaled"), (k + 1) // 2)
                pp.do(pool.tensor_tensor(facc[:, k, :], facc[:, k, :], mix[:, k, :], ALU.add), "y_ready_odd")

        def end_sp(sp):
            sp.wait_ge(S("tail_out"), 4)
            sp.dma_start(O["conv_p"][0:128, :], tail_stage[:, 0:128]).then_inc(S("stored"), 16)
            sp.dma_start(O["conv_p"][128:176, :], tail_stage[0:48, 128:256]).then_inc(S("stored"), 16)
            sp.dma_start(O["conv_s"].rearrange("(j p) n -> p j n", p=P),
                           tail_stage[:, 256:256 + 11 * P].rearrange("p (j n) -> p j n", n=P)).then_inc(S("stored"), 16)
            for k in range(3):
                sp.wait_ge(S("y_staged"), 10 + k)
                sp.dma_start(O["y_p"][128 * k:128 * k + 128, :] if k < 2 else O["y_s"], y_stage[k]).then_inc(S("stored"), 16)
            sp.wait_ge(S("stored"), 16 * 6)
            sp.wait_ge(S("sguv_stored"), 16)
            sp.wait_ge(S("state_stored"), 48 * (KW + 1))
            for t in range(4):
                sp.wait_ge(S(f"mem_stored{t}"), 32)

        @block.gpsimd
        def _(pool):
            pp = Prog(pool, S, "pool")
            pool_constants(pool, pp)
            mem_pool(pool)
            shift_pool(pool)
            sgu_pool(pool)
            attn_pool(pool)
            wkv_pool(pool)
            res_pool(pool, pp)
            end_pool(pool, pp)

        @block.sync
        def _(sp):
            sp_memory(sp)
            for u in range(16):
                g = u // 4
                if u == 2:
                    sp_parameters_and_x(sp)
                load_unit(sp, kv(A["w_mem_k"] if g < 2 else A["w_mem_v"], 4 * (u % 4), 512 * (g % 2), 4, 512), u)
            for h in range(2):
                load_unit(sp, kv(A["w_in"], 8 * h, 0), U_RW + h)
            with sp.Fori(0, 12) as i:
                for g in range(2):
                    for h in range(2):
                        load_unit(sp, kv(A["w_in"], 8 * h, 512 * i + 256 * (g + 1)), U_RW + 2 + 2 * g + h, 4, i)
            for n, b in enumerate((2, 1, 0)):
                with sp.Fori(0, 4) as i:
                    for g in range(2):
                        for h in range(2):
                            load_unit(sp, kv(A["w_in"], 8 * h, 512 * i + NSH + 3 * W + D * b + 256 * g), U_BR[n] + 3 * g + h, 6, i)
                        load_unit(sp, kv(A["w_branch"][b], 0, 512 * i + 256 * g), U_BR[n] + 3 * g + 2, 6, i)
            with sp.Fori(0, 4) as i:
                for g in range(2):
                    for h in range(2):
                        load_unit(sp, kv(A["w_out"], 8 * h, 512 * i + 256 * g), U_OUT + 2 * g + h, 4, i)

            def up(half, c, k, i):
                for g in range(2):
                    for h in range(2):
                        n0 = half * DFF + 256 * g + (512 if k else 0)
                        load_unit(sp, kv(A["w_up"], 8 * h, lin(n0, 512 if k else 0, i)), c + 2 * g + h, 12 if k else 0, i)

            def down(rows, c, k, i):
                src = A["w_down"].rearrange("(c kt p) n -> p c kt n", kt=4, p=P)
                for g in range(4):
                    cc = ds(i, 1) if k else slice(rows, rows + 1)
                    load_unit(sp, src[:, cc, :, 512 * g:512 * g + 512].rearrange("p c kt n -> p (c kt) n"), c + g, 12 if k else 0, i)

            up(0, UF, 0, 0)
            up(1, UF + 4, 0, 0)
            with sp.Fori(0, NCH - 1) as i:
                up(0, UF + 8, 1, i)
                down(0, UF + 12, 1, i)
                up(1, UF + 16, 1, i)
            down(NCH - 1, U_END - 4, 0, 0)
            end_sp(sp)

        @block.scalar
        def _(act):
            aa = Prog(act, S, "act")
            entry_act(act, aa)
            for u in range(NS):
                hi_unit(act, u)
            mem_act(act, aa)
            split_x_act(act, aa)
            rw_act(act)
            shift_act(act, aa)
            guq_act(act)
            sgu_act(act, aa)
            attn_act(act, aa)
            attn_split_act(act, aa)
            wkv_start_act(act, aa)
            prepare_act(act, aa, 0)
            for n in range(2):
                wkv_act(act, aa, n)
            branch_act(act, aa)
            out_act(act, aa)
            res_act(act, aa)
            ffn_act(act, aa)
            end_act(act, aa)

        @block.vector
        def _(dve):
            vv = Prog(dve, S, "dve")
            entry_dve(dve, vv)
            for u in range(NS):
                lo_unit(dve, u)
            mem_dve(dve, vv)
            split_x_dve(dve, vv)
            rw_dve(dve)
            shift_dve(dve, vv)
            guq_dve(dve, vv)
            sgu_dve(dve, vv)
            attn_dve(dve, vv)
            attn_split_dve(dve, vv)
            wkv_start_dve(dve, vv)
            for n in range(2):
                wkv_dve(dve, vv, n)
            branch_dve(dve, vv)
            out_dve(dve, vv)
            res_dve(dve, vv)
            ffn_dve(dve, vv)
            end_dve(dve, vv)

        @block.tensor
        def _(pe):
            entry_pe(pe)
            mem_pe(pe)
            rw_pe(pe)
            shift_pe(pe)
            guq_pe(pe)
            sgu_pe(pe)
            attn_pe(pe)
            wkv_start_pe(pe)
            for n in range(2):
                wkv_pe(pe, n)
            branch_pe(pe)
            out_pe(pe)
            res_pe(pe)
            ffn_pe(pe)
            end_pe(pe)


_INS = {'x_prompt': (TP, D), 'x_sample': (TS, D), 'mem_prompt': (MEM, D), 'state_wkv': (NB, NH, HD, HD), 'state_shift': (NB, NSH),
        'cache_mem_k': (NB, MEM, XH, W // XH), 'cache_mem_v': (NB, MEM, XH, W // XH), 'state_ffn_conv': (NB, 2, F2),
        'g_pre_mix': (D,), 'w_in': (D, NSH + 3 * W + 3 * D), 'mu_shift': (NSH,), 'w0': (W,), 'w_decay': (64, W), 'a0': (W,),
        'w_aaa': (64, W), 'w_gate': (128, W), 'k_k': (W,), 'k_a': (W,), 'r_k': (W,), 'lnx_w': (W,), 'lnx_b': (W,),
        'sgu_g': (W,), 'sgu_b': (W,), 'w_s': (8, 128, 128), 'b_s': (8, 128), 'g_mem': (D,), 'w_mem_k': (D, W),
        'w_mem_v': (D, W), 'w_branch': (3, W, D), 'w_out': (D, D), 'g_post_mix': (D,), 'g_pre_ffn': (D,), 'w_up': (D, F2),
        'conv_w': (3 * F2,), 'conv_b': (F2,), 'w_down': (DFF, D), 'g_post_ffn': (D,)}
_OUTS = [("y_p", (TP, D), (1, TP, D)), ("y_s", (TS, D), (NB, TB, D)),
         ("wkv_p", (NH, HD, HD), (1, 1, NH, HD, HD)), ("shift_p", (KSH, P), (1, 1, NSH)),
         ("mem_k", (MEM, W), (1, 1, MEM, XH, W // XH)), ("mem_v", (MEM, W), (1, 1, MEM, XH, W // XH)),
         ("conv_p", (2 * F2 // P, P), (1, 1, 2, F2)),
         ("wkv_s", (NB, NH, HD, HD), (1, NB, NH, HD, HD)), ("shift_s", (NB * KSH, P), (1, NB, NSH)),
         ("sgu_v", (TS, W), (1, NB, TB, W)), ("conv_s", (NB * 2 * F2 // P, P), (1, NB, 2, F2))]


def kernel(**inputs):
    import numpy as _np
    import concourse.bacc as _bacc
    from concourse import mybir as _mybir
    from concourse.bass_utils import run_bass_kernel_spmd as _run

    nc = _bacc.Bacc("TRN2", target_bir_lowering=False, num_devices=1)
    arrays, ins, outs = {}, {}, {}
    for name, shape in _INS.items():
        a = _np.ascontiguousarray(_np.asarray(inputs[name])).reshape(shape)
        arrays[f"in_{name}"] = a
        ins[name] = nc.dram_tensor(f"in_{name}", a.shape, _mybir.dt.from_np(a.dtype), kind="ExternalInput").ap()
    for name, shape, _ in _OUTS:
        outs[name] = nc.dram_tensor(f"out_{name}", shape, _mybir.dt.float32, kind="ExternalOutput").ap()
    ins["sgu_parts"] = nc.dram_tensor("sgu_parts", (2, P, KW * T), F32R, kind="Internal").ap()
    hybrid_step(nc, ins, outs)
    r = _run(nc, [arrays], core_ids=[0])
    return tuple(_np.asarray(r.results[0][f"out_{name}"]).reshape(shape) for name, _, shape in _OUTS)
```
